# Optimizing a Trainium2 kernel written in Bass

```python
import math
import jax, jax.numpy as jnp
from jax import lax
import numpy as np

D_MODEL = 1024
BATCH = 1
SEQ = 256
DEPTH = 1

EPS = 1e-5
ROPE_THETA = 10000.0
GLA_HEADS = 4
GLA_DK = 64
GLA_DV = 128
GLA_GATE_RANK = 16
GLA_GATE_TEMP = 16.0
GLA_CHUNK = 64
GLA_QK = GLA_HEADS * GLA_DK
GLA_V = GLA_HEADS * GLA_DV
DIL_PAIRS = ((128, 1), (512, 4), (2048, 16))
DIL_GROUPS = 3
DIL_HEADS = 4
DIL_HEAD_DIM = 128
DIL_BLOCK = 128
DIL_W = DIL_GROUPS * DIL_HEADS * DIL_HEAD_DIM
DIL_OUT = DIL_HEADS * DIL_HEAD_DIM
N_BRANCHES = 2
MEM_LEN = 256
XATTN_HEADS = 4
XATTN_HEAD_DIM = 128
N_EXPERTS = 32
TOP_K = 4
D_FF = D_MODEL
SWIGLU_ALPHA = 1.702
SWIGLU_LIMIT = 7.0
MOE_BLOCK = 256
IN_SIZES = (GLA_QK, GLA_QK, GLA_V, GLA_V, GLA_GATE_RANK, DIL_W, DIL_W, DIL_W)
D_IN = 2 * GLA_QK + 2 * GLA_V + GLA_GATE_RANK + 3 * DIL_W

kernel_name = "hybrid_gla_dilated_moe_block"

def rms_norm(x, g):
    xf = x.astype(jnp.float32)
    y = xf * lax.rsqrt(jnp.mean(xf * xf, axis=-1, keepdims=True) + EPS)
    return (y * g.astype(jnp.float32)).astype(x.dtype)

def apply_rotary(t, positions):
    half = t.shape[-1] // 2
    inv_freq = ROPE_THETA ** (-jnp.arange(half, dtype=jnp.float32) / half)
    ang = positions.astype(jnp.float32)[..., None] * inv_freq
    ang = ang.reshape(ang.shape[:2] + (1,) * (t.ndim - 3) + (half,))
    cos, sin = jnp.cos(ang), jnp.sin(ang)
    tf = t.astype(jnp.float32)
    t1, t2 = tf[..., :half], tf[..., half:]
    return jnp.concatenate([t1 * cos - t2 * sin, t2 * cos + t1 * sin], axis=-1).astype(t.dtype)

def gla_chunked(q, k, v, log_a):
    B_, S_, H, dk = q.shape
    dv = v.shape[-1]
    n = S_ // GLA_CHUNK

    def chunks(t):
        return t.astype(jnp.float32).reshape(B_, n, GLA_CHUNK, H, t.shape[-1]).transpose(1, 0, 3, 2, 4)

    causal = jnp.tril(jnp.ones((GLA_CHUNK, GLA_CHUNK), dtype=bool))

    def step(state, xs):
        qc, kc, vc, lac = xs
        bcum = jnp.cumsum(lac, axis=2)
        blast = bcum[:, :, -1]
        inter = jnp.einsum('bhck,bhkv->bhcv', qc * jnp.exp(bcum), state)
        diff = bcum[:, :, :, None, :] - bcum[:, :, None, :, :]
        decay = jnp.exp(jnp.where(causal[None, None, :, :, None], diff, -jnp.inf))
        scores = jnp.einsum('bhtsk,bhsk->bhts', qc[:, :, :, None, :] * decay, kc)
        intra = jnp.einsum('bhts,bhsv->bhtv', scores, vc)
        k_dec = kc * jnp.exp(blast[:, :, None, :] - bcum)
        new_state = jnp.exp(blast)[..., None] * state + jnp.einsum('bhsk,bhsv->bhkv', k_dec, vc)
        return new_state, inter + intra

    state0 = jnp.zeros((B_, H, dk, dv), jnp.float32)
    _, o = lax.scan(step, state0, (chunks(q), chunks(k), chunks(v), chunks(log_a)))
    return o.transpose(1, 0, 3, 2, 4).reshape(B_, S_, H, dv)

def dilated_window_attention(q, k, v, window, dilation):
    B_, S_, H, dh = q.shape
    span = window // dilation
    L = S_ // dilation
    nb = -(-L // DIL_BLOCK)
    Lp = nb * DIL_BLOCK

    def to_blocks(t):
        t = t.reshape(B_, L, dilation, H, dh).transpose(0, 2, 1, 3, 4)
        t = jnp.pad(t, ((0, 0), (0, 0), (0, Lp - L), (0, 0), (0, 0)))
        return t.reshape(B_, dilation, nb, DIL_BLOCK, H, dh)

    def with_prev(t):
        prev = jnp.pad(t[:, :, :-1], ((0, 0), (0, 0), (1, 0), (0, 0), (0, 0), (0, 0)))
        return jnp.concatenate([prev, t], axis=3)

    qb = to_blocks(q)
    kc = with_prev(to_blocks(k))
    vc = with_prev(to_blocks(v))
    s = jnp.einsum('bpnqhd,bpnkhd->bpnhqk', qb, kc).astype(jnp.float32)
    qi = jnp.arange(DIL_BLOCK)[:, None] + DIL_BLOCK
    kj = jnp.arange(2 * DIL_BLOCK)[None, :]
    dist = qi - kj
    band = (dist >= 0) & (dist <= span)
    has_prev = (jnp.arange(nb)[:, None, None] > 0) | (kj >= DIL_BLOCK)[None]
    mask = band[None] & has_prev
    s = jnp.where(mask[None, None, :, None], s, -jnp.inf)
    lse = jax.nn.logsumexp(s, axis=-1)
    p = jnp.exp(s - lse[..., None])
    o = jnp.einsum('bpnhqk,bpnkhd->bpnqhd', p.astype(v.dtype), vc)
    o = o.reshape(B_, dilation, Lp, H, dh)[:, :, :L].transpose(0, 2, 1, 3, 4).reshape(B_, S_, H, dh)
    lse = lse.transpose(0, 1, 2, 4, 3).reshape(B_, dilation, Lp, H)[:, :, :L]
    lse = lse.transpose(0, 2, 1, 3).reshape(B_, S_, H)
    return o, lse

def hybrid_mixer(a, positions, w_in, w_gla_a2, b_gla_a2, gla_norm_g, w_branch_gla, w_branch_dil,
                 w_branch_gate, b_branch_gate, w_mix_out):
    B_, S_, _ = a.shape
    proj = a @ w_in
    offs = [int(o) for o in np.cumsum(IN_SIZES)[:-1]]
    q_g, k_g, v_g, r_g, a_lr, q_d, k_d, v_d = jnp.split(proj, offs, axis=-1)

    q_g = q_g.reshape(B_, S_, GLA_HEADS, GLA_DK) * (GLA_DK ** -0.5)
    k_g = k_g.reshape(B_, S_, GLA_HEADS, GLA_DK)
    v_g = v_g.reshape(B_, S_, GLA_HEADS, GLA_DV)
    gate_logit = (a_lr @ w_gla_a2 + b_gla_a2).astype(jnp.float32)
    log_a = (jax.nn.log_sigmoid(gate_logit) / GLA_GATE_TEMP).reshape(B_, S_, GLA_HEADS, GLA_DK)
    o_g = gla_chunked(q_g, k_g, v_g, log_a)
    o_g = o_g * lax.rsqrt(jnp.mean(o_g * o_g, axis=-1, keepdims=True) + EPS)
    o_g = o_g.reshape(B_, S_, GLA_V) * gla_norm_g.astype(jnp.float32)
    o_g = (o_g * jax.nn.silu(r_g.astype(jnp.float32))).astype(a.dtype)

    shp = (B_, S_, DIL_GROUPS, DIL_HEADS, DIL_HEAD_DIM)
    q_d = apply_rotary(q_d.reshape(shp), positions) * (DIL_HEAD_DIM ** -0.5)
    k_d = apply_rotary(k_d.reshape(shp), positions)
    v_d = v_d.reshape(shp)
    outs, lses = [], []
    for g, (window, dilation) in enumerate(DIL_PAIRS):
        o_i, lse_i = dilated_window_attention(q_d[:, :, g], k_d[:, :, g], v_d[:, :, g], window, dilation)
        outs.append(o_i)
        lses.append(lse_i)
    o_all = jnp.stack(outs, axis=2)
    wts = jax.nn.softmax(jnp.stack(lses, axis=2), axis=2)
    o_d = jnp.sum(wts[..., None] * o_all.astype(jnp.float32), axis=2)
    o_d = o_d.reshape(B_, S_, DIL_OUT).astype(a.dtype)

    gates = jax.nn.sigmoid((a @ w_branch_gate + b_branch_gate).astype(jnp.float32))
    g_gla, g_dil = gates[..., :D_MODEL], gates[..., D_MODEL:]
    merged = g_gla * (o_g @ w_branch_gla).astype(jnp.float32) + g_dil * (o_d @ w_branch_dil).astype(jnp.float32)
    return merged.astype(a.dtype) @ w_mix_out

def memory_cross_attention(c, mem, mem_norm_g, w_xq, w_xkv, w_xo):
    B_, S_, _ = c.shape
    q = (c @ w_xq).reshape(B_, S_, XATTN_HEADS, XATTN_HEAD_DIM) * (XATTN_HEAD_DIM ** -0.5)
    kv = (rms_norm(mem, mem_norm_g) @ w_xkv).reshape(B_, MEM_LEN, 2, XATTN_HEADS, XATTN_HEAD_DIM)
    k, v = kv[:, :, 0], kv[:, :, 1]
    s = jnp.einsum('bshd,bmhd->bhsm', q, k).astype(jnp.float32)
    p = jax.nn.softmax(s, axis=-1)
    o = jnp.einsum('bhsm,bmhd->bshd', p.astype(v.dtype), v).reshape(B_, S_, XATTN_HEADS * XATTN_HEAD_DIM)
    return o @ w_xo

def clamped_swiglu(glu, lin):
    glu = jnp.minimum(glu, SWIGLU_LIMIT)
    lin = jnp.clip(lin, -SWIGLU_LIMIT, SWIGLU_LIMIT)
    return glu * jax.nn.sigmoid(SWIGLU_ALPHA * glu) * (lin + 1.0)

def moe_ffn(f, w_router, b_router, w_gate, b_gate, w_up, b_up, w_down, b_down):
    B_, S_, D = f.shape
    M = B_ * S_
    hf = f.reshape(M, D)
    logits = (hf @ w_router).astype(jnp.float32) + b_router.astype(jnp.float32)
    top_logit, top_e = lax.top_k(logits, TOP_K)
    gate = jax.nn.softmax(top_logit, axis=-1)
    P = M * TOP_K
    e_flat = top_e.reshape(P)
    tok_flat = jnp.arange(P, dtype=jnp.int32) // TOP_K
    g_flat = gate.reshape(P)
    order = jnp.argsort(e_flat)
    e_sorted = e_flat[order]
    counts = jnp.bincount(e_flat, length=N_EXPERTS)
    start = jnp.cumsum(counts) - counts
    padded = ((counts + MOE_BLOCK - 1) // MOE_BLOCK) * MOE_BLOCK
    pend = jnp.cumsum(padded)
    pstart = pend - padded
    dest = pstart[e_sorted] + (jnp.arange(P) - start[e_sorted])
    L = (-(-P // MOE_BLOCK) + N_EXPERTS) * MOE_BLOCK
    row_tok = jnp.full((L,), M, jnp.int32).at[dest].set(tok_flat[order])
    row_gate = jnp.zeros((L,), jnp.float32).at[dest].set(g_flat[order])
    n_blocks = L // MOE_BLOCK
    block_e = jnp.minimum(jnp.searchsorted(pend, jnp.arange(n_blocks) * MOE_BLOCK, side='right'),
                          N_EXPERTS - 1)
    h_pad = jnp.concatenate([hf, jnp.zeros((1, D), hf.dtype)], axis=0)
    xs = h_pad[row_tok].reshape(n_blocks, MOE_BLOCK, D)

    def expert_block(args):
        xb, e = args
        glu = xb @ w_gate[e] + b_gate[e]
        lin = xb @ w_up[e] + b_up[e]
        return clamped_swiglu(glu, lin) @ w_down[e] + b_down[e]

    ys = lax.map(expert_block, (xs, block_e)).reshape(L, D).astype(jnp.float32) * row_gate[:, None]
    out = jnp.zeros((M + 1, D), jnp.float32).at[row_tok].add(ys)[:M]
    return out.reshape(B_, S_, D).astype(f.dtype)

def setup_inputs(seed: int = 0) -> dict:
    key = jax.random.key(seed)
    ks = jax.random.split(key, 32)
    D = D_MODEL
    nrm = lambda k, shape, fan_in: jax.random.normal(k, shape, jnp.float32) * (fan_in ** -0.5)
    gain = lambda k, shape: 1.0 + 0.02 * jax.random.normal(k, shape, jnp.float32)
    bias = lambda k, shape, s=0.02: s * jax.random.normal(k, shape, jnp.float32)
    x = jax.random.normal(ks[0], (BATCH, SEQ, D), jnp.float32)
    mem = jax.random.normal(ks[1], (BATCH, MEM_LEN, D), jnp.float32)
    offset = jax.random.randint(ks[2], (BATCH, 1), 0, 1024, dtype=jnp.int32)
    positions = jnp.arange(SEQ, dtype=jnp.int32)[None, :] + offset
    return {
        "x": x,
        "mem": mem,
        "positions": positions,
        "norm1_g": gain(ks[3], (DEPTH, D)),
        "w_in": nrm(ks[4], (DEPTH, D, D_IN), D),
        "w_gla_a2": nrm(ks[5], (DEPTH, GLA_GATE_RANK, GLA_QK), GLA_GATE_RANK),
        "b_gla_a2": bias(ks[6], (DEPTH, GLA_QK), 0.1),
        "gla_norm_g": gain(ks[7], (DEPTH, GLA_V)),
        "w_branch_gla": nrm(ks[8], (DEPTH, GLA_V, D), GLA_V),
        "w_branch_dil": nrm(ks[9], (DEPTH, DIL_OUT, D), DIL_OUT),
        "w_branch_gate": nrm(ks[10], (DEPTH, D, N_BRANCHES * D), D),
        "b_branch_gate": bias(ks[11], (DEPTH, N_BRANCHES * D)),
        "w_mix_out": nrm(ks[12], (DEPTH, D, D), D),
        "norm2_g": gain(ks[13], (DEPTH, D)),
        "mem_norm_g": gain(ks[14], (DEPTH, D)),
        "w_xq": nrm(ks[15], (DEPTH, D, XATTN_HEADS * XATTN_HEAD_DIM), D),
        "w_xkv": nrm(ks[16], (DEPTH, D, 2 * XATTN_HEADS * XATTN_HEAD_DIM), D),
        "w_xo": nrm(ks[17], (DEPTH, XATTN_HEADS * XATTN_HEAD_DIM, D), XATTN_HEADS * XATTN_HEAD_DIM),
        "norm3_g": gain(ks[18], (DEPTH, D)),
        "w_router": nrm(ks[19], (DEPTH, D, N_EXPERTS), D),
        "b_router": bias(ks[20], (DEPTH, N_EXPERTS), 0.01),
        "w_gate": nrm(ks[21], (DEPTH, N_EXPERTS, D, D_FF), D),
        "b_gate": bias(ks[22], (DEPTH, N_EXPERTS, D_FF)),
        "w_up": nrm(ks[23], (DEPTH, N_EXPERTS, D, D_FF), D),
        "b_up": bias(ks[24], (DEPTH, N_EXPERTS, D_FF)),
        "w_down": nrm(ks[25], (DEPTH, N_EXPERTS, D_FF, D), D_FF),
        "b_down": bias(ks[26], (DEPTH, N_EXPERTS, D)),
        "final_norm_g": gain(ks[27], (D,)),
    }

def reference(x, mem, positions, norm1_g, w_in, w_gla_a2, b_gla_a2, gla_norm_g, w_branch_gla,
              w_branch_dil, w_branch_gate, b_branch_gate, w_mix_out, norm2_g, mem_norm_g, w_xq, w_xkv,
              w_xo, norm3_g, w_router, b_router, w_gate, b_gate, w_up, b_up, w_down, b_down,
              final_norm_g):
    h = x
    for l in range(DEPTH):
        a = rms_norm(h, norm1_g[l])
        h = h + hybrid_mixer(a, positions, w_in[l], w_gla_a2[l], b_gla_a2[l], gla_norm_g[l],
                             w_branch_gla[l], w_branch_dil[l], w_branch_gate[l], b_branch_gate[l],
                             w_mix_out[l])
        c = rms_norm(h, norm2_g[l])
        h = h + memory_cross_attention(c, mem, mem_norm_g[l], w_xq[l], w_xkv[l], w_xo[l])
        f = rms_norm(h, norm3_g[l])
        h = h + moe_ffn(f, w_router[l], b_router[l], w_gate[l], b_gate[l], w_up[l], b_up[l],
                        w_down[l], b_down[l])
    return rms_norm(h, final_norm_g)


_drawn_inputs = setup_inputs


def setup_inputs(seed=0):
    import zlib

    import numpy as np

    out = dict(_drawn_inputs(seed))
    spreads = {}
    factors = {'gla_norm_g': 2.854,
     'b_branch_gate': 4.863,
     'norm2_g': 4.011,
     'mem_norm_g': 2.842,
     'b_gate': 6.466,
     'b_up': 22.514,
     'b_down': 24.591,
     'final_norm_g': 30.228,
     'norm3_g': 3.319,
     'b_router': 4.015}
    for name, (base, spread) in spreads.items():
        noise = np.random.default_rng([zlib.crc32(name.encode()), seed]).standard_normal(out[name].shape)
        drawn = base * np.exp(spread * noise) if base else spread * noise
        out[name] = __import__('jax').numpy.asarray(drawn.astype(out[name].dtype))
    for name, factor in factors.items():
        out[name] = (out[name] * factor).astype(out[name].dtype)
    return out
```

```python
from contextlib import ExitStack

import numpy as np

import concourse.bass as bass
from concourse import mybir

F32 = mybir.dt.float32
I32 = mybir.dt.int32
U32 = mybir.dt.uint32
ALU = mybir.AluOpType
ACT = mybir.ActivationFunctionType
AX = mybir.AxisListType.X

P = 128
T = 256
TT = T // P
D = 1024
C = D // P
M = 256
EPS = 1e-5
DK = 64
GH = 4
DH = 128
NG = 3
NH = 4
SUB = 32
NSUB = P // SUB
E = 32
TOPK = 4
SLOTS = 64
EG = 4
GROUPS = E // EG
ROUNDS = T // SLOTS
LIMIT = 7.0
ALPHA = 1.702
NEG = -1.0e30
GLA_SCALE = DK ** -0.5
ATT_SCALE = DH ** -0.5
TWO_PI_HI = 6.28125
TWO_PI_LO = 2 * np.pi - TWO_PI_HI
MAGIC = 12582912.0

UNIT = 4096
NSLOT = 8
EARLY = 3
BANKS = 8

UNITS = (["qk_g", "v_g", "r_g", "q_d0", "q_d1", "q_d2", "k_d0", "k_d1", "k_d2", "v_d0", "v_d1", "v_d2",
          "gate0", "gate1", "gate2", "gate3", "xk", "xv", "b_gla", "b_dil", "mix0", "mix1", "xq", "xo"])

FILLS = ["bias", "vec"] + [f"x_T{i}" for i in range(4)] + ["alr", "q_g", "k_g", "v_g0", "v_g1", "r_g0", "r_g1", "lg"]
FILLS += [f"q_d{g}{a}" for g in range(NG) for a in range(2)] + ["cum"]
FILLS += [f"k_d{g}{a}" for g in range(NG) for a in range(2)]
FILLS += [f"gs{h}" for h in range(GH)]
FILLS += [f"v_d{g}{t}" for g in range(NG) for t in range(TT)]
FILLS += [f"m_T{i}" for i in range(4)] + ["go0", "go1"]
for _h in range(NH):
    FILLS += [f"s{_h}0", f"s{_h}1a", f"s{_h}1b", f"eg{2 * _h}", f"eg{2 * _h + 1}"]
    if _h == 0:
        FILLS += ["gt0", "gt1"]
    else:
        FILLS += [f"pt{_h - 1}{g}" for g in range(NG)]
    if _h == 2:
        FILLS += ["pv0"]
FILLS += ["xk0", "xk1", "xv0", "xv1"] + [f"pt3{g}" for g in range(NG)] + ["pv1"]
for _i in range(4):
    FILLS += [f"bg{_i}", f"bd{_i}"]
FILLS += [f"mix{t}{n}" for t in range(TT) for n in range(2)]
FILLS += [f"c_T{i}" for i in range(4)] + ["xq0", "xq1"]
FILLS += ["xs0", "xs1", "xt0", "xs2", "xt1", "xpv0", "xs3", "xt2", "xt3", "xpv1"]
FILLS += [f"xo{t}{n}" for t in range(TT) for n in range(2)]
FILLS += [f"f_T{i}" for i in range(4)] + ["rt", "pos", "gT"]
assert len(set(FILLS)) == len(FILLS)
LAST_FILL = {"qk_g": "k_g", "v_g": "v_g1", "r_g": "r_g1", "xk": "xk1", "xv": "xv1", "b_gla": "bg3", "b_dil": "bd3",
             "mix0": "mix11", "mix1": "mix11", "xq": "xq1", "xo": "xo11"}
LAST_FILL.update({f"{k}{g}": f"{k}{g}1" for k in ("q_d", "k_d", "v_d") for g in range(3)})
LAST_FILL.update({f"gate{q}": f"eg{2 * q + 1}" for q in range(4)})
BANK = {f: i % BANKS for i, f in enumerate(FILLS)}
TURN = {f: i // BANKS for i, f in enumerate(FILLS)}
USES = [sum(BANK[f] == b for f in FILLS) for b in range(BANKS)]


def _program(nc, A, out):
    ctx = ExitStack()
    with ctx:
        def sb(name, shape, dt=F32):
            return ctx.enter_context(nc.sbuf_tensor(name, shape, dt))

        def sem(name):
            return ctx.enter_context(nc.semaphore(name))

        ring = sb("ring", [P, NSLOT * UNIT])
        h = sb("h", [P, TT, D])
        reg_a = sb("reg_a", [P, C * T])
        reg_m = sb("reg_m", [P, C * T])
        reg_t = sb("reg_t", [P, C * T])
        reg_g = sb("reg_g", [P, 2 * C * T])
        reg_o = sb("reg_o", [P, 8 * T])
        reg_l = sb("reg_l", [P, 3072])
        ident = sb("ident", [P, P])
        tri16 = sb("tri16", [P, P])
        tri_s = sb("tri_s", [P, P])
        ones = sb("ones", [P, P])
        masks = sb("masks", [P, 6, P])
        vT = sb("vT", [P, 44])
        iota_s = sb("iota_s", [P, SLOTS])
        iota_e = sb("iota_e", [P, E])
        bT = sb("bT", [P, 2, C, E])
        g3 = sb("g3", [P, C])
        w_rt = sb("w_rt", [P, C, E])
        b_rt = sb("b_rt", [1, E])
        route = sb("route", [P, 3, TT, E])
        st = sb("st", [P, 64])
        neg_half = sb("neg_half", [P, 4])
        over = sb("over", [P, 1], I32)

        place, gate, mask = route[:, 0], route[:, 1], route[:, 2]

        def region(r, at, *shape):
            n = int(np.prod(shape))
            v = r[:, at:at + n]
            if len(shape) == 1:
                return v
            names = "abcdef"[:len(shape)]
            return v.rearrange(f"p ({' '.join(names)}) -> p {' '.join(names)}",
                               **{k: s for k, s in zip(names[1:], shape[1:])})

        slot = [region(ring, s * UNIT, UNIT) for s in range(NSLOT)]
        at = EARLY * UNIT
        qr = region(ring, at, NG * 2, 2, T)
        kr = region(ring, at + 3072, NG * 2, 2, T)
        vd = region(ring, at + 6144, TT, NG * NH * DH)
        brows = region(ring, at + 6144, 2, D)
        kS = region(ring, at + 9216, 2, TT, NSUB, P)
        S = region(ring, at + 11264, 2, 9 * P)
        rot = region(ring, at + 11264, 2, 2, T)
        PT = region(ring, at + 13568, 2, NG, 3 * P)
        B = region(ring, at + 13568, 2, T)
        scT = region(ring, at + 15872, GH, 3 * P)
        og = region(ring, at + 17408, TT, GH * P)
        sr = region(ring, at + 18432, TT, GH * P)
        la = region(ring, at + 19456, TT, T)
        cs = region(ring, at + 19968, 2, T)

        aT = region(reg_a, 0, C, T)
        xg = region(reg_a, 0, C, T)
        memx = region(reg_m, 0, TT, D)
        mergedT = region(reg_m, 0, C, T)
        f = region(reg_m, 0, TT, C, P)
        out_sb = region(reg_m, 0, TT, D)
        memT = region(reg_t, 0, C, T)
        hs = region(reg_t, 0, C, P)
        y = region(reg_t, 1024, 512)
        sel = region(reg_t, 1536, TT, EG * SLOTS)
        xn = region(reg_g, 0, TT, D)
        alr = region(reg_g, 2048, T)
        w2 = region(reg_g, 2304, T)
        w_alr = region(reg_g, 2560, C, 16)
        trig = region(reg_g, 2688, 3, T)
        lnz = region(reg_g, 3456, TT, T)
        gates = region(reg_g, 0, 2 * C, T)
        xP = region(reg_g, 2048, 2, TT, M)
        xPT = region(reg_g, 3072, 2, 2, T)
        oneh = region(reg_g, 0, 2 * TT * TOPK, E)
        selG = region(reg_g, 0, TT, EG, 2, SLOTS)
        selT = region(reg_g, 1024, EG, TT, P)
        g_sb = region(reg_g, 2048, C, SLOTS)
        sg_sb = region(reg_g, 2560, C, SLOTS)
        l_sb = region(reg_g, 3072, C, SLOTS)
        actT = region(reg_g, 3584, C, SLOTS)
        ogT = region(reg_o, 0, 4, T)
        odT = region(reg_o, 1024, 4, T)
        oxT = region(reg_o, 0, 4, T)
        gateT = region(reg_o, 1024, T)
        qg = region(reg_l, 0, 2, T)
        kg = region(reg_l, 512, 2, T)
        vg = region(reg_l, 1024, TT, GH * P)
        qS = region(reg_l, 2048, 2, T)
        qX = region(reg_l, 2560, 2, P)
        kX = region(reg_l, 2816, 2, P)
        xq = region(reg_l, 0, NH, T)
        xk = region(reg_l, 1024, NH, M)
        xv = region(reg_l, 2048, TT, NH * DH)
        b_dn = region(reg_l, 0, D)
        gfin = region(reg_l, 1024, D)
        rows = region(reg_l, 0, P)
        pos_i = region(reg_l, 512, T).bitcast(I32)
        invf = region(reg_l, 768, 1)
        diff_i = region(reg_l, 1024, P).bitcast(I32)
        mod_i = region(reg_l, 1152, P).bitcast(I32)
        mod_f = region(reg_l, 1280, P)
        idx_u = region(reg_l, 2048, TT, 8).bitcast(U32)
        idx_f = region(reg_l, 2064, TT, TOPK)
        top = region(reg_l, 2080, TT, 8)
        g4 = region(reg_l, 2096, TT, TOPK)
        logit = region(reg_l, 2112, TT, E)

        pt = [ctx.enter_context(nc.psum_tensor(f"bank{b}", [P, 512], F32)) for b in range(BANKS)]

        ld_x, ld_mem, ld_small, ld_late, ld_brows, consts = (sem(n) for n in
            ("ld_x", "ld_mem", "ld_small", "ld_late", "ld_brows", "consts"))
        early_ld = [sem(f"early_ld{s}") for s in range(EARLY)]
        late_ld = [sem(f"late_ld{s}") for s in range(NSLOT)]
        gu_half, dn_half = sem("gu_half"), sem("dn_half")
        full = [sem(f"full{b}") for b in range(BANKS)]
        free = [sem(f"free{b}") for b in range(BANKS)]
        dve_chain, act_chain, pool_chain = sem("dve_chain"), sem("act_chain"), sem("pool_chain")
        norm_ss, norm_xn = sem("norm_ss"), sem("norm_xn")
        trig_in, trig_out = sem("trig_in"), sem("trig_out")
        mod_ready, masks_ready = sem("mod_ready"), sem("masks_ready")
        th_r, ln_ready, anchors, gla_exp, gla_qk, go_ss = (sem(n) for n in
            ("th_r", "ln_ready", "anchors", "gla_exp", "gla_qk", "go_ss"))
        s_ready, s_exp, s_prob, merged_ready = (sem(n) for n in ("s_ready", "s_exp", "s_prob", "merged_ready"))
        xs_max, xs_exp, xs_prob = sem("xs_max"), sem("xs_exp"), sem("xs_prob")
        top_ready, top_exp, gate_ready, over_ready = (sem(n) for n in
            ("top_ready", "top_exp", "gate_ready", "over_ready"))
        sel_ready, gathered, xg_act, xg_dve, selT_full, selT_act, selT_dve = (sem(n) for n in
            ("sel_ready", "gathered", "xg_act", "xg_dve", "selT_full", "selT_act", "selT_dve"))
        h_full, hs_act, hs_dve, T_full, g_ready, sg_ready, act_ready, y_full, y_ready, moe_chain = (sem(n) for n in
            ("h_full", "hs_act", "hs_dve", "T_full", "g_ready", "sg_ready", "act_ready", "y_full", "y_ready",
             "moe_chain"))
        root_asked, root_done = sem("root_asked"), sem("root_done")
        lin_chain, round_chain = sem("lin_chain"), sem("round_chain")
        acc_full, fin_ss, fin_ready, stored = sem("acc_full"), sem("fin_ss"), sem("fin_ready"), sem("stored")

        def take(eng, name):
            eng.wait_ge(full[BANK[name]], TURN[name] + 1)
            return pt[BANK[name]]

        def emptied(eng, name):
            eng.wait_ge(free[BANK[name]], TURN[name] + 1)

        def chain(eng, s):
            count = [0]

            def link(ins):
                count[0] += 1
                ins.then_inc(s, 1)
                eng.wait_ge(s, count[0])
            return link

        def bc(ap, n):
            return ap.unsqueeze(2).to_broadcast([ap.shape[0], ap.shape[1], n])

        def mid(ap, n):
            return ap.unsqueeze(1).to_broadcast([ap.shape[0], n, ap.shape[1]])

        OFF_QG, OFF_VG, OFF_RG, OFF_AL, OFF_QD = 0, 512, 1024, 1536, 1552
        w_in = A["w_in"][0].rearrange("(c p) n -> p c n", p=P)
        w_gate_br = A["w_branch_gate"][0].rearrange("(c p) n -> p c n", p=P)
        w_xkv = A["w_xkv"][0].rearrange("(c p) n -> p c n", p=P)
        w_mix = A["w_mix_out"][0].rearrange("(c p) n -> p c n", p=P)
        SRC = {"qk_g": w_in[:, :, OFF_QG:OFF_QG + 512], "v_g": w_in[:, :, OFF_VG:OFF_VG + 512],
               "r_g": w_in[:, :, OFF_RG:OFF_RG + 512],
               "xk": w_xkv[:, :, 0:512], "xv": w_xkv[:, :, 512:1024],
               "b_gla": A["w_branch_gla"][0].rearrange("(c p) n -> p c n", p=P),
               "b_dil": A["w_branch_dil"][0].rearrange("(c p) n -> p c n", p=P),
               "mix0": w_mix[:, 0:4, :], "mix1": w_mix[:, 4:8, :],
               "xq": A["w_xq"][0].rearrange("(c p) n -> p c n", p=P),
               "xo": A["w_xo"][0].rearrange("(c p) n -> p c n", p=P)}
        for g in range(NG):
            for i, k in enumerate(("q_d", "k_d", "v_d")):
                o = OFF_QD + (i * NG + g) * 512
                SRC[f"{k}{g}"] = w_in[:, :, o:o + 512]
        for q in range(4):
            SRC[f"gate{q}"] = w_gate_br[:, :, q * 512:(q + 1) * 512]

        def unit(name):
            src = SRC[name]
            return slot[UNITS.index(name) % EARLY].rearrange("p (c n) -> p c n", n=src.shape[2])

        block = ctx.enter_context(nc.Block())

        def expert_groups(eng, body):
            with eng.Fori(0, GROUPS) as n:
                body(n, n)
            eng.wait_ge(over_ready, 1)
            more = eng.value_load(over[0:1, 0:1], min_val=0, max_val=1)
            with eng.If(more > 0):
                with eng.Fori(1, ROUNDS) as r:
                    if eng.engine == nc.vector.engine:
                        next_round(eng, r)
                    with eng.Fori(0, GROUPS) as n:
                        body(n, r * GROUPS + n)
                eng.nop()

        @block.sync
        def _(sp):
            for u, name in enumerate(UNITS):
                if u >= EARLY:
                    take(sp, LAST_FILL[UNITS[u - EARLY]])
                sp.dma_start(unit(name), SRC[name]).then_inc(early_ld[u % EARLY], 16)

            mats = [A[k][0].rearrange("e (p c) n -> e p (c n)", c=C) for k in ("w_gate", "w_up", "w_down")]
            ORDER = ((0, 0), (1, 0), (0, 1), (1, 1), (2, 0), (2, 1))

            def load(v, e, m, half):
                s = v % NSLOT
                src = mats[m][bass.ds(e, 1), :, half * UNIT:(half + 1) * UNIT]
                sp.dma_start(slot[s], src.rearrange("e p n -> p (e n)")).then_inc(late_ld[s], 16)

            per = 6 * EG
            LEFT = (gu_half, gu_half, h_full, h_full, dn_half, y_full)

            def slot_left(v, e0):
                sp.wait_ge(LEFT[(v - NSLOT) % 6], e0 + ((v - NSLOT) // 6 + 1))

            for v in range(per):
                if v < EARLY:
                    take(sp, LAST_FILL[UNITS[len(UNITS) - EARLY + v]])
                elif v == EARLY:
                    take(sp, "pv1")
                elif v >= NSLOT:
                    slot_left(v, 0)
                load(v, v // 6, *ORDER[v % 6])

            def body(n, k):
                for v in range(per):
                    slot_left(v, k * EG)
                    load(v, n * EG + v // 6, *ORDER[v % 6])

            with sp.Fori(1, GROUPS) as n:
                body(n, n)
            sp.wait_ge(over_ready, 1)
            more = sp.value_load(over[0:1, 0:1], min_val=0, max_val=1)
            with sp.If(more > 0):
                with sp.Fori(1, ROUNDS) as r:
                    with sp.Fori(0, GROUPS) as n:
                        body(n, r * GROUPS + n)
                sp.nop()
            for t in range(TT):
                sp.wait_ge(fin_ready, t + 1)
                sp.dma_start(out[0, t * P:(t + 1) * P, :], out_sb[:, t, :]).then_inc(stored, 16)
            sp.wait_ge(stored, 16 * TT)

        SMALL = 16 * 9

        @block.gpsimd
        def _(pool):
            link = chain(pool, pool_chain)
            roots = [0]

            def root(a, b):
                roots[0] += 1
                pool.wait_ge(root_asked, roots[0])
                pool.tensor_tensor(st[:, a:b], st[:, a:b], neg_half[:, 0:b - a], ALU.pow).then_inc(root_done, 1)

            for name, at_row, n in (("norm1_g", 0, 8), ("mem_norm_g", 8, 8), ("norm2_g", 16, 8),
                                    ("gla_norm_g", 24, 4), ("b_branch_gate", 28, 16)):
                pool.dma_start(rows[at_row:at_row + n, :],
                               A[name][0].rearrange("(c p) -> c p", p=P)).then_inc(ld_small, 16)
            pool.dma_start(w2[0:16, :], A["w_gla_a2"][0]).then_inc(ld_small, 16)
            pool.dma_start(w2[16:17, :], A["b_gla_a2"]).then_inc(ld_small, 16)
            pool.dma_start(invf, A["inv_freq"]).then_inc(ld_small, 16)
            pool.dma_start(pos_i, A["positions"].to_broadcast([P, T])).then_inc(ld_small, 16)
            link(pool.memset(ident[:], 0.0))
            pool.affine_select(out=ident[:], in_=ident[:], compare_op=ALU.not_equal, fill=1.0, base=0,
                               pattern=[[-1, P]], channel_multiplier=1).then_inc(consts, 1)
            link(pool.memset(neg_half[:], -0.5))
            root(0, 2)
            link(pool.memset(tri16[:], 1.0 / 16))
            pool.affine_select(out=tri16[:], in_=tri16[:], compare_op=ALU.is_ge, fill=0.0, base=0,
                               pattern=[[1, P]], channel_multiplier=-1).then_inc(consts, 1)
            link(pool.memset(tri_s[:], 1.0))
            pool.affine_select(out=tri_s[:], in_=tri_s[:], compare_op=ALU.is_gt, fill=0.0, base=0,
                               pattern=[[1, P]], channel_multiplier=-1).then_inc(consts, 1)
            pool.memset(ones[:], 1.0).then_inc(consts, 1)
            pool.memset(alr[0:32, :], 1.0).then_inc(consts, 1)
            pool.memset(kS, 0.0).then_inc(consts, 1)
            pool.iota(iota_s[:], pattern=[[1, SLOTS]], base=0, channel_multiplier=0,
                      allow_small_or_imprecise_dtypes=True).then_inc(consts, 1)
            pool.iota(iota_e[:], pattern=[[1, E]], base=0, channel_multiplier=0,
                      allow_small_or_imprecise_dtypes=True).then_inc(consts, 1)
            pool.iota(diff_i, pattern=[[1, P]], base=T, channel_multiplier=-1).then_inc(consts, 1)
            pool.dma_start(w_alr, w_in[:, :, OFF_AL:OFF_AL + 16]).then_inc(ld_late, 16)
            pool.dma_start(w_rt[:], A["w_router"][0].rearrange("(p c) e -> p c e", c=C)).then_inc(ld_late, 16)
            pool.dma_start(b_rt[:], A["b_router"]).then_inc(ld_late, 16)
            pool.dma_start(g3[:], A["norm3_g"][0].rearrange("(p c) -> p c", c=C)).then_inc(ld_late, 16)
            link(pool.memset(masks[:, 0:2, :], 0.0))
            pool.affine_select(out=masks[:, 0, :], in_=masks[:, 0, :], compare_op=ALU.is_ge, fill=NEG, base=0,
                               pattern=[[1, P]], channel_multiplier=-1).then_inc(masks_ready, 1)
            pool.wait_ge(mod_ready, 1)
            for m in (1, 3, 5):
                pool.affine_select(out=masks[:, m, :], in_=masks[:, m, :], compare_op=ALU.is_ge, fill=NEG,
                                   base=0, pattern=[[-1, P]], channel_multiplier=1).then_inc(masks_ready, 1)
            root(2, 4)
            root(8, 12)
            root(12, 16)
            root(4, 6)
            take(pool, "xo11")
            pool.dma_start(b_dn[0:E, :], A["b_down"][0]).then_inc(ld_late, 16)
            pool.dma_start(gfin, A["final_norm_g"].rearrange("(a n) -> a n", a=1).to_broadcast([P, D]))\
                .then_inc(ld_late, 16)
            root(6, 8)
            pool.wait_ge(ld_late, 16 * 6)
            root(56, 57)
            root(58, 59)

        @block.scalar
        def _(act):
            link = chain(act, act_chain)
            xt_src = A["x"][0].rearrange("(t p) d -> p t d", p=P)
            for t in range(TT):
                act.dma_start(h[:, t, :], xt_src[:, t, :]).then_inc(ld_x, 16)
            for i, k in enumerate(("b_gate", "b_up")):
                act.dma_start(brows[0:E, i, :], A[k][0]).then_inc(ld_brows, 16)
            act.dma_start(memx, A["mem"][0].rearrange("(t p) d -> p t d", p=P)).then_inc(ld_mem, 16)

            def copy(dst, src):
                return act.activation(dst, src, ACT.Copy)

            def free_bank(name):
                return free[BANK[name]]

            def squares(src, junk, at):
                for t in range(TT):
                    act.activation(junk[:, t, :], src[:, t, :], ACT.Square, accum_out=st[:, at + t:at + t + 1])\
                        .then_inc(norm_ss, 1)

            act.wait_ge(ld_x, 32)
            squares(h, xn, 0)
            for i in range(2):
                act.wait_ge(trig_in, i + 1)
                act.activation(cs[:, i, :], trig[:, 2, :], ACT.Sin).then_inc(trig_out, 1)
            b = take(act, "alr")
            act.wait_ge(consts, 9)
            copy(alr[0:16, :], b[0:16, 0:T]).then_inc(free_bank("alr"), 1)
            for name, dst in (("q_g", qg), ("k_g", kg)):
                b = take(act, name)
                if name == "q_g":
                    act.wait_ge(trig_in, 2)
                copy(dst.rearrange("p a b -> p (a b)"), b[:]).then_inc(free_bank(name), 1)
            act.wait_ge(masks_ready, 1)
            act.wait_ge(mod_ready, 1)
            for t in range(TT):
                b = take(act, f"v_g{t}")
                copy(vg[:, t, :], b[:]).then_inc(free_bank(f"v_g{t}"), 1)
            for t in range(TT):
                b = take(act, f"r_g{t}")
                act.activation(sr[:, t, :], b[:], ACT.Tanh, scale=0.5).then_inc(th_r, 1)
            b = take(act, "lg")
            link(act.activation(lnz.rearrange("p a b -> p (a b)"), b[:], ACT.Abs))
            link(act.activation(lnz, lnz, ACT.Exp, scale=-1.0))
            act.activation(lnz, lnz, ACT.Ln, bias=1.0).then_inc(ln_ready, 1)
            b = take(act, "cum")
            copy(B.rearrange("p a b -> p (a b)"), b[:]).then_inc(free_bank("cum"), 1)
            act.wait_ge(anchors, 1)
            for fc in range(2):
                for t in range(TT):
                    for i in range(NSUB):
                        a0 = t * P + i * SUB
                        act.activation(qS[:, fc, a0:a0 + SUB], B[:, fc, a0:a0 + SUB], ACT.Exp,
                                       bias=st[:, 16 + fc * 8 + t * 4 + i:17 + fc * 8 + t * 4 + i])
                        act.activation(kS[:, fc, t, i, 0:(i + 1) * SUB], B[:, fc, t * P:t * P + (i + 1) * SUB],
                                       ACT.Exp, scale=-1.0, bias=B[:, fc, a0 + SUB // 2:a0 + SUB // 2 + 1])
                act.activation(kX[:, fc, :], B[:, fc, 0:P], ACT.Exp, scale=-1.0, bias=B[:, fc, P - 1:P])
            act.activation(qX, B[:, :, P:T], ACT.Exp).then_inc(gla_exp, 1)
            for g in range(NG):
                for t in range(TT):
                    b = take(act, f"v_d{g}{t}")
                    copy(vd[:, t, g * 512:(g + 1) * 512], b[:])\
                        .then_inc(free_bank(f"v_d{g}{t}"), 1)
                    if g == 0 and t == 0:
                        act.wait_ge(ld_mem, 16)
                        squares(memx, xn, 2)
            for t in range(TT):
                b = take(act, f"go{t}")
                for hd in range(GH):
                    act.activation(og[:, t, hd * P:(hd + 1) * P], b[:, hd * P:(hd + 1) * P], ACT.Square,
                                   accum_out=st[:, 8 + t * 4 + hd:9 + t * 4 + hd]).then_inc(go_ss, 1)

            def softmax_exp(hd):
                act.wait_ge(s_ready, hd + 1)
                for t, (c0, c1) in enumerate(((0, 3 * P), (3 * P, 9 * P))):
                    act.activation(S[:, hd % 2, c0:c1], S[:, hd % 2, c0:c1], ACT.Exp, scale=ATT_SCALE,
                                   bias=st[:, 36 + 2 * (hd % 2) + t:37 + 2 * (hd % 2) + t],
                                   accum_out=st[:, 40 + 2 * (hd % 2) + t:41 + 2 * (hd % 2) + t]).then_inc(s_exp, 1)

            def probs_T(hd):
                for g in range(2):
                    b = take(act, f"pt{hd}{g}")
                    copy(PT[:, hd % 2, g, :], b[:, 0:3 * P]).then_inc(free_bank(f"pt{hd}{g}"), 1)

            def branch_gates(q):
                b = take(act, f"eg{q}")
                for i in range(2):
                    c = 2 * q + i
                    ins = act.activation(gates[:, c, :], b[:, i * T:(i + 1) * T], ACT.Tanh, scale=0.5,
                                         bias=vT[:, 28 + c:29 + c])
                ins.then_inc(free_bank(f"eg{q}"), 1)

            def out_T(a):
                b = take(act, f"pv{a}")
                copy(odT[:, 2 * a:2 * a + 2, :].rearrange("p a b -> p (a b)"), b[:])\
                    .then_inc(free_bank(f"pv{a}"), 1)

            for hd in range(NH):
                softmax_exp(hd)
                branch_gates(2 * hd)
                branch_gates(2 * hd + 1)
                if hd >= 1:
                    probs_T(hd - 1)
                if hd == 2:
                    out_T(0)
            for a in range(2):
                b = take(act, f"xk{a}")
                copy(xk[:, 2 * a:2 * a + 2, :].rearrange("p a b -> p (a b)"), b[:]).then_inc(free_bank(f"xk{a}"), 1)
            for t in range(TT):
                b = take(act, f"xv{t}")
                copy(xv[:, t, :], b[:]).then_inc(free_bank(f"xv{t}"), 1)
            probs_T(3)
            out_T(1)
            for name in ("mix00", "mix01", "mix10", "mix11"):
                emptied(act, name)
            squares(h, xn, 4)
            for a in range(2):
                b = take(act, f"xq{a}")
                copy(xq[:, 2 * a:2 * a + 2, :].rearrange("p a b -> p (a b)"), b[:])\
                    .then_inc(free_bank(f"xq{a}"), 1)

            def x_exp(hd):
                act.wait_ge(xs_max, hd + 1)
                b = pt[BANK[f"xs{hd}"]]
                for t in range(TT):
                    act.activation(xP[:, hd % 2, t, :], b[:, t * M:(t + 1) * M], ACT.Exp, scale=ATT_SCALE,
                                   bias=st[:, 44 + 2 * (hd % 2) + t:45 + 2 * (hd % 2) + t],
                                   accum_out=st[:, 48 + 2 * (hd % 2) + t:49 + 2 * (hd % 2) + t])\
                        .then_inc(xs_exp if t == 0 else free_bank(f"xs{hd}"), 1)

            def x_probs_T(hd):
                b = take(act, f"xt{hd}")
                copy(xPT[:, hd % 2].rearrange("p a b -> p (a b)"), b[:]).then_inc(free_bank(f"xt{hd}"), 1)

            def x_out_T(a):
                b = take(act, f"xpv{a}")
                copy(oxT[:, 2 * a:2 * a + 2, :].rearrange("p a b -> p (a b)"), b[:])\
                    .then_inc(free_bank(f"xpv{a}"), 1)

            x_exp(0)
            x_exp(1)
            x_probs_T(0)
            x_exp(2)
            x_probs_T(1)
            x_out_T(0)
            x_exp(3)
            x_probs_T(2)
            x_probs_T(3)
            x_out_T(1)
            for name in ("xo00", "xo01", "xo10", "xo11"):
                emptied(act, name)
            squares(h, xn, 6)
            act.wait_ge(top_ready, 1)
            for t in range(TT):
                act.activation(g4[:, t, :], top[:, t, 0:TOPK], ACT.Exp, bias=st[:, 52 + t:53 + t],
                               accum_out=st[:, 54 + t:55 + t]).then_inc(top_exp, 1)

            def body(n, k):
                for q in (0, 2):
                    act.wait_ge(gathered, 4 * k + (q + 1))
                    for i in range(2):
                        c = 2 * q + i
                        ins = act.activation(xg[:, c, :], pt[q][:, i * T:(i + 1) * T], ACT.Copy,
                                             scale=g3[:, c:c + 1])
                    ins.then_inc(xg_act, 1)
                act.wait_ge(selT_full, 2 * k + 1)
                copy(selT[:, 0:2].rearrange("p e t s -> p (e t s)"), pt[0][:]).then_inc(selT_act, 1)
                for j in range(EG):
                    act.wait_ge(h_full, k * EG + (j + 1))
                    copy(hs[:, :, 0:64], pt[0][:].rearrange("p (q c) -> p c q", c=C)).then_inc(hs_act, 1)
                    for i in range(2):
                        act.wait_ge(g_ready, k * 2 * EG + (2 * j + i + 1))
                        act.activation(sg_sb[:, 4 * i:4 * i + 4, :], g_sb[:, 4 * i:4 * i + 4, :], ACT.Sigmoid,
                                       scale=ALPHA).then_inc(sg_ready, 1)
                    act.wait_ge(y_full, k * EG + (j + 1))
                    copy(y, pt[2][:]).then_inc(y_ready, 1)

            expert_groups(act, body)

            for t in range(TT):
                act.wait_ge(acc_full, 2 * t + 2)
                for i in range(2):
                    act.activation(out_sb[:, t, i * 512:(i + 1) * 512], pt[4 + 2 * t + i][:], ACT.Square,
                                   accum_out=st[:, 56 + 2 * t + i:57 + 2 * t + i]).then_inc(fin_ss, 1)

        LINKS = 2 + 3 * 2 * EG

        def next_round(dve, r):
            dve.wait_ge(round_chain, r)
            dve.tensor_scalar(place, place, -float(SLOTS), None, ALU.add).then_inc(round_chain, 1)
            dve.wait_ge(round_chain, r + 1)
            dve.memset(st[:, 62:63], 0.0)

        @block.vector
        def _(dve):
            link = chain(dve, dve_chain)

            roots = [0]

            def rsqrt_mean(dst, src, n):
                dve.tensor_scalar(dst, src, 1.0 / n, EPS, ALU.mult, ALU.add).then_inc(root_asked, 1)
                roots[0] += 1
                dve.wait_ge(root_done, roots[0])

            def free_bank(name):
                return free[BANK[name]]

            def normed(src, dst, at):
                dve.wait_ge(norm_ss, at + 2)
                rsqrt_mean(st[:, at:at + 2], st[:, at:at + 2], D)
                for t in range(TT):
                    dve.tensor_scalar(dst(t), src(t), st[:, at + t:at + t + 1], None, ALU.mult)\
                        .then_inc(norm_xn, 1)

            def norm_out(prefix, dst, gain):
                for q in range(4):
                    b = take(dve, f"{prefix}{q}")
                    dve.tensor_tensor(dst[:, 2 * q:2 * q + 2, :], b[:].rearrange("p (a b) -> p a b", a=2),
                                      bc(gain[:, 2 * q:2 * q + 2], T), ALU.mult)\
                        .then_inc(free_bank(f"{prefix}{q}"), 1)

            normed(lambda t: h[:, t, :], lambda t: xn[:, t, :], 0)
            b = take(dve, "bias")
            dve.tensor_copy(bT[:].rearrange("p a c e -> p (a c e)"), b[:]).then_inc(free_bank("bias"), 1)
            b = take(dve, "vec")
            dve.tensor_copy(vT[:, 0:24], b[:, 0:24])
            dve.tensor_scalar(vT[:, 24:44], b[:, 24:44], 0.5, None, ALU.mult).then_inc(free_bank("vec"), 1)
            emptied(dve, "vec")
            norm_out("x_T", aT, vT[:, 0:8])
            dve.wait_ge(ld_small, SMALL)
            link(dve.tensor_copy(trig[:, 1, :], pos_i))
            link(dve.tensor_scalar(trig[:, 0, :], trig[:, 1, :], invf, None, ALU.mult))
            for i, phase in enumerate((np.pi / 2, 0.0)):
                link(dve.tensor_scalar(trig[:, 1, :], trig[:, 0, :], float(0.5 / np.pi), float(phase * 0.5 / np.pi),
                                       ALU.mult, ALU.add))
                link(dve.tensor_scalar(trig[:, 1, :], trig[:, 1, :], MAGIC, None, ALU.add))
                link(dve.tensor_scalar(trig[:, 1, :], trig[:, 1, :], -MAGIC, None, ALU.add))
                if i:
                    dve.wait_ge(trig_out, 1)
                link(dve.scalar_tensor_tensor(trig[:, 2, :], trig[:, 1, :], -TWO_PI_HI, trig[:, 0, :],
                                              ALU.mult, ALU.add))
                link(dve.scalar_tensor_tensor(trig[:, 2, :], trig[:, 1, :], -float(TWO_PI_LO), trig[:, 2, :],
                                              ALU.mult, ALU.add))
                link(dve.tensor_scalar(trig[:, 2, :], trig[:, 2, :], float(phase), 3.1415925, ALU.add, ALU.min))
                dve.tensor_scalar(trig[:, 2, :], trig[:, 2, :], -3.1415925, None, ALU.max).then_inc(trig_in, 1)
            dve.wait_ge(consts, 9)
            dve.wait_ge(masks_ready, 1)
            for m, d in ((2, 4), (4, 16)):
                link(dve.tensor_scalar(mod_i, diff_i, d - 1, None, ALU.bitwise_and))
                link(dve.tensor_copy(mod_f, mod_i))
                link(dve.tensor_scalar(mod_f, mod_f, 0.0, -NEG, ALU.is_equal, ALU.mult))
                link(dve.tensor_scalar(masks[:, m, :], mod_f, NEG, None, ALU.add))
                ins = dve.tensor_copy(masks[:, m + 1, :], masks[:, m, :])
            ins.then_inc(mod_ready, 1)
            for t in range(TT):
                b = take(dve, f"r_g{t}")
                dve.wait_ge(th_r, t + 1)
                dve.scalar_tensor_tensor(sr[:, t, :], sr[:, t, :], 1.0, b[:], ALU.add, ALU.mult)\
                    .then_inc(free_bank(f"r_g{t}"), 1)
            b = take(dve, "lg")
            dve.wait_ge(ln_ready, 1)
            dve.scalar_tensor_tensor(la.rearrange("p a b -> p (a b)"), b[:], 0.0,
                                     lnz.rearrange("p a b -> p (a b)"), ALU.min, ALU.subtract)\
                .then_inc(free_bank("lg"), 1)

            def rotary(name, dst, before):
                if before:
                    emptied(dve, before)
                b = take(dve, name)
                ps = b[:].rearrange("p (a b) -> p a b", a=2)
                dve.tensor_tensor(rot[:, 0], ps, mid(cs[:, 0, :], 2), ALU.mult)
                link(dve.tensor_tensor(rot[:, 1], ps, mid(cs[:, 1, :], 2), ALU.mult))
                dve.tensor_tensor(dst[:, 0, :], rot[:, 0, 0, :], rot[:, 1, 1, :], ALU.subtract)
                dve.tensor_tensor(dst[:, 1, :], rot[:, 0, 1, :], rot[:, 1, 0, :], ALU.add)\
                    .then_inc(free_bank(name), 1)

            dve.wait_ge(trig_out, 2)
            before = None
            for g in range(NG):
                for a in range(2):
                    rotary(f"q_d{g}{a}", qr[:, 2 * g + a], before)
                    before = f"q_d{g}{a}"
            emptied(dve, "cum")
            dve.tensor_scalar(st[:, 16:32].rearrange("p (f i) -> p f i", f=2),
                              B[:, :, SUB // 2::SUB], -1.0, None, ALU.mult).then_inc(anchors, 1)
            for a in range(2):
                rotary(f"k_d0{a}", kr[:, a], before)
                before = f"k_d0{a}"
            dve.wait_ge(gla_exp, 1)
            emptied(dve, "q_g")
            emptied(dve, "k_g")
            dve.scalar_tensor_tensor(qS, qS, 16 * GLA_SCALE, qg, ALU.mult, ALU.mult)
            dve.scalar_tensor_tensor(qX, qX, GLA_SCALE, qg[:, :, P:T], ALU.mult, ALU.mult)
            dve.tensor_tensor(kX, kX, kg[:, :, 0:P], ALU.mult)
            for t in range(TT):
                for i in range(NSUB):
                    n = (i + 1) * SUB
                    ins = dve.tensor_tensor(kS[:, :, t, i, 0:n], kS[:, :, t, i, 0:n], kg[:, :, t * P:t * P + n],
                                            ALU.mult)
            ins.then_inc(gla_qk, 1)
            for g in range(1, NG):
                for a in range(2):
                    rotary(f"k_d{g}{a}", kr[:, 2 * g + a], before)
                    before = f"k_d{g}{a}"
            for hd in range(GH):
                b = take(dve, f"gs{hd}")
                dve.tensor_tensor(scT[:, hd, 0:2 * P].rearrange("p (a b) -> p a b", a=2),
                                  b[:, 0:2 * P].rearrange("p (a b) -> p a b", a=2), mid(tri16[:], 2), ALU.mult)
                dve.tensor_copy(scT[:, hd, 2 * P:3 * P], b[:, 2 * P:3 * P]).then_inc(free_bank(f"gs{hd}"), 1)
            normed(lambda t: memx[:, t, :], lambda t: memx[:, t, :], 2)
            norm_out("m_T", memT, vT[:, 8:16])
            for t in range(TT):
                dve.wait_ge(go_ss, 4 * t + 4)
                rsqrt_mean(st[:, 8 + 4 * t:12 + 4 * t], st[:, 8 + 4 * t:12 + 4 * t], P)
                b = pt[BANK[f"go{t}"]]
                for hd in range(GH):
                    sl = slice(hd * P, (hd + 1) * P)
                    ins = dve.scalar_tensor_tensor(og[:, t, sl], b[:, sl], st[:, 8 + 4 * t + hd:9 + 4 * t + hd],
                                                   sr[:, t, sl], ALU.mult, ALU.mult)
                ins.then_inc(free_bank(f"go{t}"), 1)

            maskf = masks[:].rearrange("p m s -> p (m s)")

            def scores(hd):
                i = hd % 2
                dve.wait_ge(masks_ready, 4)
                b = take(dve, f"s{hd}0")
                dve.tensor_tensor_reduce(out=S[:, i, 0:3 * P].rearrange("p (g s) -> p g s", g=NG),
                                         in0=b[:, 0:3 * P].rearrange("p (g s) -> p g s", g=NG),
                                         in1=masks[:, 1::2, :], scale=1.0, scalar=-3e38, op0=ALU.add, op1=ALU.max,
                                         accum_out=st[:, 32:33]).then_inc(free_bank(f"s{hd}0"), 1)
                b = take(dve, f"s{hd}1a")
                dve.tensor_tensor_reduce(out=S[:, i, 3 * P:7 * P], in0=b[:], in1=maskf[:, 0:4 * P], scale=1.0,
                                         scalar=-3e38, op0=ALU.add, op1=ALU.max, accum_out=st[:, 33:34])\
                    .then_inc(free_bank(f"s{hd}1a"), 1)
                b = take(dve, f"s{hd}1b")
                dve.tensor_tensor_reduce(out=S[:, i, 7 * P:9 * P], in0=b[:, 0:2 * P], in1=maskf[:, 4 * P:6 * P],
                                         scale=1.0, scalar=-3e38, op0=ALU.add, op1=ALU.max,
                                         accum_out=st[:, 34:35]).then_inc(free_bank(f"s{hd}1b"), 1)
                emptied(dve, f"s{hd}1b")
                link(dve.tensor_tensor(st[:, 33:34], st[:, 33:34], st[:, 34:35], ALU.max))
                dve.tensor_scalar(st[:, 36 + 2 * i:38 + 2 * i], st[:, 32:34], -ATT_SCALE, None, ALU.mult)\
                    .then_inc(s_ready, 1)

            def probs(hd):
                i = hd % 2
                dve.wait_ge(s_exp, 2 * hd + 2)
                link(dve.reciprocal(st[:, 40 + 2 * i:42 + 2 * i], st[:, 40 + 2 * i:42 + 2 * i]))
                dve.tensor_scalar(S[:, i, 0:3 * P], S[:, i, 0:3 * P], st[:, 40 + 2 * i:41 + 2 * i], None, ALU.mult)
                dve.tensor_scalar(S[:, i, 3 * P:9 * P], S[:, i, 3 * P:9 * P], st[:, 41 + 2 * i:42 + 2 * i], None,
                                  ALU.mult).then_inc(s_prob, 1)

            def probs_T(hd):
                b = take(dve, f"pt{hd}2")
                dve.tensor_copy(PT[:, hd % 2, 2, :], b[:, 0:3 * P]).then_inc(free_bank(f"pt{hd}2"), 1)

            for hd in range(NH):
                scores(hd)
                probs(hd)
                if hd == 0:
                    for q in range(2):
                        b = take(dve, f"gt{q}")
                        dve.tensor_tensor(ogT[:, 2 * q:2 * q + 2, :], b[:].rearrange("p (a b) -> p a b", a=2),
                                          bc(vT[:, 24 + 2 * q:26 + 2 * q], T), ALU.mult).then_inc(free_bank(f"gt{q}"), 1)
                else:
                    probs_T(hd - 1)
            probs_T(3)
            for q in range(4):
                b = take(dve, f"bg{q}")
                if q == 0:
                    emptied(dve, "eg7")
                dst = mergedT[:, 2 * q:2 * q + 2, :].rearrange("p a b -> p (a b)")
                g0 = gates[:, 2 * q:2 * q + 2, :].rearrange("p a b -> p (a b)")
                g1 = gates[:, 8 + 2 * q:10 + 2 * q, :].rearrange("p a b -> p (a b)")
                dve.scalar_tensor_tensor(dst, g0, 1.0, b[:], ALU.add, ALU.mult).then_inc(free_bank(f"bg{q}"), 1)
                b = take(dve, f"bd{q}")
                dve.scalar_tensor_tensor(g1, g1, 1.0, b[:], ALU.add, ALU.mult).then_inc(free_bank(f"bd{q}"), 1)
                emptied(dve, f"bd{q}")
                dve.tensor_tensor(dst, dst, g1, ALU.add).then_inc(merged_ready, 1)
            for t in range(TT):
                for n in range(2):
                    b = take(dve, f"mix{t}{n}")
                    hh = h[:, t, n * 512:(n + 1) * 512]
                    dve.scalar_tensor_tensor(hh, b[:], 0.5, hh, ALU.mult, ALU.add)\
                        .then_inc(free_bank(f"mix{t}{n}"), 1)
            normed(lambda t: h[:, t, :], lambda t: xn[:, t, :], 4)
            norm_out("c_T", aT, vT[:, 16:24])

            def x_max(hd):
                i = hd % 2
                b = take(dve, f"xs{hd}")
                m = st[:, 32 + 2 * i:34 + 2 * i]
                link(dve.reduce_max(m, b[:].rearrange("p (a b) -> p a b", a=2), AX))
                dve.tensor_scalar(st[:, 44 + 2 * i:46 + 2 * i], m, -ATT_SCALE, None, ALU.mult)\
                    .then_inc(xs_max, 1)

            def x_prob(hd):
                i = hd % 2
                dve.wait_ge(xs_exp, hd + 1)
                emptied(dve, f"xs{hd}")
                link(dve.reciprocal(st[:, 48 + 2 * i:50 + 2 * i], st[:, 48 + 2 * i:50 + 2 * i]))
                for t in range(TT):
                    ins = dve.tensor_scalar(xP[:, i, t, :], xP[:, i, t, :], st[:, 48 + 2 * i + t:49 + 2 * i + t],
                                            None, ALU.mult)
                ins.then_inc(xs_prob, 1)

            x_max(0)
            x_max(1)
            for hd in range(NH):
                x_prob(hd)
                if hd + 2 < NH:
                    x_max(hd + 2)
            for t in range(TT):
                for n in range(2):
                    b = take(dve, f"xo{t}{n}")
                    hh = h[:, t, n * 512:(n + 1) * 512]
                    dve.tensor_tensor(hh, b[:], hh, ALU.add).then_inc(free_bank(f"xo{t}{n}"), 1)
            normed(lambda t: h[:, t, :].rearrange("p (q c) -> p c q", c=C), lambda t: f[:, t], 6)
            norm_out("f_T", aT, g3[:])
            b = take(dve, "rt")
            dve.tensor_copy(logit.rearrange("p a b -> p (a b)"), b[:, 0:TT * E]).then_inc(free_bank("rt"), 1)
            emptied(dve, "rt")
            for t in range(TT):
                link(dve.max(top[:, t, :], logit[:, t, :]))
                link(dve.max_index(idx_u[:, t, :], top[:, t, :], logit[:, t, :]))
            link(dve.tensor_copy(idx_f, idx_u[:, :, 0:TOPK]))
            dve.tensor_scalar(st[:, 52:54], top[:, :, 0], -1.0, None, ALU.mult).then_inc(top_ready, 1)
            hot, hot_g = oneh[:, 0:TT * TOPK, :], oneh[:, TT * TOPK:, :]
            link(dve.tensor_tensor(hot, mid(iota_e[:], TT * TOPK), bc(idx_f.rearrange("p a b -> p (a b)"), E),
                                   ALU.is_equal))
            dve.reduce_sum(mask, hot.rearrange("p (t k) e -> p t e k", t=TT), AX).then_inc(gate_ready, 1)
            dve.wait_ge(top_exp, 2)
            link(dve.reciprocal(st[:, 54:56], st[:, 54:56]))
            link(dve.tensor_tensor(g4, g4, bc(st[:, 54:56], TOPK), ALU.mult))
            link(dve.tensor_tensor(hot_g, hot, bc(g4.rearrange("p a b -> p (a b)"), E), ALU.mult))
            dve.reduce_sum(gate, hot_g.rearrange("p (t k) e -> p t e k", t=TT), AX).then_inc(gate_ready, 1)
            b = take(dve, "pos")
            link(dve.scalar_tensor_tensor(place.rearrange("p a b -> p (a b)"), b[:, 0:TT * E], 1.0,
                                          mask.rearrange("p a b -> p (a b)"), ALU.add, ALU.mult))
            link(dve.tensor_scalar(place, place, -1.0, None, ALU.add))
            link(dve.reduce_max(st[:, 60:61], b[:, TT * E:(TT + 1) * E], AX))
            dve.tensor_scalar(over[:], st[:, 60:61], float(SLOTS), None, ALU.is_gt).then_inc(over_ready, 1)
            dve.wait_ge(over_ready, 1)
            dve.memset(st[:, 61:62], 0.0).then_inc(free_bank("pos"), 1)
            b = take(dve, "gT")
            dve.tensor_copy(gateT[0:E, :], b[0:E, 0:T]).then_inc(free_bank("gT"), 1)
            dve.memset(st[:, 63:64], 0.0).then_inc(round_chain, 1)

            def body(n, k):
                count = [0]

                def link2(ins):
                    count[0] += 1
                    ins.then_inc(moe_chain, 1)
                    dve.wait_ge(moe_chain, k * LINKS + count[0])

                for t in range(TT):
                    link2(dve.tensor_tensor(sel[:, t, :].rearrange("p (e s) -> p e s", e=EG),
                                            bc(place[:, t, bass.ds(n * EG, EG)], SLOTS), mid(iota_s[:], EG),
                                            ALU.is_equal))
                for t in range(TT):
                    s4 = sel[:, t, :].rearrange("p (e s) -> p e s", e=EG)
                    ins = dve.tensor_tensor(
                        selG[:, t], s4.unsqueeze(2).to_broadcast([P, EG, 2, SLOTS]),
                        gate[:, t, bass.ds(n * EG, EG)].unsqueeze(2).unsqueeze(3).to_broadcast([P, EG, 2, SLOTS]),
                        ALU.mult)
                ins.then_inc(sel_ready, 1)
                for q in (1, 3):
                    dve.wait_ge(gathered, 4 * k + (q + 1))
                    dve.tensor_tensor(xg[:, 2 * q:2 * q + 2, :], pt[q][:].rearrange("p (a b) -> p a b", a=2),
                                      bc(g3[:, 2 * q:2 * q + 2], T), ALU.mult).then_inc(xg_dve, 1)
                dve.wait_ge(selT_full, 2 * k + 2)
                dve.tensor_copy(selT[:, 2:4].rearrange("p e t s -> p (e t s)"), pt[1][:]).then_inc(selT_dve, 1)
                for j in range(EG):
                    e = n * EG + j
                    dve.wait_ge(h_full, k * EG + (j + 1))
                    dve.tensor_copy(hs[:, :, 64:128], pt[1][:].rearrange("p (q c) -> p c q", c=C))\
                        .then_inc(hs_dve, 1)
                    for i in range(2):
                        cc = slice(4 * i, 4 * i + 4)
                        up = pt[i][:].rearrange("p (c b s) -> p b c s", c=4, b=2)
                        bias = [bT[:, b, cc, bass.ds(e, 1)].to_broadcast([P, 4, SLOTS]) for b in range(2)]
                        dve.wait_ge(T_full, k * 2 * EG + (2 * j + i + 1))
                        link2(dve.tensor_tensor(g_sb[:, cc, :], up[:, 0], bias[0], ALU.add))
                        dve.tensor_scalar(g_sb[:, cc, :], g_sb[:, cc, :], LIMIT, None, ALU.min)\
                            .then_inc(g_ready, 1)
                        link2(dve.tensor_tensor(l_sb[:, cc, :], up[:, 1], bias[1], ALU.add))
                        link2(dve.tensor_scalar(l_sb[:, cc, :], l_sb[:, cc, :], LIMIT, -LIMIT, ALU.min, ALU.max))
                        dve.scalar_tensor_tensor(l_sb[:, cc, :], l_sb[:, cc, :], 1.0, g_sb[:, cc, :],
                                                 ALU.add, ALU.mult).then_inc(lin_chain, 1)
                        dve.wait_ge(lin_chain, k * 2 * EG + (2 * j + i + 1))
                        dve.wait_ge(sg_ready, k * 2 * EG + (2 * j + i + 1))
                        dve.tensor_tensor(actT[:, cc, :], l_sb[:, cc, :], sg_sb[:, cc, :], ALU.mult)\
                            .then_inc(act_ready, 1)
                assert count[0] == LINKS, count[0]

            expert_groups(dve, body)

            for t in range(TT):
                dve.wait_ge(fin_ss, 2 * t + 2)
                v = st[:, 56 + 2 * t:57 + 2 * t]
                link(dve.tensor_tensor(v, v, st[:, 57 + 2 * t:58 + 2 * t], ALU.add))
                rsqrt_mean(v, v, D)
                if t == 0:
                    dve.wait_ge(ld_late, 16 * 6)
                for i in range(2):
                    ins = dve.scalar_tensor_tensor(out_sb[:, t, i * 512:(i + 1) * 512], pt[4 + 2 * t + i][:], v,
                                                   gfin[:, i * 512:(i + 1) * 512], ALU.mult, ALU.mult)
                ins.then_inc(fin_ready, 1)

        @block.tensor
        def _(pe):
            mm = pe.matmul

            def fill(name):
                if TURN[name]:
                    pe.wait_ge(free[BANK[name]], TURN[name])
                return pt[BANK[name]]

            def filled(ins, name):
                ins.then_inc(full[BANK[name]], 1)

            def weights(name):
                u = UNITS.index(name)
                pe.wait_ge(early_ld[u % EARLY], 16 * (u // EARLY + 1))
                return unit(name)

            def feature_major(name, w, cols, rhs, nk):
                b = fill(name)
                for i in range(2):
                    for c in range(nk):
                        ins = mm(b[:, i * T:(i + 1) * T], cols(w, c, i), rhs[:, c, :], start=(c == 0),
                                 stop=(c == nk - 1))
                filled(ins, name)

            def token_major(name, w, lhs, t, n0, ks):
                b = fill(name)
                for i, (c, row) in enumerate(ks):
                    ins = mm(b[:], lhs[:, c, t * P:(t + 1) * P], w[row][:, n0:n0 + 512],
                             start=(i == 0), stop=(i == len(ks) - 1))
                filled(ins, name)

            def norm_transposes(prefix, src, count):
                pe.wait_ge(norm_xn, count)
                for q in range(4):
                    b = fill(f"{prefix}{q}")
                    for i in range(2):
                        for t in range(TT):
                            ins = pe.transpose(b[:, i * T + t * P:i * T + (t + 1) * P], src(t, 2 * q + i), ident[:])
                    filled(ins, f"{prefix}{q}")

            pe.wait_ge(consts, 9)
            pe.wait_ge(ld_brows, 32)
            b = fill("bias")
            for k in range(2):
                for c in range(C):
                    o = (k * C + c) * E
                    ins = pe.transpose(b[:, o:o + E], brows[0:E, k, c::C], ident[0:E, 0:E])
            filled(ins, "bias")
            pe.wait_ge(ld_small, SMALL)
            b = fill("vec")
            filled(pe.transpose(b[:, 0:44], rows[0:44, :], ident[0:44, 0:44]), "vec")

            norm_transposes("x_T", lambda t, c: xn[:, t, c * P:(c + 1) * P], 2)
            for q in range(4):
                emptied(pe, f"x_T{q}")
            pe.wait_ge(ld_late, 64)
            b = fill("alr")
            for c in range(C):
                ins = mm(b[0:16, 0:T], w_alr[:, c, :], aT[:, c, :], start=(c == 0), stop=(c == C - 1))
            filled(ins, "alr")
            w = weights("qk_g")
            feature_major("q_g", w, lambda w, c, i: w[:, c, i * P:(i + 1) * P], aT, C)
            feature_major("k_g", w, lambda w, c, i: w[:, c, 256 + i * P:256 + (i + 1) * P], aT, C)
            for k in ("v_g", "r_g"):
                w = weights(k)
                rows_w = [w[:, c, :] for c in range(C)]
                for t in range(TT):
                    token_major(f"{k}{t}", rows_w, aT, t, 0, [(c, c) for c in range(C)])
            b = fill("lg")
            emptied(pe, "alr")
            for t in range(TT):
                ins = mm(b[:, t * T:(t + 1) * T], alr[0:17, t * P:(t + 1) * P], w2[0:17, :], start=True, stop=True)
            filled(ins, "lg")

            def rotary_halves(name, w, a):
                b = fill(name)
                for i in range(2):
                    for c in range(C):
                        for hp in range(2):
                            o = (2 * a + hp) * DH + 64 * i
                            ins = mm(b[64 * hp:64 * hp + 64, i * T:(i + 1) * T], w[:, c, o:o + 64], aT[:, c, :],
                                     start=(c == 0), stop=(c == C - 1))
                filled(ins, name)

            for g in range(NG):
                w = weights(f"q_d{g}")
                for a in range(2):
                    rotary_halves(f"q_d{g}{a}", w, a)
            b = fill("cum")
            emptied(pe, "lg")
            for fc in range(2):
                for t in range(TT):
                    ins = mm(b[:, fc * T + t * P:fc * T + (t + 1) * P], la[:, t, fc * P:(fc + 1) * P], tri16[:],
                             start=True, stop=True)
            filled(ins, "cum")
            for g in range(NG):
                w = weights(f"k_d{g}")
                for a in range(2):
                    rotary_halves(f"k_d{g}{a}", w, a)
            pe.wait_ge(gla_qk, 1)
            for hd in range(GH):
                b = fill(f"gs{hd}")
                hp, fc = slice(64 * (hd % 2), 64 * (hd % 2) + 64), hd // 2
                for t in range(TT):
                    for i in range(NSUB):
                        a0 = t * P + i * SUB
                        mm(b[:, a0:a0 + SUB], kS[hp, fc, t, i, :], qS[hp, fc, a0:a0 + SUB], start=True, stop=True)
                filled(mm(b[:, 2 * P:3 * P], kX[hp, fc, :], qX[hp, fc, :], start=True, stop=True), f"gs{hd}")
            for g in range(NG):
                w = weights(f"v_d{g}")
                for t in range(TT):
                    token_major(f"v_d{g}{t}", [w[:, c, :] for c in range(C)], aT, t, 0,
                                [(c, c) for c in range(C)])
            norm_transposes("m_T", lambda t, c: memx[:, t, c * P:(c + 1) * P], 4)
            emptied(pe, "gs3")
            emptied(pe, "v_g1")
            for t in range(TT):
                b = fill(f"go{t}")
                for hd in range(GH):
                    sl = slice(hd * P, (hd + 1) * P)
                    ins = mm(b[:, sl], scT[:, hd, t * P:(t + 1) * P], vg[:, t, sl], start=True, stop=(t == 0))
                    if t:
                        ins = mm(b[:, sl], scT[:, hd, 2 * P:3 * P], vg[:, 0, sl], start=False, stop=True)
                filled(ins, f"go{t}")

            def dil_scores(hd):
                hp, a = slice(64 * (hd % 2), 64 * (hd % 2) + 64), hd // 2

                def one(dst, g, t):
                    for j in range(2):
                        ins = mm(dst, qr[hp, 2 * g + a, j, t * P:(t + 1) * P], kr[hp, 2 * g + a, j, 0:(t + 1) * P],
                                 start=(j == 0), stop=(j == 1))
                    return ins
                b = fill(f"s{hd}0")
                for g in range(NG):
                    ins = one(b[:, g * P:(g + 1) * P], g, 0)
                filled(ins, f"s{hd}0")
                b = fill(f"s{hd}1a")
                for g in range(2):
                    ins = one(b[:, g * T:(g + 1) * T], g, 1)
                filled(ins, f"s{hd}1a")
                b = fill(f"s{hd}1b")
                filled(one(b[:, 0:T], 2, 1), f"s{hd}1b")

            def dil_transposes(hd):
                pe.wait_ge(s_prob, hd + 1)
                for g in range(NG):
                    b = fill(f"pt{hd}{g}")
                    for i, c0 in enumerate((g * P, 3 * P + g * T, 3 * P + g * T + P)):
                        ins = pe.transpose(b[:, i * P:(i + 1) * P], S[:, hd % 2, c0:c0 + P], ident[:])
                    filled(ins, f"pt{hd}{g}")

            def dil_out(a):
                b = fill(f"pv{a}")
                for i in range(2):
                    hd = 2 * a + i
                    for g in range(NG):
                        emptied(pe, f"pt{hd}{g}")
                        mm(b[:, i * T:(i + 1) * T], vd[:, 0, g * 512 + hd * P:g * 512 + (hd + 1) * P],
                           PT[:, i, g, 0:T], start=(g == 0), stop=False)
                    for g in range(NG):
                        ins = mm(b[:, i * T + P:(i + 1) * T], vd[:, 1, g * 512 + hd * P:g * 512 + (hd + 1) * P],
                                 PT[:, i, g, T:3 * P], start=False, stop=(g == NG - 1))
                filled(ins, f"pv{a}")

            plain = lambda a: (lambda w, c, i: w[:, c, (2 * a + i) * P:(2 * a + i + 1) * P])
            for hd in range(NH):
                dil_scores(hd)
                w = weights(f"gate{hd}")
                for a in range(2):
                    feature_major(f"eg{2 * hd + a}", w, plain(a), aT, C)
                if hd == 0:
                    emptied(pe, "go0")
                    emptied(pe, "go1")
                    for q in range(2):
                        b = fill(f"gt{q}")
                        for i in range(2):
                            for t in range(TT):
                                c = 2 * q + i
                                ins = pe.transpose(b[:, i * T + t * P:i * T + (t + 1) * P],
                                                   og[:, t, c * P:(c + 1) * P], ident[:])
                        filled(ins, f"gt{q}")
                else:
                    dil_transposes(hd - 1)
                if hd == 2:
                    dil_out(0)
            for q in range(4):
                emptied(pe, f"m_T{q}")
            w = weights("xk")
            for a in range(2):
                feature_major(f"xk{a}", w, plain(a), memT, C)
            w = weights("xv")
            for t in range(TT):
                token_major(f"xv{t}", [w[:, c, :] for c in range(C)], memT, t, 0, [(c, c) for c in range(C)])
            dil_transposes(3)
            dil_out(1)

            wg, wd = weights("b_gla"), weights("b_dil")
            for name in ("gt0", "gt1", "pv0", "pv1"):
                emptied(pe, name)
            for q in range(4):
                feature_major(f"bg{q}", wg, plain(q), ogT, 4)
                feature_major(f"bd{q}", wd, plain(q), odT, 4)
            wm = [weights("mix0"), weights("mix1")]
            mrows = [wm[c // 4][:, c % 4, :] for c in range(C)]
            pe.wait_ge(merged_ready, 4)
            for t in range(TT):
                for n in range(2):
                    b = fill(f"mix{t}{n}")
                    for c in range(C):
                        ins = mm(b[:], mergedT[:, c, t * P:(t + 1) * P], mrows[c][:, n * 512:(n + 1) * 512],
                                 start=(c == 0), stop=(c == C - 1))
                    filled(ins, f"mix{t}{n}")

            norm_transposes("c_T", lambda t, c: xn[:, t, c * P:(c + 1) * P], 6)
            for q in range(4):
                emptied(pe, f"c_T{q}")
            w = weights("xq")
            for a in range(2):
                feature_major(f"xq{a}", w, plain(a), aT, C)

            def x_scores(hd):
                emptied(pe, f"xq{hd // 2}")
                b = fill(f"xs{hd}")
                for t in range(TT):
                    ins = mm(b[:, t * M:(t + 1) * M], xq[:, hd, t * P:(t + 1) * P], xk[:, hd, :], start=True,
                             stop=True)
                filled(ins, f"xs{hd}")

            def x_transposes(hd):
                pe.wait_ge(xs_prob, hd + 1)
                b = fill(f"xt{hd}")
                for s in range(2):
                    for t in range(TT):
                        ins = pe.transpose(b[:, s * T + t * P:s * T + (t + 1) * P],
                                           xP[:, hd % 2, t, s * P:(s + 1) * P], ident[:])
                filled(ins, f"xt{hd}")

            def x_out(a):
                b = fill(f"xpv{a}")
                for i in range(2):
                    hd = 2 * a + i
                    emptied(pe, f"xt{hd}")
                    for s in range(2):
                        ins = mm(b[:, i * T:(i + 1) * T], xv[:, s, hd * P:(hd + 1) * P], xPT[:, i, s, :],
                                 start=(s == 0), stop=(s == 1))
                filled(ins, f"xpv{a}")

            for name in ("xk0", "xk1", "xv0", "xv1"):
                emptied(pe, name)
            x_scores(0)
            x_scores(1)
            x_transposes(0)
            x_scores(2)
            x_transposes(1)
            x_out(0)
            x_scores(3)
            x_transposes(2)
            x_transposes(3)
            x_out(1)
            w = weights("xo")
            emptied(pe, "xpv0")
            emptied(pe, "xpv1")
            for t in range(TT):
                for n in range(2):
                    b = fill(f"xo{t}{n}")
                    for c in range(4):
                        ins = mm(b[:], oxT[:, c, t * P:(t + 1) * P], w[:, c, n * 512:(n + 1) * 512],
                                 start=(c == 0), stop=(c == 3))
                    filled(ins, f"xo{t}{n}")

            norm_transposes("f_T", lambda t, c: f[:, t, c, :], 8)
            for q in range(4):
                emptied(pe, f"f_T{q}")
            b = fill("rt")
            for t in range(TT):
                for c in range(C):
                    mm(b[:, t * E:(t + 1) * E], aT[:, c, t * P:(t + 1) * P], w_rt[:, c, :], start=(c == 0), stop=False)
                ins = mm(b[:, t * E:(t + 1) * E], ones[0:1, :], b_rt[0:1, :], start=False, stop=True)
            filled(ins, "rt")
            pe.wait_ge(gate_ready, 1)
            b = fill("pos")
            mm(b[:, 0:E], tri_s[:], mask[:, 0, :], start=True, stop=True)
            mm(b[:, E:2 * E], tri_s[:], mask[:, 1, :], start=True, stop=False)
            mm(b[:, E:2 * E], ones[:], mask[:, 0, :], start=False, stop=True)
            mm(b[:, 2 * E:3 * E], ones[:], mask[:, 0, :], start=True, stop=False)
            filled(mm(b[:, 2 * E:3 * E], ones[:], mask[:, 1, :], start=False, stop=True), "pos")
            pe.wait_ge(gate_ready, 2)
            b = fill("gT")
            for t in range(TT):
                ins = pe.transpose(b[0:E, t * P:(t + 1) * P], gate[:, t, :], ident[:])
            filled(ins, "gT")

            acc = [[pt[4 + 2 * t + n] for n in range(2)] for t in range(TT)]
            for b in range(BANKS):
                pe.wait_ge(free[b], USES[b])
            for t in range(TT):
                for n in range(2):
                    mm(acc[t][n][:], ident[:], h[:, t, n * 512:(n + 1) * 512], start=True, stop=False)

            per = 6 * EG

            def body(n, k):
                pe.wait_ge(sel_ready, k + 1)
                for q in range(4):
                    for i in range(2):
                        for t in range(TT):
                            ins = mm(pt[q][:, i * T:(i + 1) * T], f[:, t, 2 * q + i, :], sel[:, t, :],
                                     start=(t == 0), stop=(t == TT - 1))
                    ins.then_inc(gathered, 1)
                for q in range(2):
                    if q == 0:
                        pe.wait_ge(xg_act, 2 * k + 1)
                    else:
                        pe.wait_ge(xg_dve, 2 * k + 1)
                    for i in range(2):
                        for t in range(TT):
                            o = (i * TT + t) * P
                            ins = pe.transpose(pt[q][:, o:o + P],
                                               selG[:, t, 2 * q + i].rearrange("p a s -> p (a s)"), ident[:])
                    ins.then_inc(selT_full, 1)
                pe.wait_ge(xg_act, 2 * k + 2)
                pe.wait_ge(xg_dve, 2 * k + 2)
                pe.wait_ge(selT_act, k + 1)
                pe.wait_ge(selT_dve, k + 1)

                def loaded(v):
                    pe.wait_ge(late_ld[v % NSLOT], k * (16 * per // NSLOT) + 16 * (v // NSLOT + 1))
                    return slot[v % NSLOT].rearrange("p (c n) -> p c n", n=D)

                for j in range(EG):
                    v = 6 * j
                    xe = [xg[:, c, j * SLOTS:(j + 1) * SLOTS] for c in range(C)]
                    for half in range(2):
                        wg, wu = loaded(v + 2 * half), loaded(v + 2 * half + 1)
                        for c4 in range(4):
                            c = 4 * half + c4
                            for nh in range(2):
                                for col, w in ((0, wg), (64, wu)):
                                    ins = mm(pt[nh][col:col + 64, :], xe[c], w[:, c4, nh * 512:(nh + 1) * 512],
                                             start=(c == 0), stop=(c == C - 1))
                        if half == 0:
                            ins.then_inc(gu_half, 1)
                    ins.then_inc(h_full, 1)
                    pe.wait_ge(hs_act, k * EG + (j + 1))
                    pe.wait_ge(hs_dve, k * EG + (j + 1))
                    for i in range(2):
                        for c in range(4):
                            ins = pe.transpose(pt[i][:, c * P:(c + 1) * P], hs[:, 4 * i + c, :], ident[:])
                        ins.then_inc(T_full, 1)
                    for half in range(2):
                        w = loaded(v + 4 + half)
                        pe.wait_ge(act_ready, k * 2 * EG + (2 * j + half + 1))
                        for c4 in range(4):
                            c = 4 * half + c4
                            for nh in range(2):
                                ins = mm(pt[2][64 * nh:64 * nh + 64, :], actT[:, c, :],
                                         w[:, c4, nh * 512:(nh + 1) * 512], start=(c == 0), stop=(c == C - 1))
                        if half == 0:
                            ins.then_inc(dn_half, 1)
                    ins.then_inc(y_full, 1)
                    pe.wait_ge(y_ready, k * EG + (j + 1))
                    for t in range(TT):
                        for nh in range(2):
                            rows_h = slice(64 * nh, 64 * nh + 64)
                            mm(acc[t][nh][:], selT[rows_h, j, t, :], y[rows_h, :], start=False, stop=False)

            expert_groups(pe, body)

            pe.wait_ge(ld_late, 16 * 6)
            for t in range(TT):
                for n in range(2):
                    mm(acc[t][n][:], gateT[0:E, t * P:(t + 1) * P], b_dn[0:E, n * 512:(n + 1) * 512],
                       start=False, stop=True).then_inc(acc_full, 1)


_INS = ['x', 'mem', 'positions', 'norm1_g', 'w_in', 'w_gla_a2', 'b_gla_a2', 'gla_norm_g', 'w_branch_gla',
        'w_branch_dil', 'w_branch_gate', 'b_branch_gate', 'w_mix_out', 'norm2_g', 'mem_norm_g', 'w_xq', 'w_xkv',
        'w_xo', 'norm3_g', 'w_router', 'b_router', 'w_gate', 'b_gate', 'w_up', 'b_up', 'w_down', 'b_down',
        'final_norm_g']


def kernel(**inputs):
    import concourse.bacc as bacc
    from concourse.bass_utils import run_bass_kernel_spmd

    nc = bacc.Bacc("TRN2", target_bir_lowering=False, num_devices=1)
    arrays, A = {}, {}
    freq = np.float32(10000.0) ** (-np.arange(64, dtype=np.float32) / np.float32(64))
    inputs["inv_freq"] = np.concatenate([freq, freq]).reshape(128, 1).astype(np.float32)
    for name in _INS + ["inv_freq"]:
        a = np.ascontiguousarray(inputs[name])
        arrays[f"in_{name}"] = a
        A[name] = nc.dram_tensor(f"in_{name}", a.shape, mybir.dt.from_np(a.dtype), kind="ExternalInput").ap()
    out = nc.dram_tensor("out_0", (1, T, D), F32, kind="ExternalOutput").ap()
    _program(nc, A, out)
    r = run_bass_kernel_spmd(nc, [arrays], core_ids=[0])
    return r.results[0]["out_0"]
```

```python
from contextlib import ExitStack

import numpy as np

import concourse.bass as bass
from concourse import mybir

F32 = mybir.dt.float32
F16 = mybir.dt.float16
I32 = mybir.dt.int32
U32 = mybir.dt.uint32
ALU = mybir.AluOpType
ACT = mybir.ActivationFunctionType
AX = mybir.AxisListType.X

P = 128
T = 256
TT = T // P
D = 1024
C = D // P
M = 256
EPS = 1e-5
DK = 64
GH = 4
DH = 128
NG = 3
NH = 4
SUB = 32
NSUB = P // SUB
E = 32
TOPK = 4
SLOTS = 64
EG = 4
GROUPS = E // EG
ROUNDS = T // SLOTS
LIMIT = 7.0
ALPHA = 1.702
NEG = -1.0e30
GLA_SCALE = DK ** -0.5
ATT_SCALE = DH ** -0.5
TWO_PI_HI = 6.28125
TWO_PI_LO = 2 * np.pi - TWO_PI_HI
MAGIC = 12582912.0

UNIT = 4096
NSLOT = 8
EARLY = 3
BANKS = 8

HALVES = ["q_g", "k_g", "v_g0", "v_g1", "r_g0", "r_g1"]
HALVES += [f"{k}{g}{a}" for k in ("q_d", "k_d", "v_d") for g in range(NG) for a in range(2)]
HALVES += [f"eg{q}" for q in range(8)] + ["xk0", "xk1", "gla0", "dil0", "gla1", "dil1"]
HALVES += [f"mix{q}" for q in range(4)] + ["xv0", "xv1", "xq0", "xq1", "xo0", "xo1"]
HALF = 2048
WS = 64.0

FILLS = ["vec"] + [f"x_T{i}" for i in range(4)] + ["alr", "q_g", "k_g", "v_g0", "v_g1", "r_g0", "r_g1", "lg"]
FILLS += [f"q_d{g}{a}" for g in range(NG) for a in range(2)] + ["bias", "cum"]
FILLS += [f"k_d{g}{a}" for g in range(NG) for a in range(2)] + ["v_d00", "v_d01"]
FILLS += [f"gs{h}" for h in range(GH)]
FILLS += ["v_d10", "v_d11"] + [f"m_T{i}" for i in range(4)] + ["v_d20", "v_d21", "go0", "go1"]
for _h in range(NH):
    FILLS += [f"s{_h}0", f"s{_h}1a", f"s{_h}1b", f"eg{2 * _h}", f"eg{2 * _h + 1}"]
    if _h == 0:
        FILLS += ["gt0", "gt1"]
    else:
        FILLS += [f"pt{_h - 1}{g}" for g in range(NG)]
    if _h == 2:
        FILLS += ["pv0"]
FILLS += ["xk0", "xk1"] + [f"pt3{g}" for g in range(NG)] + ["pv1"]
for _i in range(2):
    FILLS += [f"bg{2 * _i}", f"bg{2 * _i + 1}", f"bd{2 * _i}", f"bd{2 * _i + 1}"]
FILLS += [f"mix{q}" for q in range(4)] + ["xv0"] + [f"c_T{i}" for i in range(4)] + ["xv1", "xq0", "xq1"]
FILLS += ["xs0", "xs1", "xt0", "xs2", "xt1", "xpv0", "xs3", "xt2", "xt3", "xpv1"]
FILLS += [f"xo{n}{t}" for n in range(2) for t in range(TT)]
FILLS += [f"f_T{i}" for i in range(4)] + ["rt", "pos", "gT"]
assert len(set(FILLS)) == len(FILLS)
LAST_FILL = {k: k for k in HALVES if k in FILLS}
LAST_FILL.update({"gla0": "bg1", "dil0": "bd1", "gla1": "bg3", "dil1": "bd3", "xo0": "xo01", "xo1": "xo11"})
_N = FILLS.index("f_T0")
BANK = {f: i % BANKS if i < _N else (i - _N) % 4 for i, f in enumerate(FILLS)}
TURN = {f: sum(BANK[e] == BANK[f] for e in FILLS[:i]) for i, f in enumerate(FILLS)}
USES = [sum(BANK[f] == b for f in FILLS) for b in range(BANKS)]


def _program(nc, A, out):
    ctx = ExitStack()
    with ctx:
        def sb(name, shape, dt=F32):
            return ctx.enter_context(nc.sbuf_tensor(name, shape, dt))

        def sem(name):
            return ctx.enter_context(nc.semaphore(name))

        ring = sb("ring", [P, NSLOT * UNIT])
        h = sb("h", [P, TT, D])
        reg_a = sb("reg_a", [P, C * T])
        reg_m = sb("reg_m", [P, C * T])
        reg_t = sb("reg_t", [P, C * T])
        reg_g = sb("reg_g", [P, 2 * C * T])
        reg_o = sb("reg_o", [P, 8 * T])
        reg_l = sb("reg_l", [P, 3072])
        ident = sb("ident", [P, P])
        tri16 = sb("tri16", [P, P])
        tri_s = sb("tri_s", [P, P])
        ones = sb("ones", [P, P])
        masks = sb("masks", [P, 6, P])
        vT = sb("vT", [P, 44])
        iota_s = sb("iota_s", [P, SLOTS])
        iota_e = sb("iota_e", [P, E])
        bT = sb("bT", [P, 2, C, E])
        g3 = sb("g3", [P, C])
        w_rt = sb("w_rt", [P, C, E])
        b_rt = sb("b_rt", [1, E])
        route = sb("route", [P, 3, TT, E])
        st = sb("st", [P, 64])
        ssq = sb("ssq", [P, 4, TT, 4])
        neg_half = sb("neg_half", [P, 4])
        over = sb("over", [P, 1], I32)

        place, gate, mask = route[:, 0], route[:, 1], route[:, 2]

        def region(r, at, *shape):
            n = int(np.prod(shape))
            v = r[:, at:at + n]
            if len(shape) == 1:
                return v
            names = "abcdef"[:len(shape)]
            return v.rearrange(f"p ({' '.join(names)}) -> p {' '.join(names)}",
                               **{k: s for k, s in zip(names[1:], shape[1:])})

        slot = [region(ring, s * UNIT, UNIT) for s in range(NSLOT)]
        at = EARLY * UNIT
        qr = region(ring, at, NG * 2, 2, T)
        kr = region(ring, at + 3072, NG * 2, 2, T)
        vd = region(ring, at + 6144, TT, NG * NH * DH)
        brows = region(ring, at + 6144, 2, D)
        kS = region(ring, at + 9216, 2, TT, NSUB, P)
        S = region(ring, at + 11264, 2, 9 * P)
        rot = region(ring, at + 11264, 2, 2, T)
        PT = region(ring, at + 13568, 2, NG, 3 * P)
        B = region(ring, at + 13568, 2, T)
        scT = region(ring, at + 15872, GH, 3 * P)
        og = region(ring, at + 17408, TT, GH * P)
        sr = region(ring, at + 18432, TT, GH * P)
        la = region(ring, at + 19456, TT, T)
        cs = region(ring, at + 19968, 2, T)

        raw = [region(ring, i * HALF, HALF) for i in range(EARLY)]
        cut = [ring[:, (EARLY + i) * HALF:(EARLY + i + 1) * HALF].bitcast(F16)
               .rearrange("p (k n) -> p k n", k=2) for i in range(EARLY)]

        def parts(r, at, chunks):
            return r[:, at:at + chunks * T].bitcast(F16).rearrange("p (k c t) -> p k c t", k=2, c=chunks)

        aT = parts(reg_a, 0, C)
        fT = region(reg_a, 0, C, T)
        xg = region(reg_a, 0, C, T)
        memx = region(reg_m, 0, TT, D)
        mergedT = parts(reg_m, 0, C)
        f = region(reg_m, 0, TT, C, P)
        out_sb = region(reg_m, 0, TT, D)
        memT = parts(reg_t, 0, C)
        hs = region(reg_t, 0, C, P)
        y = region(reg_t, 1024, 512)
        sel = region(reg_t, 1536, TT, EG * SLOTS)
        xn = region(reg_g, 0, TT, D)
        alr = region(reg_g, 2048, T)
        w2 = region(reg_g, 2304, T)
        w_alr = region(reg_g, 2560, C, 16)
        w_alr16 = reg_g[:, 3968:4096].bitcast(F16).rearrange("p (k c n) -> p k c n", k=2, c=C)
        trig = region(reg_g, 2688, 3, T)
        lnz = region(reg_g, 3456, TT, T)
        gates = region(reg_g, 0, 2 * C, T)
        xP = region(reg_g, 2048, 2, TT, M)
        xPT = region(reg_g, 3072, 2, 2, T)
        oneh = region(reg_g, 0, 2 * TT * TOPK, E)
        selG = region(reg_g, 0, TT, EG, 2, SLOTS)
        selT = region(reg_g, 1024, EG, TT, P)
        g_sb = region(reg_g, 2048, C, SLOTS)
        sg_sb = region(reg_g, 2560, C, SLOTS)
        l_sb = region(reg_g, 3072, C, SLOTS)
        actT = region(reg_g, 3584, C, SLOTS)
        ogT = parts(reg_o, 0, 4)
        odT = parts(reg_o, 1024, 4)
        oxT = parts(reg_o, 0, 4)
        gateT = region(reg_o, 1024, T)
        qg = region(reg_l, 0, 2, T)
        kg = region(reg_l, 512, 2, T)
        vg = region(reg_l, 1024, TT, GH * P)
        qS = region(reg_l, 2048, 2, T)
        qX = region(reg_l, 2560, 2, P)
        kX = region(reg_l, 2816, 2, P)
        xq = region(reg_l, 0, NH, T)
        xk = region(reg_l, 1024, NH, M)
        xv = region(reg_l, 2048, TT, NH * DH)
        b_dn = region(reg_l, 0, D)
        gfin = region(reg_l, 1024, D)
        rows = region(reg_l, 0, P)
        pos_i = region(reg_l, 512, T).bitcast(I32)
        invf = region(reg_l, 768, 1)
        diff_i = region(reg_l, 1024, P).bitcast(I32)
        mod_i = region(reg_l, 1152, P).bitcast(I32)
        mod_f = region(reg_l, 1280, P)
        idx_u = region(reg_l, 2048, TT, 8).bitcast(U32)
        idx_f = region(reg_l, 2064, TT, TOPK)
        top = region(reg_l, 2080, TT, 8)
        g4 = region(reg_l, 2096, TT, TOPK)
        logit = region(reg_l, 2112, TT, E)

        pt = [ctx.enter_context(nc.psum_tensor(f"bank{b}", [P, 512], F32)) for b in range(BANKS)]

        ld_x = [sem(f"ld_x{t}") for t in range(TT)]
        ld_mem, ld_small, ld_late, ld_brows, consts = (sem(n) for n in
            ("ld_mem", "ld_small", "ld_late", "ld_brows", "consts"))
        half_ld = [sem(f"half_ld{s}") for s in range(EARLY)]
        w_high, w_low = sem("w_high"), sem("w_low")
        x_high = sem("x_high")
        alr_cut = sem("alr_cut")
        late_ld = [sem(f"late_ld{s}") for s in range(NSLOT)]
        gu_half, dn_half = sem("gu_half"), sem("dn_half")
        full = [sem(f"full{b}") for b in range(BANKS)]
        free = [sem(f"free{b}") for b in range(BANKS)]
        dve_chain, act_chain, pool_chain = sem("dve_chain"), sem("act_chain"), sem("pool_chain")
        norm_ss, norm_xn = sem("norm_ss"), sem("norm_xn")
        trig_in, trig_out = sem("trig_in"), sem("trig_out")
        mod_ready, masks_ready = sem("mod_ready"), sem("masks_ready")
        th_r, ln_ready, anchors, gla_exp, gla_qk, go_ss = (sem(n) for n in
            ("th_r", "ln_ready", "anchors", "gla_exp", "gla_qk", "go_ss"))
        s_ready, s_exp, s_prob, merged_sum, merged_ready = (sem(n) for n in
            ("s_ready", "s_exp", "s_prob", "merged_sum", "merged_ready"))
        xs_max, xs_exp, xs_prob = sem("xs_max"), sem("xs_exp"), sem("xs_prob")
        top_ready, top_exp, gate_ready, over_ready = (sem(n) for n in
            ("top_ready", "top_exp", "gate_ready", "over_ready"))
        sel_ready, gathered, xg_act, xg_dve, selT_full, selT_act, selT_dve = (sem(n) for n in
            ("sel_ready", "gathered", "xg_act", "xg_dve", "selT_full", "selT_act", "selT_dve"))
        h_full, hs_act, hs_dve, T_full, g_ready, sg_ready, act_ready, y_full, y_ready, moe_chain = (sem(n) for n in
            ("h_full", "hs_act", "hs_dve", "T_full", "g_ready", "sg_ready", "act_ready", "y_full", "y_ready",
             "moe_chain"))
        root_asked, root_done = sem("root_asked"), sem("root_done")
        lin_chain, round_chain = sem("lin_chain"), sem("round_chain")
        acc_full, fin_ss, fin_ready, stored = sem("acc_full"), sem("fin_ss"), sem("fin_ready"), sem("stored")

        def take(eng, name):
            eng.wait_ge(full[BANK[name]], TURN[name] + 1)
            return pt[BANK[name]]

        def emptied(eng, name):
            eng.wait_ge(free[BANK[name]], TURN[name] + 1)

        def chain(eng, s):
            count = [0]

            def link(ins):
                count[0] += 1
                ins.then_inc(s, 1)
                eng.wait_ge(s, count[0])
            return link

        def bc(ap, n):
            return ap.unsqueeze(2).to_broadcast([ap.shape[0], ap.shape[1], n])

        def mid(ap, n):
            return ap.unsqueeze(1).to_broadcast([ap.shape[0], n, ap.shape[1]])

        OFF_QG, OFF_VG, OFF_RG, OFF_AL, OFF_QD = 0, 512, 1024, 1536, 1552
        w_in = A["w_in"][0].rearrange("(c p) n -> p c n", p=P)
        w_gate_br = A["w_branch_gate"][0].rearrange("(c p) n -> p c n", p=P)
        w_xkv = A["w_xkv"][0].rearrange("(c p) n -> p c n", p=P)
        dense = {k: A[n][0].rearrange("(c p) n -> p c n", p=P) for k, n in
                 (("gla", "w_branch_gla"), ("dil", "w_branch_dil"), ("mix", "w_mix_out"), ("xq", "w_xq"),
                  ("xo", "w_xo"))}
        SRC = {"q_g": w_in[:, :, OFF_QG:OFF_QG + 256], "k_g": w_in[:, :, OFF_QG + 256:OFF_VG]}
        for a in range(2):
            SRC[f"v_g{a}"] = w_in[:, :, OFF_VG + a * 256:OFF_VG + (a + 1) * 256]
            SRC[f"r_g{a}"] = w_in[:, :, OFF_RG + a * 256:OFF_RG + (a + 1) * 256]
            for g in range(NG):
                for i, k in enumerate(("q_d", "k_d", "v_d")):
                    o = OFF_QD + (i * NG + g) * 512 + a * 256
                    SRC[f"{k}{g}{a}"] = w_in[:, :, o:o + 256]
            SRC[f"xk{a}"] = w_xkv[:, :, a * 256:(a + 1) * 256]
            SRC[f"xv{a}"] = w_xkv[:, :, 512 + a * 256:512 + (a + 1) * 256]
            for k, n in (("gla", 512), ("dil", 512), ("xo", 512), ("xq", 256)):
                SRC[f"{k}{a}"] = dense[k][:, :, a * n:(a + 1) * n]
        for q in range(4):
            SRC[f"mix{q}"] = dense["mix"][:, :, q * 256:(q + 1) * 256]
        for q in range(8):
            SRC[f"eg{q}"] = w_gate_br[:, :, q * 256:(q + 1) * 256]

        block = ctx.enter_context(nc.Block())

        def expert_groups(eng, body):
            with eng.Fori(0, GROUPS) as n:
                body(n, n)
            eng.wait_ge(over_ready, 1)
            more = eng.value_load(over[0:1, 0:1], min_val=0, max_val=1)
            with eng.If(more > 0):
                with eng.Fori(1, ROUNDS) as r:
                    if eng.engine == nc.vector.engine:
                        next_round(eng, r)
                    with eng.Fori(0, GROUPS) as n:
                        body(n, r * GROUPS + n)
                eng.nop()

        @block.sync
        def _(sp):
            xt_src = A["x"][0].rearrange("(t p) d -> p t d", p=P)
            for t in range(TT):
                sp.dma_start(h[:, t, :], xt_src[:, t, :]).then_inc(ld_x[t], 16)
            for u, name in enumerate(HALVES):
                if u >= EARLY:
                    sp.wait_ge(w_low, u - EARLY + 1)
                sp.dma_start(raw[u % EARLY].rearrange("p (c n) -> p c n", n=SRC[name].shape[2]), SRC[name])\
                    .then_inc(half_ld[u % EARLY], 16)

            mats = [A[k][0].rearrange("e (p c) n -> e p (c n)", c=C) for k in ("w_gate", "w_up", "w_down")]
            ORDER = ((0, 0), (1, 0), (0, 1), (1, 1), (2, 0), (2, 1))

            def load(v, e, m, half):
                s = v % NSLOT
                src = mats[m][bass.ds(e, 1), :, half * UNIT:(half + 1) * UNIT]
                sp.dma_start(slot[s], src.rearrange("e p n -> p (e n)")).then_inc(late_ld[s], 16)

            per = 6 * EG
            LEFT = (gu_half, gu_half, h_full, h_full, dn_half, y_full)

            def slot_left(v, e0):
                sp.wait_ge(LEFT[(v - NSLOT) % 6], e0 + ((v - NSLOT) // 6 + 1))

            for v in range(per):
                if v == 0:
                    sp.wait_ge(w_low, len(HALVES))
                elif v == 1:
                    take(sp, "xo11")
                elif v == EARLY:
                    take(sp, "pv1")
                elif v >= NSLOT:
                    slot_left(v, 0)
                load(v, v // 6, *ORDER[v % 6])

            def body(n, k):
                for v in range(per):
                    slot_left(v, k * EG)
                    load(v, n * EG + v // 6, *ORDER[v % 6])

            with sp.Fori(1, GROUPS) as n:
                body(n, n)
            sp.wait_ge(over_ready, 1)
            more = sp.value_load(over[0:1, 0:1], min_val=0, max_val=1)
            with sp.If(more > 0):
                with sp.Fori(1, ROUNDS) as r:
                    with sp.Fori(0, GROUPS) as n:
                        body(n, r * GROUPS + n)
                sp.nop()
            for t in range(TT):
                sp.wait_ge(fin_ready, t + 1)
                sp.dma_start(out[0, t * P:(t + 1) * P, :], out_sb[:, t, :]).then_inc(stored, 16)
            sp.wait_ge(stored, 16 * TT)

        SMALL = 16 * 9

        @block.gpsimd
        def _(pool):
            link = chain(pool, pool_chain)
            roots = [0]

            def root(a, b):
                roots[0] += 1
                pool.wait_ge(root_asked, roots[0])
                pool.tensor_tensor(st[:, a:b], st[:, a:b], neg_half[:, 0:b - a], ALU.pow).then_inc(root_done, 1)

            for name, at_row, n in (("norm1_g", 0, 8), ("mem_norm_g", 8, 8), ("norm2_g", 16, 8),
                                    ("gla_norm_g", 24, 4), ("b_branch_gate", 28, 16)):
                pool.dma_start(rows[at_row:at_row + n, :],
                               A[name][0].rearrange("(c p) -> c p", p=P)).then_inc(ld_small, 16)
            pool.dma_start(w2[0:16, :], A["w_gla_a2"][0]).then_inc(ld_small, 16)
            pool.dma_start(w2[16:17, :], A["b_gla_a2"]).then_inc(ld_small, 16)
            pool.dma_start(invf, A["inv_freq"]).then_inc(ld_small, 16)
            pool.dma_start(pos_i, A["positions"].to_broadcast([P, T])).then_inc(ld_small, 16)
            link(pool.memset(ident[:], 0.0))
            pool.affine_select(out=ident[:], in_=ident[:], compare_op=ALU.not_equal, fill=1.0, base=0,
                               pattern=[[-1, P]], channel_multiplier=1).then_inc(consts, 1)
            link(pool.memset(neg_half[:], -0.5))
            root(0, 2)
            link(pool.memset(tri16[:], 1.0 / 16))
            pool.affine_select(out=tri16[:], in_=tri16[:], compare_op=ALU.is_ge, fill=0.0, base=0,
                               pattern=[[1, P]], channel_multiplier=-1).then_inc(consts, 1)
            link(pool.memset(tri_s[:], 1.0))
            pool.affine_select(out=tri_s[:], in_=tri_s[:], compare_op=ALU.is_gt, fill=0.0, base=0,
                               pattern=[[1, P]], channel_multiplier=-1).then_inc(consts, 1)
            pool.memset(ones[:], 1.0).then_inc(consts, 1)
            pool.memset(alr[0:32, :], 1.0).then_inc(consts, 1)
            pool.memset(kS, 0.0).then_inc(consts, 1)
            pool.iota(iota_s[:], pattern=[[1, SLOTS]], base=0, channel_multiplier=0,
                      allow_small_or_imprecise_dtypes=True).then_inc(consts, 1)
            pool.iota(iota_e[:], pattern=[[1, E]], base=0, channel_multiplier=0,
                      allow_small_or_imprecise_dtypes=True).then_inc(consts, 1)
            pool.iota(diff_i, pattern=[[1, P]], base=T, channel_multiplier=-1).then_inc(consts, 1)
            pool.dma_start(w_alr, w_in[:, :, OFF_AL:OFF_AL + 16]).then_inc(ld_late, 16)
            pool.dma_start(w_rt[:], A["w_router"][0].rearrange("(p c) e -> p c e", c=C)).then_inc(ld_late, 16)
            pool.dma_start(b_rt[:], A["b_router"]).then_inc(ld_late, 16)
            pool.dma_start(g3[:], A["norm3_g"][0].rearrange("(p c) -> p c", c=C)).then_inc(ld_late, 16)
            link(pool.memset(masks[:, 0:2, :], 0.0))
            pool.affine_select(out=masks[:, 0, :], in_=masks[:, 0, :], compare_op=ALU.is_ge, fill=NEG, base=0,
                               pattern=[[1, P]], channel_multiplier=-1).then_inc(masks_ready, 1)
            pool.wait_ge(mod_ready, 1)
            for m in (1, 3, 5):
                pool.affine_select(out=masks[:, m, :], in_=masks[:, m, :], compare_op=ALU.is_ge, fill=NEG,
                                   base=0, pattern=[[-1, P]], channel_multiplier=1).then_inc(masks_ready, 1)
            root(2, 4)
            root(8, 12)
            root(12, 16)
            root(4, 6)
            take(pool, "xo11")
            pool.dma_start(b_dn[0:E, :], A["b_down"][0]).then_inc(ld_late, 16)
            pool.dma_start(gfin, A["final_norm_g"].rearrange("(a n) -> a n", a=1).to_broadcast([P, D]))\
                .then_inc(ld_late, 16)
            root(6, 8)
            pool.wait_ge(ld_late, 16 * 6)
            root(56, 57)
            root(58, 59)

        @block.scalar
        def _(act):
            link = chain(act, act_chain)
            for i, k in enumerate(("b_gate", "b_up")):
                act.dma_start(brows[0:E, i, :], A[k][0]).then_inc(ld_brows, 16)
            act.dma_start(memx, A["mem"][0].rearrange("(t p) d -> p t d", p=P)).then_inc(ld_mem, 16)

            def copy(dst, src):
                return act.activation(dst, src, ACT.Copy)

            def unscaled(dst, src):
                return act.activation(dst, src, ACT.Copy, scale=1 / WS)

            def free_bank(name):
                return free[BANK[name]]

            halves = [0]

            def cut_ahead(name):
                while halves[0] < min(HALVES.index(name) + 3, len(HALVES)):
                    u = halves[0]
                    halves[0] += 1
                    act.wait_ge(half_ld[u % EARLY], 16 * (u // EARLY + 1))
                    if u >= EARLY:
                        take(act, LAST_FILL[HALVES[u - EARLY]])
                    act.activation(cut[u % EARLY][:, 0, :], raw[u % EARLY], ACT.Copy, scale=WS).then_inc(w_high, 1)

            def high(dst, src, scale):
                act.activation(dst, src, ACT.Copy, scale=scale).then_inc(x_high, 1)

            def high_T(prefix, q, dst, gain):
                b = take(act, f"{prefix}{q}")
                for i in range(2):
                    high(dst[:, 0, 2 * q + i, :], b[:, i * T:(i + 1) * T], gain[:, 2 * q + i:2 * q + i + 1])

            def squares(norm, src, junk, t, part, n):
                act.activation(junk[:, t, part * n:(part + 1) * n], src[:, t, part * n:(part + 1) * n], ACT.Square,
                               accum_out=ssq[:, norm, t, part:part + 1]).then_inc(norm_ss, 1)

            for t in range(TT):
                act.wait_ge(ld_x[t], 16)
                squares(0, h, xn, t, 0, D)
            cut_ahead("q_g")
            emptied(act, "vec")
            for q in range(4):
                high_T("x_T", q, aT, vT[:, 0:8])
            act.wait_ge(ld_late, 64)
            act.activation(w_alr16[:, 0], w_alr, ACT.Copy, scale=WS).then_inc(alr_cut, 1)
            for i in range(2):
                act.wait_ge(trig_in, i + 1)
                act.activation(cs[:, i, :], trig[:, 2, :], ACT.Sin).then_inc(trig_out, 1)
            b = take(act, "alr")
            act.wait_ge(consts, 9)
            act.activation(alr[0:16, :], b[0:16, 0:T], ACT.Copy, scale=1 / WS).then_inc(free_bank("alr"), 1)
            for name, dst in (("q_g", qg), ("k_g", kg)):
                cut_ahead(name)
                b = take(act, name)
                if name == "q_g":
                    act.wait_ge(trig_in, 2)
                unscaled(dst.rearrange("p a b -> p (a b)"), b[:]).then_inc(free_bank(name), 1)
            act.wait_ge(masks_ready, 1)
            act.wait_ge(mod_ready, 1)
            def two_tiles(b):
                return b[:].rearrange("p (t n) -> p t n", t=TT)

            for a in range(2):
                cut_ahead(f"v_g{a}")
                b = take(act, f"v_g{a}")
                unscaled(vg[:, :, a * 256:(a + 1) * 256], two_tiles(b)).then_inc(free_bank(f"v_g{a}"), 1)
            for a in range(2):
                cut_ahead(f"r_g{a}")
                b = take(act, f"r_g{a}")
                act.activation(sr[:, :, a * 256:(a + 1) * 256], two_tiles(b), ACT.Tanh, scale=0.5 / WS)\
                    .then_inc(th_r, 1)
            b = take(act, "lg")
            link(act.activation(lnz.rearrange("p a b -> p (a b)"), b[:], ACT.Abs))
            link(act.activation(lnz, lnz, ACT.Exp, scale=-1.0))
            act.activation(lnz, lnz, ACT.Ln, bias=1.0).then_inc(ln_ready, 1)
            for g in range(NG):
                for a in range(2):
                    cut_ahead(f"q_d{g}{a}")
            b = take(act, "cum")
            copy(B.rearrange("p a b -> p (a b)"), b[:]).then_inc(free_bank("cum"), 1)
            act.wait_ge(anchors, 1)
            for fc in range(2):
                for t in range(TT):
                    for i in range(NSUB):
                        a0 = t * P + i * SUB
                        act.activation(qS[:, fc, a0:a0 + SUB], B[:, fc, a0:a0 + SUB], ACT.Exp,
                                       bias=st[:, 16 + fc * 8 + t * 4 + i:17 + fc * 8 + t * 4 + i])
                        act.activation(kS[:, fc, t, i, 0:(i + 1) * SUB], B[:, fc, t * P:t * P + (i + 1) * SUB],
                                       ACT.Exp, scale=-1.0, bias=B[:, fc, a0 + SUB // 2:a0 + SUB // 2 + 1])
                act.activation(kX[:, fc, :], B[:, fc, 0:P], ACT.Exp, scale=-1.0, bias=B[:, fc, P - 1:P])
            act.activation(qX, B[:, :, P:T], ACT.Exp).then_inc(gla_exp, 1)
            act.wait_ge(ld_mem, 16)
            for t in range(TT):
                squares(1, memx, xn, t, 0, D)
            for g in range(NG):
                for a in range(2):
                    cut_ahead(f"k_d{g}{a}")
            for g in range(NG):
                for a in range(2):
                    cut_ahead(f"v_d{g}{a}")
                    b = take(act, f"v_d{g}{a}")
                    o = g * 512 + a * 256
                    unscaled(vd[:, :, o:o + 256], two_tiles(b)).then_inc(free_bank(f"v_d{g}{a}"), 1)
                if g == 1:
                    for q in range(4):
                        high_T("m_T", q, memT, vT[:, 8:16])
            for t in range(TT):
                b = take(act, f"go{t}")
                for hd in range(GH):
                    act.activation(og[:, t, hd * P:(hd + 1) * P], b[:, hd * P:(hd + 1) * P], ACT.Square,
                                   accum_out=st[:, 8 + t * 4 + hd:9 + t * 4 + hd]).then_inc(go_ss, 1)

            def softmax_exp(hd):
                act.wait_ge(s_ready, hd + 1)
                for t, (c0, c1) in enumerate(((0, 3 * P), (3 * P, 9 * P))):
                    act.activation(S[:, hd % 2, c0:c1], S[:, hd % 2, c0:c1], ACT.Exp, scale=ATT_SCALE,
                                   bias=st[:, 36 + 2 * (hd % 2) + t:37 + 2 * (hd % 2) + t],
                                   accum_out=st[:, 40 + 2 * (hd % 2) + t:41 + 2 * (hd % 2) + t]).then_inc(s_exp, 1)

            def probs_T(hd):
                for g in range(2):
                    b = take(act, f"pt{hd}{g}")
                    copy(PT[:, hd % 2, g, :], b[:, 0:3 * P]).then_inc(free_bank(f"pt{hd}{g}"), 1)

            def branch_gates(q):
                cut_ahead(f"eg{q}")
                b = take(act, f"eg{q}")
                for i in range(2):
                    c = 2 * q + i
                    ins = act.activation(gates[:, c, :], b[:, i * T:(i + 1) * T], ACT.Tanh, scale=0.5 / WS,
                                         bias=vT[:, 28 + c:29 + c])
                ins.then_inc(free_bank(f"eg{q}"), 1)

            def out_T(a):
                b = take(act, f"pv{a}")
                high(odT[:, 0, 2 * a:2 * a + 2, :].rearrange("p a b -> p (a b)"), b[:], 1.0)

            for hd in range(NH):
                softmax_exp(hd)
                branch_gates(2 * hd)
                branch_gates(2 * hd + 1)
                if hd == 0:
                    for q in range(2):
                        high_T("gt", q, ogT, vT[:, 24:28])
                else:
                    probs_T(hd - 1)
                if hd == 2:
                    out_T(0)
            for a in range(2):
                cut_ahead(f"xk{a}")
                b = take(act, f"xk{a}")
                unscaled(xk[:, 2 * a:2 * a + 2, :].rearrange("p a b -> p (a b)"), b[:])\
                    .then_inc(free_bank(f"xk{a}"), 1)
            probs_T(3)
            out_T(1)
            for q in range(4):
                if q % 2 == 0:
                    cut_ahead(f"dil{q // 2}")
                act.wait_ge(merged_sum, q + 1)
                high(mergedT[:, 0, 2 * q:2 * q + 2, :].rearrange("p a b -> p (a b)"),
                     gates[:, 2 * q:2 * q + 2, :].rearrange("p a b -> p (a b)"), 0.5 / WS)
            for q in range(4):
                cut_ahead(f"mix{q}")
                emptied(act, f"mix{q}")
                for t in range(TT):
                    squares(2, h, xn, t, q, 256)

            def x_values(a):
                cut_ahead(f"xv{a}")
                b = take(act, f"xv{a}")
                unscaled(xv[:, :, a * 256:(a + 1) * 256], two_tiles(b)).then_inc(free_bank(f"xv{a}"), 1)

            x_values(0)
            for q in range(4):
                high_T("c_T", q, aT, vT[:, 16:24])
            x_values(1)
            for a in range(2):
                cut_ahead(f"xq{a}")
                b = take(act, f"xq{a}")
                unscaled(xq[:, 2 * a:2 * a + 2, :].rearrange("p a b -> p (a b)"), b[:])\
                    .then_inc(free_bank(f"xq{a}"), 1)

            def x_exp(hd):
                act.wait_ge(xs_max, hd + 1)
                b = pt[BANK[f"xs{hd}"]]
                for t in range(TT):
                    act.activation(xP[:, hd % 2, t, :], b[:, t * M:(t + 1) * M], ACT.Exp, scale=ATT_SCALE,
                                   bias=st[:, 44 + 2 * (hd % 2) + t:45 + 2 * (hd % 2) + t],
                                   accum_out=st[:, 48 + 2 * (hd % 2) + t:49 + 2 * (hd % 2) + t])\
                        .then_inc(xs_exp if t == 0 else free_bank(f"xs{hd}"), 1)

            def x_probs_T(hd):
                b = take(act, f"xt{hd}")
                copy(xPT[:, hd % 2].rearrange("p a b -> p (a b)"), b[:]).then_inc(free_bank(f"xt{hd}"), 1)

            def x_out_T(a):
                b = take(act, f"xpv{a}")
                high(oxT[:, 0, 2 * a:2 * a + 2, :].rearrange("p a b -> p (a b)"), b[:], 1.0)

            x_exp(0)
            x_exp(1)
            x_probs_T(0)
            x_exp(2)
            x_probs_T(1)
            x_out_T(0)
            x_exp(3)
            x_probs_T(2)
            x_probs_T(3)
            x_out_T(1)
            for n in range(2):
                for t in range(TT):
                    emptied(act, f"xo{n}{t}")
                    squares(3, h, xn, t, n, 512)
            act.wait_ge(top_ready, 1)
            for t in range(TT):
                act.activation(g4[:, t, :], top[:, t, 0:TOPK], ACT.Exp, bias=st[:, 52 + t:53 + t],
                               accum_out=st[:, 54 + t:55 + t]).then_inc(top_exp, 1)

            def body(n, k):
                for q in (0, 2):
                    act.wait_ge(gathered, 4 * k + (q + 1))
                    for i in range(2):
                        c = 2 * q + i
                        ins = act.activation(xg[:, c, :], pt[q][:, i * T:(i + 1) * T], ACT.Copy,
                                             scale=g3[:, c:c + 1])
                    ins.then_inc(xg_act, 1)
                act.wait_ge(selT_full, 2 * k + 1)
                copy(selT[:, 0:2].rearrange("p e t s -> p (e t s)"), pt[0][:]).then_inc(selT_act, 1)
                for j in range(EG):
                    act.wait_ge(h_full, k * EG + (j + 1))
                    copy(hs[:, :, 0:64], pt[0][:].rearrange("p (q c) -> p c q", c=C)).then_inc(hs_act, 1)
                    for i in range(2):
                        act.wait_ge(g_ready, k * 2 * EG + (2 * j + i + 1))
                        act.activation(sg_sb[:, 4 * i:4 * i + 4, :], g_sb[:, 4 * i:4 * i + 4, :], ACT.Sigmoid,
                                       scale=ALPHA).then_inc(sg_ready, 1)
                    act.wait_ge(y_full, k * EG + (j + 1))
                    copy(y, pt[2][:]).then_inc(y_ready, 1)

            expert_groups(act, body)

            for t in range(TT):
                act.wait_ge(acc_full, 2 * t + 2)
                for i in range(2):
                    act.activation(out_sb[:, t, i * 512:(i + 1) * 512], pt[4 + 2 * t + i][:], ACT.Square,
                                   accum_out=st[:, 56 + 2 * t + i:57 + 2 * t + i]).then_inc(fin_ss, 1)

        LINKS = 2 + 3 * 2 * EG

        def next_round(dve, r):
            dve.wait_ge(round_chain, r)
            dve.tensor_scalar(place, place, -float(SLOTS), None, ALU.add).then_inc(round_chain, 1)
            dve.wait_ge(round_chain, r + 1)
            dve.memset(st[:, 62:63], 0.0)

        @block.vector
        def _(dve):
            link = chain(dve, dve_chain)

            roots = [0]

            def rsqrt_mean(dst, src, n):
                dve.tensor_scalar(dst, src, 1.0 / n, EPS, ALU.mult, ALU.add).then_inc(root_asked, 1)
                roots[0] += 1
                dve.wait_ge(root_done, roots[0])

            def free_bank(name):
                return free[BANK[name]]

            squared, halves, highs = [0], [0], [0]

            def cut_ahead(name):
                while halves[0] < min(HALVES.index(name) + 3, len(HALVES)):
                    u = halves[0]
                    halves[0] += 1
                    dve.wait_ge(w_high, u + 1)
                    dve.scalar_tensor_tensor(cut[u % EARLY][:, 1, :], raw[u % EARLY], WS, cut[u % EARLY][:, 0, :],
                                             ALU.mult, ALU.subtract).then_inc(w_low, 1)

            def low(dst, src, scale, hi):
                highs[0] += 1
                dve.wait_ge(x_high, highs[0])
                return dve.scalar_tensor_tensor(dst, src, scale, hi, ALU.mult, ALU.subtract)

            def low_T(prefix, q, dst, gain):
                b = take(dve, f"{prefix}{q}")
                highs[0] += 1
                for i in range(2):
                    c = 2 * q + i
                    highs[0] -= i
                    ins = low(dst[:, 1, c, :], b[:, i * T:(i + 1) * T], gain[:, c:c + 1], dst[:, 0, c, :])
                ins.then_inc(free_bank(f"{prefix}{q}"), 1)

            def normed(norm, nparts, src, dst, at):
                squared[0] += TT * nparts
                dve.wait_ge(norm_ss, squared[0])
                if nparts == 1:
                    rsqrt_mean(st[:, at:at + 2], ssq[:, norm, :, 0], D)
                else:
                    link(dve.reduce_sum(st[:, at:at + 2], ssq[:, norm, :, 0:nparts], AX))
                    rsqrt_mean(st[:, at:at + 2], st[:, at:at + 2], D)
                for t in range(TT):
                    dve.tensor_scalar(dst(t), src(t), st[:, at + t:at + t + 1], None, ALU.mult)\
                        .then_inc(norm_xn, 1)

            normed(0, 1, lambda t: h[:, t, :], lambda t: xn[:, t, :], 0)
            b = take(dve, "vec")
            dve.tensor_copy(vT[:, 0:24], b[:, 0:24])
            dve.tensor_scalar(vT[:, 24:28], b[:, 24:28], 0.5 / WS, None, ALU.mult)
            dve.tensor_scalar(vT[:, 28:44], b[:, 28:44], 0.5, None, ALU.mult).then_inc(free_bank("vec"), 1)
            emptied(dve, "vec")
            cut_ahead("q_g")
            for q in range(4):
                low_T("x_T", q, aT, vT[:, 0:8])
            dve.wait_ge(alr_cut, 1)
            dve.scalar_tensor_tensor(w_alr16[:, 1], w_alr, WS, w_alr16[:, 0], ALU.mult, ALU.subtract)\
                .then_inc(alr_cut, 1)
            dve.wait_ge(ld_small, SMALL)
            link(dve.tensor_copy(trig[:, 1, :], pos_i))
            link(dve.tensor_scalar(trig[:, 0, :], trig[:, 1, :], invf, None, ALU.mult))
            for i, phase in enumerate((np.pi / 2, 0.0)):
                link(dve.tensor_scalar(trig[:, 1, :], trig[:, 0, :], float(0.5 / np.pi), float(phase * 0.5 / np.pi),
                                       ALU.mult, ALU.add))
                link(dve.tensor_scalar(trig[:, 1, :], trig[:, 1, :], MAGIC, None, ALU.add))
                link(dve.tensor_scalar(trig[:, 1, :], trig[:, 1, :], -MAGIC, None, ALU.add))
                if i:
                    dve.wait_ge(trig_out, 1)
                link(dve.scalar_tensor_tensor(trig[:, 2, :], trig[:, 1, :], -TWO_PI_HI, trig[:, 0, :],
                                              ALU.mult, ALU.add))
                link(dve.scalar_tensor_tensor(trig[:, 2, :], trig[:, 1, :], -float(TWO_PI_LO), trig[:, 2, :],
                                              ALU.mult, ALU.add))
                link(dve.tensor_scalar(trig[:, 2, :], trig[:, 2, :], float(phase), 3.1415925, ALU.add, ALU.min))
                dve.tensor_scalar(trig[:, 2, :], trig[:, 2, :], -3.1415925, None, ALU.max).then_inc(trig_in, 1)
            cut_ahead("k_g")
            dve.wait_ge(consts, 9)
            dve.wait_ge(masks_ready, 1)
            for m, d in ((2, 4), (4, 16)):
                link(dve.tensor_scalar(mod_i, diff_i, d - 1, None, ALU.bitwise_and))
                link(dve.tensor_copy(mod_f, mod_i))
                link(dve.tensor_scalar(mod_f, mod_f, 0.0, -NEG, ALU.is_equal, ALU.mult))
                link(dve.tensor_scalar(masks[:, m, :], mod_f, NEG, None, ALU.add))
                ins = dve.tensor_copy(masks[:, m + 1, :], masks[:, m, :])
            ins.then_inc(mod_ready, 1)
            for a in range(2):
                cut_ahead(f"v_g{a}")
            for a in range(2):
                cut_ahead(f"r_g{a}")
                b = take(dve, f"r_g{a}")
                dve.wait_ge(th_r, a + 1)
                v = sr[:, :, a * 256:(a + 1) * 256]
                dve.scalar_tensor_tensor(v, v, 1.0, b[:].rearrange("p (t n) -> p t n", t=TT), ALU.add, ALU.mult)\
                    .then_inc(free_bank(f"r_g{a}"), 1)
            b = take(dve, "lg")
            dve.wait_ge(ln_ready, 1)
            dve.scalar_tensor_tensor(la.rearrange("p a b -> p (a b)"), b[:], 0.0,
                                     lnz.rearrange("p a b -> p (a b)"), ALU.min, ALU.subtract)\
                .then_inc(free_bank("lg"), 1)

            def rotary(name, dst, before):
                if before:
                    emptied(dve, before)
                cut_ahead(name)
                b = take(dve, name)
                ps = b[:].rearrange("p (a b) -> p a b", a=2)
                dve.tensor_tensor(rot[:, 0], ps, mid(cs[:, 0, :], 2), ALU.mult)
                link(dve.tensor_tensor(rot[:, 1], ps, mid(cs[:, 1, :], 2), ALU.mult))
                dve.tensor_tensor(dst[:, 0, :], rot[:, 0, 0, :], rot[:, 1, 1, :], ALU.subtract)
                dve.tensor_tensor(dst[:, 1, :], rot[:, 0, 1, :], rot[:, 1, 0, :], ALU.add)\
                    .then_inc(free_bank(name), 1)

            dve.wait_ge(trig_out, 2)
            link(dve.tensor_scalar(cs, cs, 1 / WS, None, ALU.mult))
            before = None
            for g in range(NG):
                for a in range(2):
                    rotary(f"q_d{g}{a}", qr[:, 2 * g + a], before)
                    before = f"q_d{g}{a}"
            b = take(dve, "bias")
            dve.tensor_copy(bT[:].rearrange("p a c e -> p (a c e)"), b[:]).then_inc(free_bank("bias"), 1)
            emptied(dve, "cum")
            dve.tensor_scalar(st[:, 16:32].rearrange("p (f i) -> p f i", f=2),
                              B[:, :, SUB // 2::SUB], -1.0, None, ALU.mult).then_inc(anchors, 1)
            for a in range(2):
                rotary(f"k_d0{a}", kr[:, a], before)
                before = f"k_d0{a}"
            dve.wait_ge(gla_exp, 1)
            emptied(dve, "q_g")
            emptied(dve, "k_g")
            dve.scalar_tensor_tensor(qS, qS, 16 * GLA_SCALE, qg, ALU.mult, ALU.mult)
            dve.scalar_tensor_tensor(qX, qX, GLA_SCALE, qg[:, :, P:T], ALU.mult, ALU.mult)
            dve.tensor_tensor(kX, kX, kg[:, :, 0:P], ALU.mult)
            for t in range(TT):
                for i in range(NSUB):
                    n = (i + 1) * SUB
                    ins = dve.tensor_tensor(kS[:, :, t, i, 0:n], kS[:, :, t, i, 0:n], kg[:, :, t * P:t * P + n],
                                            ALU.mult)
            ins.then_inc(gla_qk, 1)
            for g in range(1, NG):
                for a in range(2):
                    rotary(f"k_d{g}{a}", kr[:, 2 * g + a], before)
                    before = f"k_d{g}{a}"
            for a in range(2):
                cut_ahead(f"v_d0{a}")
            for hd in range(GH):
                b = take(dve, f"gs{hd}")
                dve.tensor_tensor(scT[:, hd, 0:2 * P].rearrange("p (a b) -> p a b", a=2),
                                  b[:, 0:2 * P].rearrange("p (a b) -> p a b", a=2), mid(tri16[:], 2), ALU.mult)
                dve.tensor_copy(scT[:, hd, 2 * P:3 * P], b[:, 2 * P:3 * P]).then_inc(free_bank(f"gs{hd}"), 1)
            normed(1, 1, lambda t: memx[:, t, :], lambda t: memx[:, t, :], 2)
            for a in range(2):
                cut_ahead(f"v_d1{a}")
            for q in range(4):
                low_T("m_T", q, memT, vT[:, 8:16])
            for a in range(2):
                cut_ahead(f"v_d2{a}")
            for t in range(TT):
                dve.wait_ge(go_ss, 4 * t + 4)
                rsqrt_mean(st[:, 8 + 4 * t:12 + 4 * t], st[:, 8 + 4 * t:12 + 4 * t], P)
                b = pt[BANK[f"go{t}"]]
                for hd in range(GH):
                    sl = slice(hd * P, (hd + 1) * P)
                    ins = dve.scalar_tensor_tensor(og[:, t, sl], b[:, sl], st[:, 8 + 4 * t + hd:9 + 4 * t + hd],
                                                   sr[:, t, sl], ALU.mult, ALU.mult)
                ins.then_inc(free_bank(f"go{t}"), 1)

            maskf = masks[:].rearrange("p m s -> p (m s)")

            def scores(hd):
                i = hd % 2
                dve.wait_ge(masks_ready, 4)
                b = take(dve, f"s{hd}0")
                dve.tensor_tensor_reduce(out=S[:, i, 0:3 * P].rearrange("p (g s) -> p g s", g=NG),
                                         in0=b[:, 0:3 * P].rearrange("p (g s) -> p g s", g=NG),
                                         in1=masks[:, 1::2, :], scale=1.0, scalar=-3e38, op0=ALU.add, op1=ALU.max,
                                         accum_out=st[:, 32:33]).then_inc(free_bank(f"s{hd}0"), 1)
                b = take(dve, f"s{hd}1a")
                dve.tensor_tensor_reduce(out=S[:, i, 3 * P:7 * P], in0=b[:], in1=maskf[:, 0:4 * P], scale=1.0,
                                         scalar=-3e38, op0=ALU.add, op1=ALU.max, accum_out=st[:, 33:34])\
                    .then_inc(free_bank(f"s{hd}1a"), 1)
                b = take(dve, f"s{hd}1b")
                dve.tensor_tensor_reduce(out=S[:, i, 7 * P:9 * P], in0=b[:, 0:2 * P], in1=maskf[:, 4 * P:6 * P],
                                         scale=1.0, scalar=-3e38, op0=ALU.add, op1=ALU.max,
                                         accum_out=st[:, 34:35]).then_inc(free_bank(f"s{hd}1b"), 1)
                emptied(dve, f"s{hd}1b")
                link(dve.tensor_tensor(st[:, 33:34], st[:, 33:34], st[:, 34:35], ALU.max))
                dve.tensor_scalar(st[:, 36 + 2 * i:38 + 2 * i], st[:, 32:34], -ATT_SCALE, None, ALU.mult)\
                    .then_inc(s_ready, 1)

            def probs(hd):
                i = hd % 2
                dve.wait_ge(s_exp, 2 * hd + 2)
                link(dve.reciprocal(st[:, 40 + 2 * i:42 + 2 * i], st[:, 40 + 2 * i:42 + 2 * i]))
                dve.tensor_scalar(S[:, i, 0:3 * P], S[:, i, 0:3 * P], st[:, 40 + 2 * i:41 + 2 * i], None, ALU.mult)
                dve.tensor_scalar(S[:, i, 3 * P:9 * P], S[:, i, 3 * P:9 * P], st[:, 41 + 2 * i:42 + 2 * i], None,
                                  ALU.mult).then_inc(s_prob, 1)

            def probs_T(hd):
                b = take(dve, f"pt{hd}2")
                dve.tensor_copy(PT[:, hd % 2, 2, :], b[:, 0:3 * P]).then_inc(free_bank(f"pt{hd}2"), 1)

            def out_low(name, dst, a):
                b = take(dve, name)
                low(dst[:, 1, 2 * a:2 * a + 2, :].rearrange("p a b -> p (a b)"), b[:], 1.0,
                    dst[:, 0, 2 * a:2 * a + 2, :].rearrange("p a b -> p (a b)")).then_inc(free_bank(name), 1)

            for hd in range(NH):
                scores(hd)
                cut_ahead(f"eg{2 * hd}")
                probs(hd)
                cut_ahead(f"eg{2 * hd + 1}")
                if hd == 0:
                    for q in range(2):
                        low_T("gt", q, ogT, vT[:, 24:28])
                else:
                    probs_T(hd - 1)
                if hd == 2:
                    out_low("pv0", odT, 0)
            for a in range(2):
                cut_ahead(f"xk{a}")
            probs_T(3)
            out_low("pv1", odT, 1)
            for i in range(2):
                cut_ahead(f"gla{i}")
                for q in (2 * i, 2 * i + 1):
                    b = take(dve, f"bg{q}")
                    if q == 0:
                        emptied(dve, "eg7")
                    g0 = gates[:, 2 * q:2 * q + 2, :].rearrange("p a b -> p (a b)")
                    dve.scalar_tensor_tensor(g0, g0, 1.0, b[:], ALU.add, ALU.mult).then_inc(free_bank(f"bg{q}"), 1)
                cut_ahead(f"dil{i}")
                for q in (2 * i, 2 * i + 1):
                    b = take(dve, f"bd{q}")
                    g0 = gates[:, 2 * q:2 * q + 2, :].rearrange("p a b -> p (a b)")
                    g1 = gates[:, 8 + 2 * q:10 + 2 * q, :].rearrange("p a b -> p (a b)")
                    dve.scalar_tensor_tensor(g1, g1, 1.0, b[:], ALU.add, ALU.mult).then_inc(free_bank(f"bd{q}"), 1)
                    emptied(dve, f"bd{q}")
                    dve.tensor_tensor(g0, g0, g1, ALU.add).then_inc(merged_sum, 1)
                    m = mergedT[:, :, 2 * q:2 * q + 2, :].rearrange("p k a b -> p k (a b)")
                    low(m[:, 1], g0, 0.5 / WS, m[:, 0]).then_inc(merged_ready, 1)
            for q in range(4):
                cut_ahead(f"mix{q}")
                b = take(dve, f"mix{q}")
                hh = h[:, :, q * 256:(q + 1) * 256]
                dve.scalar_tensor_tensor(hh, b[:].rearrange("p (t n) -> p t n", t=TT), 1 / WS, hh, ALU.mult, ALU.add)\
                    .then_inc(free_bank(f"mix{q}"), 1)
            normed(2, 4, lambda t: h[:, t, :], lambda t: xn[:, t, :], 4)
            cut_ahead("xv0")
            for q in range(4):
                low_T("c_T", q, aT, vT[:, 16:24])
            for name in ("xv1", "xq0", "xq1"):
                cut_ahead(name)

            def x_max(hd):
                i = hd % 2
                b = take(dve, f"xs{hd}")
                m = st[:, 32 + 2 * i:34 + 2 * i]
                link(dve.reduce_max(m, b[:].rearrange("p (a b) -> p a b", a=2), AX))
                dve.tensor_scalar(st[:, 44 + 2 * i:46 + 2 * i], m, -ATT_SCALE, None, ALU.mult)\
                    .then_inc(xs_max, 1)

            def x_prob(hd):
                i = hd % 2
                dve.wait_ge(xs_exp, hd + 1)
                emptied(dve, f"xs{hd}")
                link(dve.reciprocal(st[:, 48 + 2 * i:50 + 2 * i], st[:, 48 + 2 * i:50 + 2 * i]))
                for t in range(TT):
                    ins = dve.tensor_scalar(xP[:, i, t, :], xP[:, i, t, :], st[:, 48 + 2 * i + t:49 + 2 * i + t],
                                            None, ALU.mult)
                ins.then_inc(xs_prob, 1)

            x_max(0)
            x_max(1)
            for hd in range(NH):
                x_prob(hd)
                if hd + 2 < NH:
                    x_max(hd + 2)
                if hd == 2:
                    out_low("xpv0", oxT, 0)
            out_low("xpv1", oxT, 1)
            for n in range(2):
                cut_ahead(f"xo{n}")
                for t in range(TT):
                    b = take(dve, f"xo{n}{t}")
                    hh = h[:, t, n * 512:(n + 1) * 512]
                    dve.scalar_tensor_tensor(hh, b[:], 1 / WS, hh, ALU.mult, ALU.add)\
                        .then_inc(free_bank(f"xo{n}{t}"), 1)
            normed(3, 2, lambda t: h[:, t, :].rearrange("p (q c) -> p c q", c=C), lambda t: f[:, t], 6)
            for q in range(4):
                b = take(dve, f"f_T{q}")
                dve.tensor_tensor(fT[:, 2 * q:2 * q + 2, :], b[:].rearrange("p (a b) -> p a b", a=2),
                                  bc(g3[:, 2 * q:2 * q + 2], T), ALU.mult).then_inc(free_bank(f"f_T{q}"), 1)
            b = take(dve, "rt")
            dve.tensor_copy(logit.rearrange("p a b -> p (a b)"), b[:, 0:TT * E]).then_inc(free_bank("rt"), 1)
            emptied(dve, "rt")
            for t in range(TT):
                link(dve.max(top[:, t, :], logit[:, t, :]))
                link(dve.max_index(idx_u[:, t, :], top[:, t, :], logit[:, t, :]))
            link(dve.tensor_copy(idx_f, idx_u[:, :, 0:TOPK]))
            dve.tensor_scalar(st[:, 52:54], top[:, :, 0], -1.0, None, ALU.mult).then_inc(top_ready, 1)
            hot, hot_g = oneh[:, 0:TT * TOPK, :], oneh[:, TT * TOPK:, :]
            link(dve.tensor_tensor(hot, mid(iota_e[:], TT * TOPK), bc(idx_f.rearrange("p a b -> p (a b)"), E),
                                   ALU.is_equal))
            dve.reduce_sum(mask, hot.rearrange("p (t k) e -> p t e k", t=TT), AX).then_inc(gate_ready, 1)
            dve.wait_ge(top_exp, 2)
            link(dve.reciprocal(st[:, 54:56], st[:, 54:56]))
            link(dve.tensor_tensor(g4, g4, bc(st[:, 54:56], TOPK), ALU.mult))
            link(dve.tensor_tensor(hot_g, hot, bc(g4.rearrange("p a b -> p (a b)"), E), ALU.mult))
            dve.reduce_sum(gate, hot_g.rearrange("p (t k) e -> p t e k", t=TT), AX).then_inc(gate_ready, 1)
            b = take(dve, "pos")
            link(dve.scalar_tensor_tensor(place.rearrange("p a b -> p (a b)"), b[:, 0:TT * E], 1.0,
                                          mask.rearrange("p a b -> p (a b)"), ALU.add, ALU.mult))
            link(dve.tensor_scalar(place, place, -1.0, None, ALU.add))
            link(dve.reduce_max(st[:, 60:61], b[:, TT * E:(TT + 1) * E], AX))
            dve.tensor_scalar(over[:], st[:, 60:61], float(SLOTS), None, ALU.is_gt).then_inc(over_ready, 1)
            dve.wait_ge(over_ready, 1)
            dve.memset(st[:, 61:62], 0.0).then_inc(free_bank("pos"), 1)
            b = take(dve, "gT")
            dve.tensor_copy(gateT[0:E, :], b[0:E, 0:T]).then_inc(free_bank("gT"), 1)
            dve.memset(st[:, 63:64], 0.0).then_inc(round_chain, 1)

            def body(n, k):
                count = [0]

                def link2(ins):
                    count[0] += 1
                    ins.then_inc(moe_chain, 1)
                    dve.wait_ge(moe_chain, k * LINKS + count[0])

                for t in range(TT):
                    link2(dve.tensor_tensor(sel[:, t, :].rearrange("p (e s) -> p e s", e=EG),
                                            bc(place[:, t, bass.ds(n * EG, EG)], SLOTS), mid(iota_s[:], EG),
                                            ALU.is_equal))
                for t in range(TT):
                    s4 = sel[:, t, :].rearrange("p (e s) -> p e s", e=EG)
                    ins = dve.tensor_tensor(
                        selG[:, t], s4.unsqueeze(2).to_broadcast([P, EG, 2, SLOTS]),
                        gate[:, t, bass.ds(n * EG, EG)].unsqueeze(2).unsqueeze(3).to_broadcast([P, EG, 2, SLOTS]),
                        ALU.mult)
                ins.then_inc(sel_ready, 1)
                for q in (1, 3):
                    dve.wait_ge(gathered, 4 * k + (q + 1))
                    dve.tensor_tensor(xg[:, 2 * q:2 * q + 2, :], pt[q][:].rearrange("p (a b) -> p a b", a=2),
                                      bc(g3[:, 2 * q:2 * q + 2], T), ALU.mult).then_inc(xg_dve, 1)
                dve.wait_ge(selT_full, 2 * k + 2)
                dve.tensor_copy(selT[:, 2:4].rearrange("p e t s -> p (e t s)"), pt[1][:]).then_inc(selT_dve, 1)
                for j in range(EG):
                    e = n * EG + j
                    dve.wait_ge(h_full, k * EG + (j + 1))
                    dve.tensor_copy(hs[:, :, 64:128], pt[1][:].rearrange("p (q c) -> p c q", c=C))\
                        .then_inc(hs_dve, 1)
                    for i in range(2):
                        cc = slice(4 * i, 4 * i + 4)
                        up = pt[i][:].rearrange("p (c b s) -> p b c s", c=4, b=2)
                        bias = [bT[:, b, cc, bass.ds(e, 1)].to_broadcast([P, 4, SLOTS]) for b in range(2)]
                        dve.wait_ge(T_full, k * 2 * EG + (2 * j + i + 1))
                        link2(dve.tensor_tensor(g_sb[:, cc, :], up[:, 0], bias[0], ALU.add))
                        dve.tensor_scalar(g_sb[:, cc, :], g_sb[:, cc, :], LIMIT, None, ALU.min)\
                            .then_inc(g_ready, 1)
                        link2(dve.tensor_tensor(l_sb[:, cc, :], up[:, 1], bias[1], ALU.add))
                        link2(dve.tensor_scalar(l_sb[:, cc, :], l_sb[:, cc, :], LIMIT, -LIMIT, ALU.min, ALU.max))
                        dve.scalar_tensor_tensor(l_sb[:, cc, :], l_sb[:, cc, :], 1.0, g_sb[:, cc, :],
                                                 ALU.add, ALU.mult).then_inc(lin_chain, 1)
                        dve.wait_ge(lin_chain, k * 2 * EG + (2 * j + i + 1))
                        dve.wait_ge(sg_ready, k * 2 * EG + (2 * j + i + 1))
                        dve.tensor_tensor(actT[:, cc, :], l_sb[:, cc, :], sg_sb[:, cc, :], ALU.mult)\
                            .then_inc(act_ready, 1)
                assert count[0] == LINKS, count[0]

            expert_groups(dve, body)

            for t in range(TT):
                dve.wait_ge(fin_ss, 2 * t + 2)
                v = st[:, 56 + 2 * t:57 + 2 * t]
                link(dve.tensor_tensor(v, v, st[:, 57 + 2 * t:58 + 2 * t], ALU.add))
                rsqrt_mean(v, v, D)
                if t == 0:
                    dve.wait_ge(ld_late, 16 * 6)
                for i in range(2):
                    ins = dve.scalar_tensor_tensor(out_sb[:, t, i * 512:(i + 1) * 512], pt[4 + 2 * t + i][:], v,
                                                   gfin[:, i * 512:(i + 1) * 512], ALU.mult, ALU.mult)
                ins.then_inc(fin_ready, 1)

        @block.tensor
        def _(pe):
            mm = pe.matmul

            def fill(name):
                if TURN[name]:
                    pe.wait_ge(free[BANK[name]], TURN[name])
                return pt[BANK[name]]

            def filled(ins, name):
                ins.then_inc(full[BANK[name]], 1)

            def weights(name):
                u = HALVES.index(name)
                pe.wait_ge(w_low, u + 1)
                return cut[u % EARLY].rearrange("p k (c n) -> p k c n", n=SRC[name].shape[2])

            PASSES = ((0, 0), (0, 1), (1, 0))

            def feature_major(name, w, rhs, nk, col=0):
                b = fill(name)
                for i in range(2):
                    o = col + i * P
                    for c in range(nk):
                        for k, (pw, px) in enumerate(PASSES):
                            ins = mm(b[:, i * T:(i + 1) * T], w[:, pw, c, o:o + P], rhs[:, px, c, :],
                                     start=(c == 0 and k == 0), stop=(c == nk - 1 and k == 2))
                filled(ins, name)

            def token_major(name, w, lhs, nk, tiles, n):
                b = fill(name)
                for i, t in enumerate(tiles):
                    for c in range(nk):
                        for k, (pw, px) in enumerate(PASSES):
                            ins = mm(b[:, i * n:(i + 1) * n], lhs[:, px, c, t * P:(t + 1) * P], w[:, pw, c, 0:n],
                                     start=(c == 0 and k == 0), stop=(c == nk - 1 and k == 2))
                filled(ins, name)

            def norm_transposes(prefix, src, count):
                pe.wait_ge(norm_xn, count)
                for q in range(4):
                    b = fill(f"{prefix}{q}")
                    for i in range(2):
                        for t in range(TT):
                            ins = pe.transpose(b[:, i * T + t * P:i * T + (t + 1) * P], src(t, 2 * q + i), ident[:])
                    filled(ins, f"{prefix}{q}")

            pe.wait_ge(consts, 9)
            pe.wait_ge(ld_small, SMALL)
            b = fill("vec")
            filled(pe.transpose(b[:, 0:44], rows[0:44, :], ident[0:44, 0:44]), "vec")

            norm_transposes("x_T", lambda t, c: xn[:, t, c * P:(c + 1) * P], 2)
            for q in range(4):
                emptied(pe, f"x_T{q}")
            pe.wait_ge(alr_cut, 2)
            b = fill("alr")
            for c in range(C):
                for k, (pw, px) in enumerate(PASSES):
                    ins = mm(b[0:16, 0:T], w_alr16[:, pw, c, :], aT[:, px, c, :], start=(c == 0 and k == 0),
                             stop=(c == C - 1 and k == 2))
            filled(ins, "alr")
            for k in ("q_g", "k_g"):
                feature_major(k, weights(k), aT, C)
            for k in ("v_g0", "v_g1", "r_g0", "r_g1"):
                token_major(k, weights(k), aT, C, (0, 1), 256)
            b = fill("lg")
            emptied(pe, "alr")
            for t in range(TT):
                ins = mm(b[:, t * T:(t + 1) * T], alr[0:17, t * P:(t + 1) * P], w2[0:17, :], start=True, stop=True)
            filled(ins, "lg")

            def rotary_halves(name, w):
                b = fill(name)
                for i in range(2):
                    for c in range(C):
                        for k, (pw, px) in enumerate(PASSES):
                            for hp in range(2):
                                o = hp * DH + 64 * i
                                ins = mm(b[64 * hp:64 * hp + 64, i * T:(i + 1) * T], w[:, pw, c, o:o + 64],
                                         aT[:, px, c, :], start=(c == 0 and k == 0), stop=(c == C - 1 and k == 2))
                filled(ins, name)

            for g in range(NG):
                for a in range(2):
                    rotary_halves(f"q_d{g}{a}", weights(f"q_d{g}{a}"))
            pe.wait_ge(ld_brows, 32)
            b = fill("bias")
            for k in range(2):
                for c in range(C):
                    o = (k * C + c) * E
                    ins = pe.transpose(b[:, o:o + E], brows[0:E, k, c::C], ident[0:E, 0:E])
            filled(ins, "bias")
            b = fill("cum")
            emptied(pe, "lg")
            for fc in range(2):
                for t in range(TT):
                    ins = mm(b[:, fc * T + t * P:fc * T + (t + 1) * P], la[:, t, fc * P:(fc + 1) * P], tri16[:],
                             start=True, stop=True)
            filled(ins, "cum")
            for g in range(NG):
                for a in range(2):
                    rotary_halves(f"k_d{g}{a}", weights(f"k_d{g}{a}"))

            def v_dil(g):
                for a in range(2):
                    token_major(f"v_d{g}{a}", weights(f"v_d{g}{a}"), aT, C, (0, 1), 256)

            v_dil(0)
            pe.wait_ge(gla_qk, 1)
            for hd in range(GH):
                b = fill(f"gs{hd}")
                hp, fc = slice(64 * (hd % 2), 64 * (hd % 2) + 64), hd // 2
                for t in range(TT):
                    for i in range(NSUB):
                        a0 = t * P + i * SUB
                        mm(b[:, a0:a0 + SUB], kS[hp, fc, t, i, :], qS[hp, fc, a0:a0 + SUB], start=True, stop=True)
                filled(mm(b[:, 2 * P:3 * P], kX[hp, fc, :], qX[hp, fc, :], start=True, stop=True), f"gs{hd}")
            v_dil(1)
            norm_transposes("m_T", lambda t, c: memx[:, t, c * P:(c + 1) * P], 4)
            v_dil(2)
            emptied(pe, "gs3")
            emptied(pe, "v_g1")
            for t in range(TT):
                b = fill(f"go{t}")
                for hd in range(GH):
                    sl = slice(hd * P, (hd + 1) * P)
                    ins = mm(b[:, sl], scT[:, hd, t * P:(t + 1) * P], vg[:, t, sl], start=True, stop=(t == 0))
                    if t:
                        ins = mm(b[:, sl], scT[:, hd, 2 * P:3 * P], vg[:, 0, sl], start=False, stop=True)
                filled(ins, f"go{t}")

            def dil_scores(hd):
                hp, a = slice(64 * (hd % 2), 64 * (hd % 2) + 64), hd // 2

                def one(dst, g, t):
                    for j in range(2):
                        ins = mm(dst, qr[hp, 2 * g + a, j, t * P:(t + 1) * P], kr[hp, 2 * g + a, j, 0:(t + 1) * P],
                                 start=(j == 0), stop=(j == 1))
                    return ins
                b = fill(f"s{hd}0")
                for g in range(NG):
                    ins = one(b[:, g * P:(g + 1) * P], g, 0)
                filled(ins, f"s{hd}0")
                b = fill(f"s{hd}1a")
                for g in range(2):
                    ins = one(b[:, g * T:(g + 1) * T], g, 1)
                filled(ins, f"s{hd}1a")
                b = fill(f"s{hd}1b")
                filled(one(b[:, 0:T], 2, 1), f"s{hd}1b")

            def dil_transposes(hd):
                pe.wait_ge(s_prob, hd + 1)
                for g in range(NG):
                    b = fill(f"pt{hd}{g}")
                    for i, c0 in enumerate((g * P, 3 * P + g * T, 3 * P + g * T + P)):
                        ins = pe.transpose(b[:, i * P:(i + 1) * P], S[:, hd % 2, c0:c0 + P], ident[:])
                    filled(ins, f"pt{hd}{g}")

            def dil_out(a):
                b = fill(f"pv{a}")
                for i in range(2):
                    hd = 2 * a + i
                    for g in range(NG):
                        emptied(pe, f"pt{hd}{g}")
                        mm(b[:, i * T:(i + 1) * T], vd[:, 0, g * 512 + hd * P:g * 512 + (hd + 1) * P],
                           PT[:, i, g, 0:T], start=(g == 0), stop=False)
                    for g in range(NG):
                        ins = mm(b[:, i * T + P:(i + 1) * T], vd[:, 1, g * 512 + hd * P:g * 512 + (hd + 1) * P],
                                 PT[:, i, g, T:3 * P], start=False, stop=(g == NG - 1))
                filled(ins, f"pv{a}")

            for hd in range(NH):
                dil_scores(hd)
                for q in (2 * hd, 2 * hd + 1):
                    feature_major(f"eg{q}", weights(f"eg{q}"), aT, C)
                if hd == 0:
                    emptied(pe, "go0")
                    emptied(pe, "go1")
                    for q in range(2):
                        b = fill(f"gt{q}")
                        for i in range(2):
                            for t in range(TT):
                                c = 2 * q + i
                                ins = pe.transpose(b[:, i * T + t * P:i * T + (t + 1) * P],
                                                   og[:, t, c * P:(c + 1) * P], ident[:])
                        filled(ins, f"gt{q}")
                else:
                    dil_transposes(hd - 1)
                if hd == 2:
                    dil_out(0)
            for q in range(4):
                emptied(pe, f"m_T{q}")
            for a in range(2):
                feature_major(f"xk{a}", weights(f"xk{a}"), memT, C)
            dil_transposes(3)
            dil_out(1)

            for name in ("gt0", "gt1", "pv0", "pv1"):
                emptied(pe, name)
            for i in range(2):
                for k, half, src in (("bg", "gla", ogT), ("bd", "dil", odT)):
                    w = weights(f"{half}{i}")
                    for j in range(2):
                        feature_major(f"{k}{2 * i + j}", w, src, 4, j * 256)
            pe.wait_ge(merged_ready, 4)
            for q in range(4):
                token_major(f"mix{q}", weights(f"mix{q}"), mergedT, C, (0, 1), 256)
            token_major("xv0", weights("xv0"), memT, C, (0, 1), 256)

            norm_transposes("c_T", lambda t, c: xn[:, t, c * P:(c + 1) * P], 6)
            token_major("xv1", weights("xv1"), memT, C, (0, 1), 256)
            for q in range(4):
                emptied(pe, f"c_T{q}")
            for a in range(2):
                feature_major(f"xq{a}", weights(f"xq{a}"), aT, C)

            def x_scores(hd):
                emptied(pe, f"xq{hd // 2}")
                b = fill(f"xs{hd}")
                for t in range(TT):
                    ins = mm(b[:, t * M:(t + 1) * M], xq[:, hd, t * P:(t + 1) * P], xk[:, hd, :], start=True,
                             stop=True)
                filled(ins, f"xs{hd}")

            def x_transposes(hd):
                pe.wait_ge(xs_prob, hd + 1)
                b = fill(f"xt{hd}")
                for s in range(2):
                    for t in range(TT):
                        ins = pe.transpose(b[:, s * T + t * P:s * T + (t + 1) * P],
                                           xP[:, hd % 2, t, s * P:(s + 1) * P], ident[:])
                filled(ins, f"xt{hd}")

            def x_out(a):
                b = fill(f"xpv{a}")
                for i in range(2):
                    hd = 2 * a + i
                    emptied(pe, f"xt{hd}")
                    for s in range(2):
                        ins = mm(b[:, i * T:(i + 1) * T], xv[:, s, hd * P:(hd + 1) * P], xPT[:, i, s, :],
                                 start=(s == 0), stop=(s == 1))
                filled(ins, f"xpv{a}")

            for name in ("xk0", "xk1", "xv0", "xv1"):
                emptied(pe, name)
            x_scores(0)
            x_scores(1)
            x_transposes(0)
            x_scores(2)
            x_transposes(1)
            x_out(0)
            x_scores(3)
            x_transposes(2)
            x_transposes(3)
            x_out(1)
            emptied(pe, "xpv0")
            emptied(pe, "xpv1")
            for n in range(2):
                w = weights(f"xo{n}")
                for t in range(TT):
                    token_major(f"xo{n}{t}", w, oxT, 4, (t,), 512)
            acc = [[pt[4 + 2 * t + n] for n in range(2)] for t in range(TT)]
            for b in range(4, BANKS):
                pe.wait_ge(free[b], USES[b])
            for n in range(2):
                for t in range(TT):
                    emptied(pe, f"xo{n}{t}")
                    mm(acc[t][n][:], ident[:], h[:, t, n * 512:(n + 1) * 512], start=True, stop=False)

            norm_transposes("f_T", lambda t, c: f[:, t, c, :], 8)
            for q in range(4):
                emptied(pe, f"f_T{q}")
            b = fill("rt")
            for t in range(TT):
                for c in range(C):
                    mm(b[:, t * E:(t + 1) * E], fT[:, c, t * P:(t + 1) * P], w_rt[:, c, :], start=(c == 0), stop=False)
                ins = mm(b[:, t * E:(t + 1) * E], ones[0:1, :], b_rt[0:1, :], start=False, stop=True)
            filled(ins, "rt")
            pe.wait_ge(gate_ready, 1)
            b = fill("pos")
            mm(b[:, 0:E], tri_s[:], mask[:, 0, :], start=True, stop=True)
            mm(b[:, E:2 * E], tri_s[:], mask[:, 1, :], start=True, stop=False)
            mm(b[:, E:2 * E], ones[:], mask[:, 0, :], start=False, stop=True)
            mm(b[:, 2 * E:3 * E], ones[:], mask[:, 0, :], start=True, stop=False)
            filled(mm(b[:, 2 * E:3 * E], ones[:], mask[:, 1, :], start=False, stop=True), "pos")
            pe.wait_ge(gate_ready, 2)
            b = fill("gT")
            for t in range(TT):
                ins = pe.transpose(b[0:E, t * P:(t + 1) * P], gate[:, t, :], ident[:])
            filled(ins, "gT")

            for b in range(4):
                pe.wait_ge(free[b], USES[b])

            per = 6 * EG

            def body(n, k):
                pe.wait_ge(sel_ready, k + 1)
                for q in range(4):
                    for i in range(2):
                        for t in range(TT):
                            ins = mm(pt[q][:, i * T:(i + 1) * T], f[:, t, 2 * q + i, :], sel[:, t, :],
                                     start=(t == 0), stop=(t == TT - 1))
                    ins.then_inc(gathered, 1)
                for q in range(2):
                    if q == 0:
                        pe.wait_ge(xg_act, 2 * k + 1)
                    else:
                        pe.wait_ge(xg_dve, 2 * k + 1)
                    for i in range(2):
                        for t in range(TT):
                            o = (i * TT + t) * P
                            ins = pe.transpose(pt[q][:, o:o + P],
                                               selG[:, t, 2 * q + i].rearrange("p a s -> p (a s)"), ident[:])
                    ins.then_inc(selT_full, 1)
                pe.wait_ge(xg_act, 2 * k + 2)
                pe.wait_ge(xg_dve, 2 * k + 2)
                pe.wait_ge(selT_act, k + 1)
                pe.wait_ge(selT_dve, k + 1)

                def loaded(v):
                    pe.wait_ge(late_ld[v % NSLOT], k * (16 * per // NSLOT) + 16 * (v // NSLOT + 1))
                    return slot[v % NSLOT].rearrange("p (c n) -> p c n", n=D)

                for j in range(EG):
                    v = 6 * j
                    xe = [xg[:, c, j * SLOTS:(j + 1) * SLOTS] for c in range(C)]
                    for half in range(2):
                        wg, wu = loaded(v + 2 * half), loaded(v + 2 * half + 1)
                        for c4 in range(4):
                            c = 4 * half + c4
                            for nh in range(2):
                                for col, w in ((0, wg), (64, wu)):
                                    ins = mm(pt[nh][col:col + 64, :], xe[c], w[:, c4, nh * 512:(nh + 1) * 512],
                                             start=(c == 0), stop=(c == C - 1))
                        if half == 0:
                            ins.then_inc(gu_half, 1)
                    ins.then_inc(h_full, 1)
                    pe.wait_ge(hs_act, k * EG + (j + 1))
                    pe.wait_ge(hs_dve, k * EG + (j + 1))
                    for i in range(2):
                        for c in range(4):
                            ins = pe.transpose(pt[i][:, c * P:(c + 1) * P], hs[:, 4 * i + c, :], ident[:])
                        ins.then_inc(T_full, 1)
                    for half in range(2):
                        w = loaded(v + 4 + half)
                        pe.wait_ge(act_ready, k * 2 * EG + (2 * j + half + 1))
                        for c4 in range(4):
                            c = 4 * half + c4
                            for nh in range(2):
                                ins = mm(pt[2][64 * nh:64 * nh + 64, :], actT[:, c, :],
                                         w[:, c4, nh * 512:(nh + 1) * 512], start=(c == 0), stop=(c == C - 1))
                        if half == 0:
                            ins.then_inc(dn_half, 1)
                    ins.then_inc(y_full, 1)
                    pe.wait_ge(y_ready, k * EG + (j + 1))
                    for t in range(TT):
                        for nh in range(2):
                            rows_h = slice(64 * nh, 64 * nh + 64)
                            mm(acc[t][nh][:], selT[rows_h, j, t, :], y[rows_h, :], start=False, stop=False)

            expert_groups(pe, body)

            pe.wait_ge(ld_late, 16 * 6)
            for t in range(TT):
                for n in range(2):
                    mm(acc[t][n][:], gateT[0:E, t * P:(t + 1) * P], b_dn[0:E, n * 512:(n + 1) * 512],
                       start=False, stop=True).then_inc(acc_full, 1)


_INS = ['x', 'mem', 'positions', 'norm1_g', 'w_in', 'w_gla_a2', 'b_gla_a2', 'gla_norm_g', 'w_branch_gla',
        'w_branch_dil', 'w_branch_gate', 'b_branch_gate', 'w_mix_out', 'norm2_g', 'mem_norm_g', 'w_xq', 'w_xkv',
        'w_xo', 'norm3_g', 'w_router', 'b_router', 'w_gate', 'b_gate', 'w_up', 'b_up', 'w_down', 'b_down',
        'final_norm_g']


def kernel(**inputs):
    import concourse.bacc as bacc
    from concourse.bass_utils import run_bass_kernel_spmd

    nc = bacc.Bacc("TRN2", target_bir_lowering=False, num_devices=1)
    arrays, A = {}, {}
    freq = np.float32(10000.0) ** (-np.arange(64, dtype=np.float32) / np.float32(64))
    inputs["inv_freq"] = np.concatenate([freq, freq]).reshape(128, 1).astype(np.float32)
    for name in _INS + ["inv_freq"]:
        a = np.ascontiguousarray(inputs[name])
        arrays[f"in_{name}"] = a
        A[name] = nc.dram_tensor(f"in_{name}", a.shape, mybir.dt.from_np(a.dtype), kind="ExternalInput").ap()
    out = nc.dram_tensor("out_0", (1, T, D), F32, kind="ExternalOutput").ap()
    _program(nc, A, out)
    r = run_bass_kernel_spmd(nc, [arrays], core_ids=[0])
    return r.results[0]["out_0"]
```

```python
from contextlib import ExitStack

import numpy as np

import concourse.bass as bass
from concourse import mybir

F32 = mybir.dt.float32
F16 = mybir.dt.float16
I32 = mybir.dt.int32
U32 = mybir.dt.uint32
ALU = mybir.AluOpType
ACT = mybir.ActivationFunctionType
AX = mybir.AxisListType.X

P = 128
T = 256
TT = T // P
D = 1024
C = D // P
M = 256
EPS = 1e-5
DK = 64
GH = 4
DH = 128
NG = 3
NH = 4
SUB = 32
NSUB = P // SUB
E = 32
TOPK = 4
SLOTS = 64
EG = 4
GROUPS = E // EG
ROUNDS = T // SLOTS
LIMIT = 7.0
ALPHA = 1.702
NEG = -1.0e30
GLA_SCALE = DK ** -0.5
ATT_SCALE = DH ** -0.5
TWO_PI_HI = 6.28125
TWO_PI_LO = 2 * np.pi - TWO_PI_HI
MAGIC = 12582912.0

UNIT = 2048
NSLOT = 16
EARLY = 3
BANKS = 8

HALVES = ["q_g", "k_g", "v_g0", "v_g1", "r_g0", "r_g1"]
HALVES += [f"{k}{g}{a}" for k in ("q_d", "k_d", "v_d") for g in range(NG) for a in range(2)]
HALVES += [f"eg{q}" for q in range(8)] + ["xk0", "gla0", "dil0", "gla1", "dil1", "xk1"]
HALVES += [f"mix{q}" for q in range(4)] + ["xv0", "xv1", "xq0", "xq1", "xo0", "xo1"]
HALF = UNIT
WS = 64.0

FILLS = ["vec"] + [f"x_T{i}" for i in range(4)] + ["q_g", "k_g", "alr", "v_g0", "v_g1", "r_g0", "r_g1", "lg"]
FILLS += [f"q_d{g}{a}" for g in range(NG) for a in range(2)] + ["bias", "cum"]
FILLS += [f"k_d{g}{a}" for g in range(NG) for a in range(2)]
for _h in range(GH):
    FILLS += [f"v_d{_h // 2}{_h % 2}", f"gs{_h}"]
FILLS += [f"m_T{i}" for i in range(4)] + ["v_d20", "v_d21", "go0", "go1"]
for _h in range(NH):
    FILLS += [f"s{_h}0", f"s{_h}1a", f"s{_h}1b", f"eg{2 * _h}", f"eg{2 * _h + 1}"]
    if _h == 0:
        FILLS += ["gt0", "gt1"]
    else:
        FILLS += [f"pt{_h - 1}{g}" for g in range(NG)]
    if _h == 2:
        FILLS += ["pv0"]
FILLS += ["xk0"] + [f"pt3{g}" for g in range(NG)] + ["pv1"]
for _i in range(2):
    FILLS += [f"bg{2 * _i}", f"bg{2 * _i + 1}", f"bd{2 * _i}", f"bd{2 * _i + 1}"]
FILLS += ["xk1"] + [f"mix{q}" for q in range(4)] + ["xv0"] + [f"c_T{i}" for i in range(4)]
FILLS += ["xv10", "xq0", "xv11", "xq1", "xs0", "xs1", "xs2", "xs3", "xt0", "xt1", "xt2", "xpv0", "xt3", "xpv1"]
FILLS += [f"xo{n}{t}" for n in range(2) for t in range(TT)]
FILLS += [f"f_T{i}" for i in range(4)] + ["rt", "pos", "all", "gT"]
assert len(set(FILLS)) == len(FILLS)
LAST_FILL = {k: k for k in HALVES if k in FILLS}
LAST_FILL.update({"gla0": "bg1", "dil0": "bd1", "gla1": "bg3", "dil1": "bd3", "xv1": "xv11",
                  "xo0": "xo01", "xo1": "xo11"})
_N = FILLS.index("f_T0")
BANK = {f: i % BANKS if i < _N else (i - _N) % 4 for i, f in enumerate(FILLS)}
TURN = {f: sum(BANK[e] == BANK[f] for e in FILLS[:i]) for i, f in enumerate(FILLS)}
USES = [sum(BANK[f] == b for f in FILLS) for b in range(BANKS)]


def _program(nc, A, out):
    ctx = ExitStack()
    with ctx:
        def sb(name, shape, dt=F32):
            return ctx.enter_context(nc.sbuf_tensor(name, shape, dt))

        def sem(name):
            return ctx.enter_context(nc.semaphore(name))

        ring = sb("ring", [P, NSLOT * UNIT])
        h = sb("h", [P, TT, D])
        reg_a = sb("reg_a", [P, C * T])
        reg_m = sb("reg_m", [P, C * T])
        reg_t = sb("reg_t", [P, C * T])
        reg_g = sb("reg_g", [P, 2 * C * T])
        reg_o = sb("reg_o", [P, 8 * T])
        reg_l = sb("reg_l", [P, 3072])
        ident = sb("ident", [P, P])
        tri16 = sb("tri16", [P, P])
        tri_s = sb("tri_s", [P, P])
        ones = sb("ones", [P, P])
        masks = sb("masks", [P, 6, P])
        vT = sb("vT", [P, 44])
        iota_s = sb("iota_s", [P, SLOTS])
        iota_e = sb("iota_e", [P, E])
        bT = sb("bT", [P, 2, C, E])
        g3 = sb("g3", [P, C])
        w_rt = sb("w_rt", [P, C, E])
        b_rt = sb("b_rt", [1, E])
        route = sb("route", [P, 3, TT, E])
        st = sb("st", [P, 64])
        ssq = sb("ssq", [P, 4, TT, 4])
        neg_half = sb("neg_half", [P, 4])
        over = sb("over", [P, 1], I32)

        place, gate, mask = route[:, 0], route[:, 1], route[:, 2]

        def region(r, at, *shape):
            n = int(np.prod(shape))
            v = r[:, at:at + n]
            if len(shape) == 1:
                return v
            names = "abcdef"[:len(shape)]
            return v.rearrange(f"p ({' '.join(names)}) -> p {' '.join(names)}",
                               **{k: s for k, s in zip(names[1:], shape[1:])})

        slot = [region(ring, s * UNIT, UNIT) for s in range(NSLOT)]
        at = 2 * EARLY * UNIT
        qr = region(ring, at, NG * 2, 2, T)
        kr = region(ring, at + 3072, NG * 2, 2, T)
        vd = region(ring, at + 6144, TT, NG * NH * DH)
        brows = region(ring, at + 6144, 2, D)
        kS = region(ring, at + 9216, 2, TT, NSUB, P)
        S = region(ring, at + 11264, 2, 9 * P)
        rot = region(ring, at + 11264, 2, 2, T)
        PT = region(ring, at + 13568, 2, NG, 3 * P)
        B = region(ring, at + 13568, 2, T)
        scT = region(ring, at + 15872, GH, 3 * P)
        og = region(ring, at + 17408, TT, GH * P)
        sr = region(ring, at + 18432, TT, GH * P)
        la = region(ring, at + 19456, TT, T)
        cs = region(ring, at + 19968, 2, T)

        raw = [region(ring, i * HALF, HALF) for i in range(EARLY)]
        cut = [ring[:, (EARLY + i) * HALF:(EARLY + i + 1) * HALF].bitcast(F16)
               .rearrange("p (k n) -> p k n", k=2) for i in range(EARLY)]

        def parts(r, at, chunks):
            return r[:, at:at + chunks * T].bitcast(F16).rearrange("p (k c t) -> p k c t", k=2, c=chunks)

        def paired(u):
            return cut[u % EARLY].rearrange("p k (i c n) -> p k i c n", i=2, c=C)

        def rotary_cut(u, part, i):
            src = raw[u % EARLY].rearrange("p (c i n) -> p c i n", c=2 * C, i=2)
            dst = cut[u % EARLY].rearrange("p k (i c n) -> p k i c n", i=2, c=2 * C)
            return dst[:, part, i], src[:, :, i]

        aT = parts(reg_a, 0, C)
        fT = region(reg_a, 0, C, T)
        f16 = h[:].rearrange("p t d -> p (t d)").bitcast(F16).rearrange("p (k t c n) -> p k t c n", k=2, t=TT, c=C)
        xg = region(reg_a, 0, C, T)
        memx = region(reg_m, 0, TT, D)
        mergedT = parts(reg_m, 0, C)
        f = region(reg_m, 0, TT, C, P)
        out_sb = region(reg_m, 0, TT, D)
        memT = parts(reg_t, 0, C)
        hs = region(reg_t, 0, C, P)
        y = region(reg_t, 1024, 512)
        sel = reg_t[:, 1536:1536 + EG * SLOTS].bitcast(F16).rearrange("p (t n) -> p t n", t=TT)
        xn = region(reg_g, 0, TT, D)
        alr = region(reg_g, 2048, T)
        w2 = region(reg_g, 2304, T)
        w_alr = region(reg_g, 2560, C, 16)
        w_alr16 = reg_g[:, 3968:4096].bitcast(F16).rearrange("p (k c n) -> p k c n", k=2, c=C)
        trig = region(reg_g, 2688, 3, T)
        lnz = region(reg_g, 3456, TT, T)
        gates = region(reg_g, 0, 2 * C, T)
        xP = region(reg_g, 0, NH, TT, M)
        xPT = region(reg_g, 2048, NH, 2, T)
        oneh = region(reg_g, 0, 2 * TT * TOPK, E)
        selG = region(reg_g, 0, TT, EG, 2, SLOTS)
        selT = region(reg_g, 1024, EG, TT, P)
        g_sb = region(reg_g, 2048, C, SLOTS)
        sg_sb = region(reg_g, 2560, C, SLOTS)
        l_sb = region(reg_g, 3072, C, SLOTS)
        actT = region(reg_g, 3584, C, SLOTS)
        ogT = parts(reg_o, 0, 4)
        odT = parts(reg_o, 1024, 4)
        oxT = parts(reg_o, 0, 4)
        gateT = region(reg_o, 1024, T)
        qg = region(reg_l, 0, 2, T)
        kg = region(reg_l, 512, 2, T)
        vg = region(reg_l, 1024, TT, GH * P)
        qS = region(reg_l, 2048, 2, T)
        qX = region(reg_l, 2560, 2, P)
        kX = region(reg_l, 2816, 2, P)
        xq = region(reg_l, 0, NH, T)
        xk = region(reg_l, 1024, NH, M)
        xv = region(reg_l, 2048, TT, NH * DH)
        b_dn = region(reg_l, 0, D)
        gfin = region(reg_l, 1024, D)
        rows = region(reg_l, 0, P)
        pos_i = region(reg_l, 512, T).bitcast(I32)
        invf = region(reg_l, 768, 1)
        diff_i = region(reg_l, 1024, P).bitcast(I32)
        mod_i = region(reg_l, 1152, P).bitcast(I32)
        mod_f = region(reg_l, 1280, P)
        idx_u = region(reg_l, 2048, TT, 8).bitcast(U32)
        idx_f = region(reg_l, 2064, TT, TOPK)
        top = region(reg_l, 2080, TT, 8)
        g4 = region(reg_l, 2096, TT, TOPK)
        logit = region(reg_l, 2112, TT, E)
        totals = region(reg_l, 2176, E)

        pt = [ctx.enter_context(nc.psum_tensor(f"bank{b}", [P, 512], F32)) for b in range(BANKS)]

        ld_x = [sem(f"ld_x{t}") for t in range(TT)]
        ld_mem, ld_rows, ld_small, ld_alr, ld_route, ld_late, ld_brows, consts = (sem(n) for n in
            ("ld_mem", "ld_rows", "ld_small", "ld_alr", "ld_route", "ld_late", "ld_brows", "consts"))
        half_ld = [sem(f"half_ld{s}") for s in range(EARLY)]
        w_high, w_low = sem("w_high"), sem("w_low")
        f_high, f_low = sem("f_high"), sem("f_low")
        x_high = sem("x_high")
        alr_cut = sem("alr_cut")
        late_ld = [sem(f"late_ld{s}") for s in range(NSLOT)]
        gu_used, dn_used = sem("gu_used"), sem("dn_used")
        full = [sem(f"full{b}") for b in range(BANKS)]
        free = [sem(f"free{b}") for b in range(BANKS)]
        dve_chain, act_chain, pool_chain = sem("dve_chain"), sem("act_chain"), sem("pool_chain")
        norm_ss, norm_xn = sem("norm_ss"), sem("norm_xn")
        trig_in, trig_out = sem("trig_in"), sem("trig_out")
        mod_ready, masks_ready = sem("mod_ready"), sem("masks_ready")
        th_r, ln_ready, anchors, gla_exp, gla_qk, go_ss = (sem(n) for n in
            ("th_r", "ln_ready", "anchors", "gla_exp", "gla_qk", "go_ss"))
        s_ready, s_exp, s_prob, merged_sum, merged_ready = (sem(n) for n in
            ("s_ready", "s_exp", "s_prob", "merged_sum", "merged_ready"))
        xs_max, xs_exp, xs_prob = sem("xs_max"), sem("xs_exp"), sem("xs_prob")
        top_ready, top_exp, gate_ready, over_ready = (sem(n) for n in
            ("top_ready", "top_exp", "gate_ready", "over_ready"))
        sel_ready, selG_ready, gathered, xg_act, xg_dve, selT_full, selT_act, selT_dve = (sem(n) for n in
            ("sel_ready", "selG_ready", "gathered", "xg_act", "xg_dve", "selT_full", "selT_act", "selT_dve"))
        h_full, hs_act, hs_dve, T_full, g_ready, sg_ready, act_ready, y_full, y_ready, moe_chain = (sem(n) for n in
            ("h_full", "hs_act", "hs_dve", "T_full", "g_ready", "sg_ready", "act_ready", "y_full", "y_ready",
             "moe_chain"))
        root_asked, root_done = sem("root_asked"), sem("root_done")
        lin_chain, round_chain = sem("lin_chain"), sem("round_chain")
        acc_full, fin_ss, fin_ready, stored = sem("acc_full"), sem("fin_ss"), sem("fin_ready"), sem("stored")

        def take(eng, name):
            eng.wait_ge(full[BANK[name]], TURN[name] + 1)
            return pt[BANK[name]]

        def emptied(eng, name):
            eng.wait_ge(free[BANK[name]], TURN[name] + 1)

        def chain(eng, s):
            count = [0]

            def link(ins):
                count[0] += 1
                ins.then_inc(s, 1)
                eng.wait_ge(s, count[0])
            return link

        def bc(ap, n):
            return ap.unsqueeze(2).to_broadcast([ap.shape[0], ap.shape[1], n])

        def mid(ap, n):
            return ap.unsqueeze(1).to_broadcast([ap.shape[0], n, ap.shape[1]])

        OFF_QG, OFF_VG, OFF_RG, OFF_AL, OFF_QD = 0, 512, 1024, 1536, 1552
        w_in = A["w_in"][0].rearrange("(c p) n -> p c n", p=P)
        w_gate_br = A["w_branch_gate"][0].rearrange("(c p) n -> p c n", p=P)
        w_xkv = A["w_xkv"][0].rearrange("(c p) n -> p c n", p=P)
        dense = {k: A[n][0].rearrange("(c p) n -> p c n", p=P) for k, n in
                 (("gla", "w_branch_gla"), ("dil", "w_branch_dil"), ("mix", "w_mix_out"), ("xq", "w_xq"),
                  ("xo", "w_xo"))}
        SRC = {"q_g": w_in[:, :, OFF_QG:OFF_QG + 256], "k_g": w_in[:, :, OFF_QG + 256:OFF_VG]}
        for a in range(2):
            SRC[f"v_g{a}"] = w_in[:, :, OFF_VG + a * 256:OFF_VG + (a + 1) * 256]
            SRC[f"r_g{a}"] = w_in[:, :, OFF_RG + a * 256:OFF_RG + (a + 1) * 256]
            for g in range(NG):
                for i, k in enumerate(("q_d", "k_d", "v_d")):
                    o = OFF_QD + (i * NG + g) * 512 + a * 256
                    SRC[f"{k}{g}{a}"] = w_in[:, :, o:o + 256]
            SRC[f"xk{a}"] = w_xkv[:, :, a * 256:(a + 1) * 256]
            SRC[f"xv{a}"] = w_xkv[:, :, 512 + a * 256:512 + (a + 1) * 256]
            for k, n in (("gla", 512), ("dil", 512), ("xo", 512), ("xq", 256)):
                SRC[f"{k}{a}"] = dense[k][:, :, a * n:(a + 1) * n]
        for q in range(4):
            SRC[f"mix{q}"] = dense["mix"][:, :, q * 256:(q + 1) * 256]
        for q in range(8):
            SRC[f"eg{q}"] = w_gate_br[:, :, q * 256:(q + 1) * 256]

        def slot_of(v):
            return (v + 2 * EARLY) % NSLOT

        block = ctx.enter_context(nc.Block())

        def expert_groups(eng, body, decide=None):
            with eng.Fori(0, GROUPS) as n:
                body(n, n)
            if decide:
                decide()
            eng.wait_ge(over_ready, 1)
            more = eng.value_load(over[0:1, 0:1], min_val=0, max_val=1)
            with eng.If(more > 0):
                with eng.Fori(1, ROUNDS) as r:
                    if eng.engine == nc.vector.engine:
                        next_round(eng, r)
                    with eng.Fori(0, GROUPS) as n:
                        body(n, r * GROUPS + n)
                eng.nop()

        @block.sync
        def _(sp):
            xt_src = A["x"][0].rearrange("(t p) d -> p t d", p=P)
            for t in range(TT):
                sp.dma_start(h[:, t, :], xt_src[:, t, :]).then_inc(ld_x[t], 16)

            mats = [A[k][0].rearrange("e (p c) n -> e p (c n)", c=C) for k in ("w_gate", "w_up", "w_down")]
            ORDER = [(m, q) for q in range(4) for m in (0, 1)] + [(2, q) for q in range(4)]
            UPE = len(ORDER)

            def load(v, e):
                m, q = ORDER[v % UPE]
                s = slot_of(v)
                src = mats[m][bass.ds(e, 1), :, q * UNIT:(q + 1) * UNIT]
                sp.dma_start(slot[s], src.rearrange("e p n -> p (e n)")).then_inc(late_ld[s], 16)

            def slot_left(v, e0):
                m, q = ORDER[(v - NSLOT) % UPE]
                e = (v - NSLOT) // UPE
                if q < 3:
                    sp.wait_ge(dn_used if m == 2 else gu_used, 3 * e0 + (3 * e + q + 1))
                else:
                    sp.wait_ge(y_full if m == 2 else h_full, e0 + (e + 1))

            first = [0]

            def first_units(n):
                for v in range(first[0], first[0] + n):
                    i = slot_of(v)
                    if v == 0:
                        take(sp, "pv1")
                    elif v >= NSLOT:
                        slot_left(v, 0)
                    elif i < 2 * EARLY:
                        u = max(u for u in range(len(HALVES)) if u % EARLY == i % EARLY)
                        if i < EARLY:
                            sp.wait_ge(w_low, u + 1)
                        else:
                            take(sp, LAST_FILL[HALVES[u]])
                    load(v, v // UPE)
                first[0] += n

            for u, name in enumerate(HALVES):
                if u == 1:
                    sp.wait_ge(ld_rows, 16 * 5)
                if u >= EARLY:
                    sp.wait_ge(w_low, u - EARLY + 1)
                sp.dma_start(raw[u % EARLY].rearrange("p (c n) -> p c n", n=SRC[name].shape[2]), SRC[name])\
                    .then_inc(half_ld[u % EARLY], 16)
                if u >= HALVES.index("mix0"):
                    first_units(1)
            per = UPE * EG
            first_units(per - first[0])

            def body(n, k):
                for v in range(per):
                    slot_left(v, k * EG)
                    load(v, n * EG + v // UPE)

            with sp.Fori(1, GROUPS) as n:
                body(n, n)
            sp.wait_ge(over_ready, 1)
            more = sp.value_load(over[0:1, 0:1], min_val=0, max_val=1)
            with sp.If(more > 0):
                with sp.Fori(1, ROUNDS) as r:
                    with sp.Fori(0, GROUPS) as n:
                        body(n, r * GROUPS + n)
                sp.nop()
            for t in range(TT):
                for i in range(2):
                    sp.wait_ge(fin_ready, 2 * t + i + 1)
                    sp.dma_start(out[0, t * P:(t + 1) * P, i * 512:(i + 1) * 512], out_sb[:, t, i * 512:(i + 1) * 512])\
                        .then_inc(stored, 16)
            sp.wait_ge(stored, 16 * 2 * TT)

        @block.gpsimd
        def _(pool):
            link = chain(pool, pool_chain)
            roots = [0]

            def root(a, b):
                roots[0] += 1
                pool.wait_ge(root_asked, roots[0])
                pool.tensor_tensor(st[:, a:b], st[:, a:b], neg_half[:, 0:b - a], ALU.pow).then_inc(root_done, 1)

            link(pool.memset(ident[:], 0.0))
            pool.affine_select(out=ident[:], in_=ident[:], compare_op=ALU.not_equal, fill=1.0, base=0,
                               pattern=[[-1, P]], channel_multiplier=1).then_inc(consts, 1)
            link(pool.memset(neg_half[:], -0.5))
            pool.dma_start(w2[0:16, :], A["w_gla_a2"][0]).then_inc(ld_small, 16)
            pool.dma_start(w2[16:17, :], A["b_gla_a2"]).then_inc(ld_small, 16)
            pool.dma_start(invf, A["inv_freq"]).then_inc(ld_small, 16)
            pool.dma_start(pos_i, A["positions"].to_broadcast([P, T])).then_inc(ld_small, 16)
            pool.dma_start(w_alr, w_in[:, :, OFF_AL:OFF_AL + 16]).then_inc(ld_alr, 16)
            root(0, 2)
            link(pool.memset(tri16[:], 1.0 / 16))
            pool.affine_select(out=tri16[:], in_=tri16[:], compare_op=ALU.is_ge, fill=0.0, base=0,
                               pattern=[[1, P]], channel_multiplier=-1).then_inc(consts, 1)
            link(pool.memset(tri_s[:], 1.0))
            pool.affine_select(out=tri_s[:], in_=tri_s[:], compare_op=ALU.is_gt, fill=0.0, base=0,
                               pattern=[[1, P]], channel_multiplier=-1).then_inc(consts, 1)
            pool.memset(ones[:], 1.0).then_inc(consts, 1)
            pool.memset(alr[0:32, :], 1.0).then_inc(consts, 1)
            pool.memset(kS, 0.0).then_inc(consts, 1)
            pool.iota(iota_s[:], pattern=[[1, SLOTS]], base=0, channel_multiplier=0,
                      allow_small_or_imprecise_dtypes=True).then_inc(consts, 1)
            pool.iota(iota_e[:], pattern=[[1, E]], base=0, channel_multiplier=0,
                      allow_small_or_imprecise_dtypes=True).then_inc(consts, 1)
            pool.iota(diff_i, pattern=[[1, P]], base=T, channel_multiplier=-1).then_inc(consts, 1)
            for i, k in enumerate(("b_gate", "b_up")):
                pool.dma_start(brows[0:E, i, :], A[k][0]).then_inc(ld_brows, 16)
            pool.dma_start(memx, A["mem"][0].rearrange("(t p) d -> p t d", p=P)).then_inc(ld_mem, 16)
            pool.dma_start(w_rt[:], A["w_router"][0].rearrange("(p c) e -> p c e", c=C)).then_inc(ld_route, 16)
            pool.dma_start(b_rt[:], A["b_router"]).then_inc(ld_route, 16)
            pool.dma_start(g3[:], A["norm3_g"][0].rearrange("(p c) -> p c", c=C)).then_inc(ld_route, 16)
            link(pool.memset(masks[:, 0:2, :], 0.0))
            pool.affine_select(out=masks[:, 0, :], in_=masks[:, 0, :], compare_op=ALU.is_ge, fill=NEG, base=0,
                               pattern=[[1, P]], channel_multiplier=-1).then_inc(masks_ready, 1)
            pool.wait_ge(mod_ready, 1)
            for m in (1, 3, 5):
                pool.affine_select(out=masks[:, m, :], in_=masks[:, m, :], compare_op=ALU.is_ge, fill=NEG,
                                   base=0, pattern=[[-1, P]], channel_multiplier=1).then_inc(masks_ready, 1)
            root(2, 4)
            root(8, 12)
            root(12, 16)
            root(4, 6)
            take(pool, "xo11")
            pool.dma_start(b_dn[0:E, :], A["b_down"][0]).then_inc(ld_late, 16)
            pool.dma_start(gfin, A["final_norm_g"].rearrange("(a n) -> a n", a=1).to_broadcast([P, D]))\
                .then_inc(ld_late, 16)
            root(6, 8)
            pool.wait_ge(ld_late, 16 * 2)
            root(56, 57)
            root(58, 59)

        @block.scalar
        def _(act):
            link = chain(act, act_chain)
            for name, at_row, n in (("norm1_g", 0, 8), ("mem_norm_g", 8, 8), ("norm2_g", 16, 8),
                                    ("gla_norm_g", 24, 4), ("b_branch_gate", 28, 16)):
                act.dma_start(rows[at_row:at_row + n, :],
                              A[name][0].rearrange("(c p) -> c p", p=P)).then_inc(ld_rows, 16)

            def copy(dst, src):
                return act.activation(dst, src, ACT.Copy)

            def unscaled(dst, src):
                return act.activation(dst, src, ACT.Copy, scale=1 / WS)

            def free_bank(name):
                return free[BANK[name]]

            halves = [0]

            def cut_ahead(name, ahead=2):
                while halves[0] < min(HALVES.index(name) + ahead + 1, len(HALVES)):
                    u = halves[0]
                    halves[0] += 1
                    act.wait_ge(half_ld[u % EARLY], 16 * (u // EARLY + 1))
                    if u >= EARLY:
                        take(act, LAST_FILL[HALVES[u - EARLY]])
                    if HALVES[u][:3] in ("q_d", "k_d"):
                        for i in range(2):
                            dst, src = rotary_cut(u, 0, i)
                            ins = act.activation(dst, src, ACT.Copy, scale=WS)
                    else:
                        ins = act.activation(cut[u % EARLY][:, 0, :], raw[u % EARLY], ACT.Copy, scale=WS)
                    ins.then_inc(w_high, 1)

            def high(dst, src, scale):
                act.activation(dst, src, ACT.Copy, scale=scale).then_inc(x_high, 1)

            def high_T(prefix, q, dst, gain):
                b = take(act, f"{prefix}{q}")
                for i in range(2):
                    high(dst[:, 0, 2 * q + i, :], b[:, i * T:(i + 1) * T], gain[:, 2 * q + i:2 * q + i + 1])

            def squares(norm, src, junk, t, part, n):
                act.activation(junk[:, t, part * n:(part + 1) * n], src[:, t, part * n:(part + 1) * n], ACT.Square,
                               accum_out=ssq[:, norm, t, part:part + 1]).then_inc(norm_ss, 1)

            for t in range(TT):
                act.wait_ge(ld_x[t], 16)
                squares(0, h, xn, t, 0, D)
            cut_ahead("q_g", 0)
            emptied(act, "vec")
            for q in range(4):
                high_T("x_T", q, aT, vT[:, 0:8])
            act.wait_ge(ld_alr, 16)
            act.activation(w_alr16[:, 0], w_alr, ACT.Copy, scale=WS).then_inc(alr_cut, 1)
            cut_ahead("q_g")
            for i in range(2):
                act.wait_ge(trig_in, i + 1)
                act.activation(cs[:, i, :], trig[:, 2, :], ACT.Sin).then_inc(trig_out, 1)
            for name, dst in (("q_g", qg), ("k_g", kg)):
                cut_ahead(name)
                b = take(act, name)
                if name == "q_g":
                    act.wait_ge(trig_in, 2)
                unscaled(dst.rearrange("p a b -> p (a b)"), b[:]).then_inc(free_bank(name), 1)
            b = take(act, "alr")
            act.wait_ge(consts, 9)
            act.activation(alr[0:16, :], b[0:16, 0:T], ACT.Copy, scale=1 / WS).then_inc(free_bank("alr"), 1)
            act.wait_ge(masks_ready, 1)
            act.wait_ge(mod_ready, 1)
            def two_tiles(b):
                return b[:].rearrange("p (t n) -> p t n", t=TT)

            for a in range(2):
                cut_ahead(f"v_g{a}")
                b = take(act, f"v_g{a}")
                unscaled(vg[:, :, a * 256:(a + 1) * 256], two_tiles(b)).then_inc(free_bank(f"v_g{a}"), 1)
            for a in range(2):
                cut_ahead(f"r_g{a}")
                b = take(act, f"r_g{a}")
                act.activation(sr[:, :, a * 256:(a + 1) * 256], two_tiles(b), ACT.Tanh, scale=0.5 / WS)\
                    .then_inc(th_r, 1)
            b = take(act, "lg")
            link(act.activation(lnz.rearrange("p a b -> p (a b)"), b[:], ACT.Abs))
            link(act.activation(lnz, lnz, ACT.Exp, scale=-1.0))
            act.activation(lnz, lnz, ACT.Ln, bias=1.0).then_inc(ln_ready, 1)
            for g in range(NG):
                for a in range(2):
                    cut_ahead(f"q_d{g}{a}")
            b = take(act, "cum")
            copy(B.rearrange("p a b -> p (a b)"), b[:]).then_inc(free_bank("cum"), 1)
            act.wait_ge(anchors, 1)
            for fc in range(2):
                for t in range(TT):
                    if not (fc and t):
                        cut_ahead(f"k_d{fc}{t}")
                    for i in range(NSUB):
                        a0 = t * P + i * SUB
                        act.activation(qS[:, fc, a0:a0 + SUB], B[:, fc, a0:a0 + SUB], ACT.Exp,
                                       bias=st[:, 16 + fc * 8 + t * 4 + i:17 + fc * 8 + t * 4 + i])
                        act.activation(kS[:, fc, t, i, 0:(i + 1) * SUB], B[:, fc, t * P:t * P + (i + 1) * SUB],
                                       ACT.Exp, scale=-1.0, bias=B[:, fc, a0 + SUB // 2:a0 + SUB // 2 + 1])
                act.activation(kX[:, fc, :], B[:, fc, 0:P], ACT.Exp, scale=-1.0, bias=B[:, fc, P - 1:P])
            act.activation(qX, B[:, :, P:T], ACT.Exp).then_inc(gla_exp, 1)
            act.wait_ge(ld_mem, 16)
            for t, name in enumerate(("k_d11", "k_d20")):
                cut_ahead(name)
                squares(1, memx, xn, t, 0, D)
            cut_ahead("k_d21")
            for g in range(NG):
                for a in range(2):
                    cut_ahead(f"v_d{g}{a}")
                    b = take(act, f"v_d{g}{a}")
                    o = g * 512 + a * 256
                    unscaled(vd[:, :, o:o + 256], two_tiles(b)).then_inc(free_bank(f"v_d{g}{a}"), 1)
                if g == 1:
                    for q in range(4):
                        high_T("m_T", q, memT, vT[:, 8:16])
            for t in range(TT):
                b = take(act, f"go{t}")
                for hd in range(GH):
                    act.activation(og[:, t, hd * P:(hd + 1) * P], b[:, hd * P:(hd + 1) * P], ACT.Square,
                                   accum_out=st[:, 8 + t * 4 + hd:9 + t * 4 + hd]).then_inc(go_ss, 1)

            def softmax_exp(hd):
                act.wait_ge(s_ready, hd + 1)
                for t, (c0, c1) in enumerate(((0, 3 * P), (3 * P, 9 * P))):
                    act.activation(S[:, hd % 2, c0:c1], S[:, hd % 2, c0:c1], ACT.Exp, scale=ATT_SCALE,
                                   bias=st[:, 36 + 2 * (hd % 2) + t:37 + 2 * (hd % 2) + t],
                                   accum_out=st[:, 40 + 2 * (hd % 2) + t:41 + 2 * (hd % 2) + t]).then_inc(s_exp, 1)

            def probs_T(hd):
                for g in range(2):
                    b = take(act, f"pt{hd}{g}")
                    copy(PT[:, hd % 2, g, :], b[:, 0:3 * P]).then_inc(free_bank(f"pt{hd}{g}"), 1)

            def branch_gates(q):
                cut_ahead(f"eg{q}")
                b = take(act, f"eg{q}")
                for i in range(2):
                    c = 2 * q + i
                    ins = act.activation(gates[:, c, :], b[:, i * T:(i + 1) * T], ACT.Tanh, scale=0.5 / WS,
                                         bias=vT[:, 28 + c:29 + c])
                ins.then_inc(free_bank(f"eg{q}"), 1)

            def out_T(a):
                b = take(act, f"pv{a}")
                high(odT[:, 0, 2 * a:2 * a + 2, :].rearrange("p a b -> p (a b)"), b[:], 1.0)

            for hd in range(NH):
                softmax_exp(hd)
                branch_gates(2 * hd)
                branch_gates(2 * hd + 1)
                if hd == 0:
                    for q in range(2):
                        high_T("gt", q, ogT, vT[:, 24:28])
                else:
                    probs_T(hd - 1)
                if hd == 2:
                    out_T(0)
            def x_keys(a):
                cut_ahead(f"xk{a}")
                b = take(act, f"xk{a}")
                unscaled(xk[:, 2 * a:2 * a + 2, :].rearrange("p a b -> p (a b)"), b[:])\
                    .then_inc(free_bank(f"xk{a}"), 1)

            x_keys(0)
            probs_T(3)
            out_T(1)
            for q in range(4):
                if q % 2 == 0:
                    cut_ahead(f"dil{q // 2}")
                act.wait_ge(merged_sum, q + 1)
                high(mergedT[:, 0, 2 * q:2 * q + 2, :].rearrange("p a b -> p (a b)"),
                     gates[:, 2 * q:2 * q + 2, :].rearrange("p a b -> p (a b)"), 0.5 / WS)
            x_keys(1)
            for q in range(4):
                cut_ahead(f"mix{q}")
                emptied(act, f"mix{q}")
                for t in range(TT):
                    squares(2, h, xn, t, q, 256)

            cut_ahead("xv0")
            b = take(act, "xv0")
            unscaled(xv[:, :, 0:256], two_tiles(b)).then_inc(free_bank("xv0"), 1)
            for q in range(4):
                high_T("c_T", q, aT, vT[:, 16:24])
            cut_ahead("xv1")

            def x_values(t):
                b = take(act, f"xv1{t}")
                unscaled(xv[:, t, 256:512], b[:, 0:256]).then_inc(free_bank(f"xv1{t}"), 1)

            def x_queries(a):
                b = take(act, f"xq{a}")
                unscaled(xq[:, 2 * a:2 * a + 2, :].rearrange("p a b -> p (a b)"), b[:])\
                    .then_inc(free_bank(f"xq{a}"), 1)

            x_values(0)
            x_queries(0)
            x_values(1)
            cut_ahead("xq1")
            x_queries(1)

            def x_exp(hd):
                act.wait_ge(xs_max, hd + 1)
                b = pt[BANK[f"xs{hd}"]]
                for t in range(TT):
                    act.activation(xP[:, hd, t, :], b[:, t * M:(t + 1) * M], ACT.Exp, scale=ATT_SCALE,
                                   bias=st[:, 44 + 2 * (hd % 2) + t:45 + 2 * (hd % 2) + t],
                                   accum_out=st[:, 48 + 2 * (hd % 2) + t:49 + 2 * (hd % 2) + t])\
                        .then_inc(xs_exp if t == 0 else free_bank(f"xs{hd}"), 1)

            def x_probs_T(hd):
                b = take(act, f"xt{hd}")
                copy(xPT[:, hd].rearrange("p a b -> p (a b)"), b[:]).then_inc(free_bank(f"xt{hd}"), 1)

            def x_out_T(a):
                b = take(act, f"xpv{a}")
                high(oxT[:, 0, 2 * a:2 * a + 2, :].rearrange("p a b -> p (a b)"), b[:], 1.0)

            x_exp(0)
            x_exp(1)
            x_probs_T(0)
            x_exp(2)
            x_probs_T(1)
            x_exp(3)
            x_probs_T(2)
            x_out_T(0)
            x_probs_T(3)
            x_out_T(1)
            for n in range(2):
                for t in range(TT):
                    emptied(act, f"xo{n}{t}")
                    squares(3, h, xn, t, n, 512)
            act.wait_ge(ld_route, 48)
            for q in (0, 2):
                b = take(act, f"f_T{q}")
                for i in range(2):
                    c = 2 * q + i
                    ins = act.activation(fT[:, c, :], b[:, i * T:(i + 1) * T], ACT.Copy, scale=g3[:, c:c + 1])
                ins.then_inc(free_bank(f"f_T{q}"), 1)
            for t in range(TT):
                copy(f16[:, 0, t], f[:, t]).then_inc(f_high, 1)
            act.wait_ge(top_ready, 1)
            for t in range(TT):
                act.activation(g4[:, t, :], top[:, t, 0:TOPK], ACT.Exp, bias=st[:, 52 + t:53 + t],
                               accum_out=st[:, 54 + t:55 + t]).then_inc(top_exp, 1)

            b = take(act, "all")
            copy(totals, b[:, 0:E]).then_inc(free_bank("all"), 1)
            b = take(act, "gT")
            copy(gateT[0:E, :], b[0:E, 0:T]).then_inc(free_bank("gT"), 1)

            def body(n, k):
                for q in (0, 2):
                    act.wait_ge(gathered, 4 * k + (q + 1))
                    for i in range(2):
                        c = 2 * q + i
                        ins = act.activation(xg[:, c, :], pt[2][:, i * T:(i + 1) * T], ACT.Copy,
                                             scale=g3[:, c:c + 1])
                    ins.then_inc(xg_act, 1)
                for j in range(EG):
                    act.wait_ge(h_full, k * EG + (j + 1))
                    copy(hs[:, :, 0:64], pt[0][:].rearrange("p (q c) -> p c q", c=C)).then_inc(hs_act, 1)
                    if j == 0:
                        act.wait_ge(selT_full, 2 * k + 1)
                        copy(selT[:, 0:2].rearrange("p e t s -> p (e t s)"), pt[2][:]).then_inc(selT_act, 1)
                    for i in range(2):
                        act.wait_ge(g_ready, k * 2 * EG + (2 * j + i + 1))
                        act.activation(sg_sb[:, 4 * i:4 * i + 4, :], g_sb[:, 4 * i:4 * i + 4, :], ACT.Sigmoid,
                                       scale=ALPHA).then_inc(sg_ready, 1)
                    act.wait_ge(y_full, k * EG + (j + 1))
                    copy(y, pt[2][:]).then_inc(y_ready, 1)

            expert_groups(act, body)

            for t in range(TT):
                for i in range(2):
                    act.wait_ge(acc_full, 2 * t + i + 1)
                    act.activation(out_sb[:, t, i * 512:(i + 1) * 512], pt[4 + 2 * t + i][:], ACT.Square,
                                   accum_out=st[:, 56 + 2 * t + i:57 + 2 * t + i]).then_inc(fin_ss, 1)

        LINKS = 3 * 2 * EG

        def next_round(dve, r):
            dve.wait_ge(round_chain, r)
            dve.tensor_scalar(place, place, -float(SLOTS), None, ALU.add).then_inc(round_chain, 1)
            dve.wait_ge(round_chain, r + 1)
            dve.memset(st[:, 62:63], 0.0)

        @block.vector
        def _(dve):
            link = chain(dve, dve_chain)

            roots = [0]

            def rsqrt_mean(dst, src, n):
                dve.tensor_scalar(dst, src, 1.0 / n, EPS, ALU.mult, ALU.add).then_inc(root_asked, 1)
                roots[0] += 1
                dve.wait_ge(root_done, roots[0])

            def free_bank(name):
                return free[BANK[name]]

            squared, halves, highs = [0], [0], [0]

            def cut_ahead(name, ahead=2):
                while halves[0] < min(HALVES.index(name) + ahead + 1, len(HALVES)):
                    u = halves[0]
                    halves[0] += 1
                    dve.wait_ge(w_high, u + 1)
                    if HALVES[u][:3] in ("q_d", "k_d"):
                        for i in range(2):
                            dst, src = rotary_cut(u, 1, i)
                            ins = dve.scalar_tensor_tensor(dst, src, WS, rotary_cut(u, 0, i)[0],
                                                           ALU.mult, ALU.subtract)
                    else:
                        ins = dve.scalar_tensor_tensor(cut[u % EARLY][:, 1, :], raw[u % EARLY], WS,
                                                       cut[u % EARLY][:, 0, :], ALU.mult, ALU.subtract)
                    ins.then_inc(w_low, 1)

            def low(dst, src, scale, hi):
                highs[0] += 1
                dve.wait_ge(x_high, highs[0])
                return dve.scalar_tensor_tensor(dst, src, scale, hi, ALU.mult, ALU.subtract)

            def low_T(prefix, q, dst, gain):
                b = take(dve, f"{prefix}{q}")
                highs[0] += 1
                for i in range(2):
                    c = 2 * q + i
                    highs[0] -= i
                    ins = low(dst[:, 1, c, :], b[:, i * T:(i + 1) * T], gain[:, c:c + 1], dst[:, 0, c, :])
                ins.then_inc(free_bank(f"{prefix}{q}"), 1)

            def normed(norm, nparts, src, dst, at):
                squared[0] += TT * nparts
                dve.wait_ge(norm_ss, squared[0])
                if nparts == 1:
                    rsqrt_mean(st[:, at:at + 2], ssq[:, norm, :, 0], D)
                else:
                    link(dve.reduce_sum(st[:, at:at + 2], ssq[:, norm, :, 0:nparts], AX))
                    rsqrt_mean(st[:, at:at + 2], st[:, at:at + 2], D)
                for t in range(TT):
                    dve.tensor_scalar(dst(t), src(t), st[:, at + t:at + t + 1], None, ALU.mult)\
                        .then_inc(norm_xn, 1)

            normed(0, 1, lambda t: h[:, t, :], lambda t: xn[:, t, :], 0)
            b = take(dve, "vec")
            dve.tensor_copy(vT[:, 0:24], b[:, 0:24])
            dve.tensor_scalar(vT[:, 24:28], b[:, 24:28], 0.5 / WS, None, ALU.mult)
            dve.tensor_scalar(vT[:, 28:44], b[:, 28:44], 0.5, None, ALU.mult).then_inc(free_bank("vec"), 1)
            emptied(dve, "vec")
            cut_ahead("q_g", 0)
            for q in range(4):
                low_T("x_T", q, aT, vT[:, 0:8])
            dve.wait_ge(alr_cut, 1)
            dve.scalar_tensor_tensor(w_alr16[:, 1], w_alr, WS, w_alr16[:, 0], ALU.mult, ALU.subtract)\
                .then_inc(alr_cut, 1)
            cut_ahead("q_g")
            dve.wait_ge(ld_small, 16 * 4)
            link(dve.tensor_copy(trig[:, 1, :], pos_i))
            link(dve.tensor_scalar(trig[:, 0, :], trig[:, 1, :], invf, None, ALU.mult))
            for i, phase in enumerate((np.pi / 2, 0.0)):
                link(dve.tensor_scalar(trig[:, 1, :], trig[:, 0, :], float(0.5 / np.pi), float(phase * 0.5 / np.pi),
                                       ALU.mult, ALU.add))
                link(dve.tensor_scalar(trig[:, 1, :], trig[:, 1, :], MAGIC, None, ALU.add))
                link(dve.tensor_scalar(trig[:, 1, :], trig[:, 1, :], -MAGIC, None, ALU.add))
                if i:
                    dve.wait_ge(trig_out, 1)
                link(dve.scalar_tensor_tensor(trig[:, 2, :], trig[:, 1, :], -TWO_PI_HI, trig[:, 0, :],
                                              ALU.mult, ALU.add))
                link(dve.scalar_tensor_tensor(trig[:, 2, :], trig[:, 1, :], -float(TWO_PI_LO), trig[:, 2, :],
                                              ALU.mult, ALU.add))
                link(dve.tensor_scalar(trig[:, 2, :], trig[:, 2, :], float(phase), 3.1415925, ALU.add, ALU.min))
                dve.tensor_scalar(trig[:, 2, :], trig[:, 2, :], -3.1415925, None, ALU.max).then_inc(trig_in, 1)
            cut_ahead("k_g")
            dve.wait_ge(consts, 9)
            dve.wait_ge(masks_ready, 1)
            for m, d in ((2, 4), (4, 16)):
                link(dve.tensor_scalar(mod_i, diff_i, d - 1, None, ALU.bitwise_and))
                link(dve.tensor_copy(mod_f, mod_i))
                link(dve.tensor_scalar(mod_f, mod_f, 0.0, -NEG, ALU.is_equal, ALU.mult))
                link(dve.tensor_scalar(masks[:, m, :], mod_f, NEG, None, ALU.add))
                ins = dve.tensor_copy(masks[:, m + 1, :], masks[:, m, :])
            ins.then_inc(mod_ready, 1)
            for a in range(2):
                cut_ahead(f"v_g{a}")
            for a in range(2):
                cut_ahead(f"r_g{a}")
                b = take(dve, f"r_g{a}")
                dve.wait_ge(th_r, a + 1)
                v = sr[:, :, a * 256:(a + 1) * 256]
                dve.scalar_tensor_tensor(v, v, 1.0, b[:].rearrange("p (t n) -> p t n", t=TT), ALU.add, ALU.mult)\
                    .then_inc(free_bank(f"r_g{a}"), 1)
            b = take(dve, "lg")
            dve.wait_ge(ln_ready, 1)
            dve.scalar_tensor_tensor(la.rearrange("p a b -> p (a b)"), b[:], 0.0,
                                     lnz.rearrange("p a b -> p (a b)"), ALU.min, ALU.subtract)\
                .then_inc(free_bank("lg"), 1)

            def rotary(name, dst, before):
                if before:
                    emptied(dve, before)
                cut_ahead(name)
                b = take(dve, name)
                ps = b[:].rearrange("p (a b) -> p a b", a=2)
                dve.tensor_tensor(rot[:, 0], ps, mid(cs[:, 0, :], 2), ALU.mult)
                link(dve.tensor_tensor(rot[:, 1], ps, mid(cs[:, 1, :], 2), ALU.mult))
                dve.tensor_tensor(dst[:, 0, :], rot[:, 0, 0, :], rot[:, 1, 1, :], ALU.subtract)
                dve.tensor_tensor(dst[:, 1, :], rot[:, 0, 1, :], rot[:, 1, 0, :], ALU.add)\
                    .then_inc(free_bank(name), 1)

            dve.wait_ge(trig_out, 2)
            link(dve.tensor_scalar(cs, cs, 1 / WS, None, ALU.mult))
            before = None
            for g in range(NG):
                for a in range(2):
                    rotary(f"q_d{g}{a}", qr[:, 2 * g + a], before)
                    before = f"q_d{g}{a}"
            b = take(dve, "bias")
            dve.tensor_copy(bT[:].rearrange("p a c e -> p (a c e)"), b[:]).then_inc(free_bank("bias"), 1)
            emptied(dve, "cum")
            dve.tensor_scalar(st[:, 16:32].rearrange("p (f i) -> p f i", f=2),
                              B[:, :, SUB // 2::SUB], -1.0, None, ALU.mult).then_inc(anchors, 1)
            def rotary_keys(g, before):
                for a in range(2):
                    rotary(f"k_d{g}{a}", kr[:, 2 * g + a], before)
                    before = f"k_d{g}{a}"
                return before

            before = rotary_keys(0, before)
            before = rotary_keys(1, before)
            dve.wait_ge(gla_exp, 1)
            emptied(dve, "q_g")
            emptied(dve, "k_g")
            dve.scalar_tensor_tensor(qS, qS, 16 * GLA_SCALE, qg, ALU.mult, ALU.mult)
            dve.scalar_tensor_tensor(qX, qX, GLA_SCALE, qg[:, :, P:T], ALU.mult, ALU.mult)
            dve.tensor_tensor(kX, kX, kg[:, :, 0:P], ALU.mult)
            for t in range(TT):
                for i in range(NSUB):
                    n = (i + 1) * SUB
                    ins = dve.tensor_tensor(kS[:, :, t, i, 0:n], kS[:, :, t, i, 0:n], kg[:, :, t * P:t * P + n],
                                            ALU.mult)
            ins.then_inc(gla_qk, 1)
            rotary_keys(2, before)
            normed(1, 1, lambda t: memx[:, t, :], lambda t: memx[:, t, :], 2)
            for hd in range(GH):
                cut_ahead(f"v_d{hd // 2}{hd % 2}")
                b = take(dve, f"gs{hd}")
                dve.tensor_tensor(scT[:, hd, 0:2 * P].rearrange("p (a b) -> p a b", a=2),
                                  b[:, 0:2 * P].rearrange("p (a b) -> p a b", a=2), mid(tri16[:], 2), ALU.mult)
                dve.tensor_copy(scT[:, hd, 2 * P:3 * P], b[:, 2 * P:3 * P]).then_inc(free_bank(f"gs{hd}"), 1)
            for q in range(4):
                low_T("m_T", q, memT, vT[:, 8:16])
            for a in range(2):
                cut_ahead(f"v_d2{a}")
            for t in range(TT):
                dve.wait_ge(go_ss, 4 * t + 4)
                rsqrt_mean(st[:, 8 + 4 * t:12 + 4 * t], st[:, 8 + 4 * t:12 + 4 * t], P)
                b = pt[BANK[f"go{t}"]]
                for hd in range(GH):
                    sl = slice(hd * P, (hd + 1) * P)
                    ins = dve.scalar_tensor_tensor(og[:, t, sl], b[:, sl], st[:, 8 + 4 * t + hd:9 + 4 * t + hd],
                                                   sr[:, t, sl], ALU.mult, ALU.mult)
                ins.then_inc(free_bank(f"go{t}"), 1)

            maskf = masks[:].rearrange("p m s -> p (m s)")

            def scores(hd):
                i = hd % 2
                dve.wait_ge(masks_ready, 4)
                b = take(dve, f"s{hd}0")
                dve.tensor_tensor_reduce(out=S[:, i, 0:3 * P].rearrange("p (g s) -> p g s", g=NG),
                                         in0=b[:, 0:3 * P].rearrange("p (g s) -> p g s", g=NG),
                                         in1=masks[:, 1::2, :], scale=1.0, scalar=-3e38, op0=ALU.add, op1=ALU.max,
                                         accum_out=st[:, 32:33]).then_inc(free_bank(f"s{hd}0"), 1)
                b = take(dve, f"s{hd}1a")
                dve.tensor_tensor_reduce(out=S[:, i, 3 * P:7 * P], in0=b[:], in1=maskf[:, 0:4 * P], scale=1.0,
                                         scalar=-3e38, op0=ALU.add, op1=ALU.max, accum_out=st[:, 33:34])\
                    .then_inc(free_bank(f"s{hd}1a"), 1)
                b = take(dve, f"s{hd}1b")
                dve.tensor_tensor_reduce(out=S[:, i, 7 * P:9 * P], in0=b[:, 0:2 * P], in1=maskf[:, 4 * P:6 * P],
                                         scale=1.0, scalar=-3e38, op0=ALU.add, op1=ALU.max,
                                         accum_out=st[:, 34:35]).then_inc(free_bank(f"s{hd}1b"), 1)
                emptied(dve, f"s{hd}1b")
                link(dve.tensor_tensor(st[:, 33:34], st[:, 33:34], st[:, 34:35], ALU.max))
                dve.tensor_scalar(st[:, 36 + 2 * i:38 + 2 * i], st[:, 32:34], -ATT_SCALE, None, ALU.mult)\
                    .then_inc(s_ready, 1)

            def probs(hd):
                i = hd % 2
                dve.wait_ge(s_exp, 2 * hd + 2)
                link(dve.reciprocal(st[:, 40 + 2 * i:42 + 2 * i], st[:, 40 + 2 * i:42 + 2 * i]))
                dve.tensor_scalar(S[:, i, 0:3 * P], S[:, i, 0:3 * P], st[:, 40 + 2 * i:41 + 2 * i], None, ALU.mult)
                dve.tensor_scalar(S[:, i, 3 * P:9 * P], S[:, i, 3 * P:9 * P], st[:, 41 + 2 * i:42 + 2 * i], None,
                                  ALU.mult).then_inc(s_prob, 1)

            def probs_T(hd):
                b = take(dve, f"pt{hd}2")
                dve.tensor_copy(PT[:, hd % 2, 2, :], b[:, 0:3 * P]).then_inc(free_bank(f"pt{hd}2"), 1)

            def out_low(name, dst, a):
                b = take(dve, name)
                low(dst[:, 1, 2 * a:2 * a + 2, :].rearrange("p a b -> p (a b)"), b[:], 1.0,
                    dst[:, 0, 2 * a:2 * a + 2, :].rearrange("p a b -> p (a b)")).then_inc(free_bank(name), 1)

            for hd in range(NH):
                scores(hd)
                cut_ahead(f"eg{2 * hd}")
                probs(hd)
                cut_ahead(f"eg{2 * hd + 1}")
                if hd == 0:
                    for q in range(2):
                        low_T("gt", q, ogT, vT[:, 24:28])
                else:
                    probs_T(hd - 1)
                if hd == 2:
                    out_low("pv0", odT, 0)
            cut_ahead("xk0")
            probs_T(3)
            out_low("pv1", odT, 1)
            for i in range(2):
                cut_ahead(f"gla{i}")
                for q in (2 * i, 2 * i + 1):
                    b = take(dve, f"bg{q}")
                    if q == 0:
                        emptied(dve, "eg7")
                    g0 = gates[:, 2 * q:2 * q + 2, :].rearrange("p a b -> p (a b)")
                    dve.scalar_tensor_tensor(g0, g0, 1.0, b[:], ALU.add, ALU.mult).then_inc(free_bank(f"bg{q}"), 1)
                cut_ahead(f"dil{i}")
                for q in (2 * i, 2 * i + 1):
                    b = take(dve, f"bd{q}")
                    g0 = gates[:, 2 * q:2 * q + 2, :].rearrange("p a b -> p (a b)")
                    g1 = gates[:, 8 + 2 * q:10 + 2 * q, :].rearrange("p a b -> p (a b)")
                    dve.scalar_tensor_tensor(g1, g1, 1.0, b[:], ALU.add, ALU.mult).then_inc(free_bank(f"bd{q}"), 1)
                    emptied(dve, f"bd{q}")
                    dve.tensor_tensor(g0, g0, g1, ALU.add).then_inc(merged_sum, 1)
                    m = mergedT[:, :, 2 * q:2 * q + 2, :].rearrange("p k a b -> p k (a b)")
                    low(m[:, 1], g0, 0.5 / WS, m[:, 0]).then_inc(merged_ready, 1)
            cut_ahead("xk1")
            for q in range(4):
                cut_ahead(f"mix{q}")
                b = take(dve, f"mix{q}")
                hh = h[:, :, q * 256:(q + 1) * 256]
                dve.scalar_tensor_tensor(hh, b[:].rearrange("p (t n) -> p t n", t=TT), 1 / WS, hh, ALU.mult, ALU.add)\
                    .then_inc(free_bank(f"mix{q}"), 1)
            normed(2, 4, lambda t: h[:, t, :], lambda t: xn[:, t, :], 4)
            cut_ahead("xv0")
            for q in range(4):
                low_T("c_T", q, aT, vT[:, 16:24])
            cut_ahead("xv1")

            def x_max(hd):
                i = hd % 2
                b = take(dve, f"xs{hd}")
                m = st[:, 32 + 2 * i:34 + 2 * i]
                link(dve.reduce_max(m, b[:].rearrange("p (a b) -> p a b", a=2), AX))
                dve.tensor_scalar(st[:, 44 + 2 * i:46 + 2 * i], m, -ATT_SCALE, None, ALU.mult)\
                    .then_inc(xs_max, 1)

            def x_prob(hd):
                i = hd % 2
                dve.wait_ge(xs_exp, hd + 1)
                emptied(dve, f"xs{hd}")
                link(dve.reciprocal(st[:, 48 + 2 * i:50 + 2 * i], st[:, 48 + 2 * i:50 + 2 * i]))
                for t in range(TT):
                    ins = dve.tensor_scalar(xP[:, hd, t, :], xP[:, hd, t, :], st[:, 48 + 2 * i + t:49 + 2 * i + t],
                                            None, ALU.mult)
                ins.then_inc(xs_prob, 1)

            cut_ahead("xq1")
            x_max(0)
            x_max(1)
            for hd in range(NH):
                x_prob(hd)
                if hd + 2 < NH:
                    x_max(hd + 2)
            out_low("xpv0", oxT, 0)
            out_low("xpv1", oxT, 1)
            for n in range(2):
                cut_ahead(f"xo{n}")
                for t in range(TT):
                    b = take(dve, f"xo{n}{t}")
                    hh = h[:, t, n * 512:(n + 1) * 512]
                    dve.scalar_tensor_tensor(hh, b[:], 1 / WS, hh, ALU.mult, ALU.add)\
                        .then_inc(free_bank(f"xo{n}{t}"), 1)
            normed(3, 2, lambda t: h[:, t, :].rearrange("p (q c) -> p c q", c=C), lambda t: f[:, t], 6)
            dve.wait_ge(ld_route, 48)
            for q in (1, 3):
                b = take(dve, f"f_T{q}")
                dve.tensor_tensor(fT[:, 2 * q:2 * q + 2, :], b[:].rearrange("p (a b) -> p a b", a=2),
                                  bc(g3[:, 2 * q:2 * q + 2], T), ALU.mult).then_inc(free_bank(f"f_T{q}"), 1)
            for t in range(TT):
                dve.wait_ge(f_high, t + 1)
                dve.tensor_tensor(f16[:, 1, t], f[:, t], f16[:, 0, t], ALU.subtract).then_inc(f_low, 1)
            b = take(dve, "rt")
            dve.tensor_copy(logit.rearrange("p a b -> p (a b)"), b[:, 0:TT * E]).then_inc(free_bank("rt"), 1)
            emptied(dve, "rt")
            for t in range(TT):
                ins = dve.max(top[:, t, :], logit[:, t, :])
            link(ins)
            for t in range(TT):
                ins = dve.max_index(idx_u[:, t, :], top[:, t, :], logit[:, t, :])
            link(ins)
            link(dve.tensor_copy(idx_f, idx_u[:, :, 0:TOPK]))
            dve.tensor_scalar(st[:, 52:54], top[:, :, 0], -1.0, None, ALU.mult).then_inc(top_ready, 1)
            hot, hot_g = oneh[:, 0:TT * TOPK, :], oneh[:, TT * TOPK:, :]
            link(dve.tensor_tensor(hot, mid(iota_e[:], TT * TOPK), bc(idx_f.rearrange("p a b -> p (a b)"), E),
                                   ALU.is_equal))
            dve.reduce_sum(mask, hot.rearrange("p (t k) e -> p t e k", t=TT), AX).then_inc(gate_ready, 1)
            dve.wait_ge(top_exp, 2)
            link(dve.reciprocal(st[:, 54:56], st[:, 54:56]))
            link(dve.tensor_tensor(g4, g4, bc(st[:, 54:56], TOPK), ALU.mult))
            link(dve.tensor_tensor(hot_g, hot, bc(g4.rearrange("p a b -> p (a b)"), E), ALU.mult))
            dve.reduce_sum(gate, hot_g.rearrange("p (t k) e -> p t e k", t=TT), AX).then_inc(gate_ready, 1)
            b = take(dve, "pos")
            link(dve.scalar_tensor_tensor(place.rearrange("p a b -> p (a b)"), b[:, 0:TT * E], 1.0,
                                          mask.rearrange("p a b -> p (a b)"), ALU.add, ALU.mult))
            link(dve.tensor_scalar(place, place, -1.0, None, ALU.add))
            dve.memset(st[:, 61:62], 0.0).then_inc(free_bank("pos"), 1)
            dve.memset(st[:, 63:64], 0.0).then_inc(round_chain, 1)

            def overflow():
                emptied(dve, "all")
                link(dve.reduce_max(st[:, 60:61], totals, AX))
                dve.tensor_scalar(over[:], st[:, 60:61], float(SLOTS), None, ALU.is_gt).then_inc(over_ready, 1)

            def body(n, k):
                count = [0]

                def link2(ins):
                    count[0] += 1
                    ins.then_inc(moe_chain, 1)
                    dve.wait_ge(moe_chain, k * LINKS + count[0])

                for t in range(TT):
                    ins = dve.tensor_tensor(sel[:, t, :].rearrange("p (e s) -> p e s", e=EG),
                                            bc(place[:, t, bass.ds(n * EG, EG)], SLOTS), mid(iota_s[:], EG),
                                            ALU.is_equal)
                ins.then_inc(sel_ready, 1)
                dve.wait_ge(sel_ready, k + 1)
                for t in range(TT):
                    s4 = sel[:, t, :].rearrange("p (e s) -> p e s", e=EG)
                    ins = dve.tensor_tensor(
                        selG[:, t], s4.unsqueeze(2).to_broadcast([P, EG, 2, SLOTS]),
                        gate[:, t, bass.ds(n * EG, EG)].unsqueeze(2).unsqueeze(3).to_broadcast([P, EG, 2, SLOTS]),
                        ALU.mult)
                ins.then_inc(selG_ready, 1)
                for q in (1, 3):
                    dve.wait_ge(gathered, 4 * k + (q + 1))
                    dve.tensor_tensor(xg[:, 2 * q:2 * q + 2, :], pt[3][:].rearrange("p (a b) -> p a b", a=2),
                                      bc(g3[:, 2 * q:2 * q + 2], T), ALU.mult).then_inc(xg_dve, 1)
                for j in range(EG):
                    e = n * EG + j
                    dve.wait_ge(h_full, k * EG + (j + 1))
                    dve.tensor_copy(hs[:, :, 64:128], pt[1][:].rearrange("p (q c) -> p c q", c=C))\
                        .then_inc(hs_dve, 1)
                    if j == 0:
                        dve.wait_ge(selT_full, 2 * k + 2)
                        dve.tensor_copy(selT[:, 2:4].rearrange("p e t s -> p (e t s)"), pt[3][:])\
                            .then_inc(selT_dve, 1)
                    for i in range(2):
                        cc = slice(4 * i, 4 * i + 4)
                        up = pt[i][:].rearrange("p (c b s) -> p b c s", c=4, b=2)
                        bias = [bT[:, b, cc, bass.ds(e, 1)].to_broadcast([P, 4, SLOTS]) for b in range(2)]
                        dve.wait_ge(T_full, k * 2 * EG + (2 * j + i + 1))
                        link2(dve.tensor_tensor(g_sb[:, cc, :], up[:, 0], bias[0], ALU.add))
                        dve.tensor_scalar(g_sb[:, cc, :], g_sb[:, cc, :], LIMIT, None, ALU.min)\
                            .then_inc(g_ready, 1)
                        link2(dve.tensor_tensor(l_sb[:, cc, :], up[:, 1], bias[1], ALU.add))
                        link2(dve.tensor_scalar(l_sb[:, cc, :], l_sb[:, cc, :], LIMIT, -LIMIT, ALU.min, ALU.max))
                        dve.scalar_tensor_tensor(l_sb[:, cc, :], l_sb[:, cc, :], 1.0, g_sb[:, cc, :],
                                                 ALU.add, ALU.mult).then_inc(lin_chain, 1)
                        dve.wait_ge(lin_chain, k * 2 * EG + (2 * j + i + 1))
                        dve.wait_ge(sg_ready, k * 2 * EG + (2 * j + i + 1))
                        dve.tensor_tensor(actT[:, cc, :], l_sb[:, cc, :], sg_sb[:, cc, :], ALU.mult)\
                            .then_inc(act_ready, 1)
                assert count[0] == LINKS, count[0]

            expert_groups(dve, body, overflow)

            for t in range(TT):
                dve.wait_ge(fin_ss, 2 * t + 2)
                v = st[:, 56 + 2 * t:57 + 2 * t]
                link(dve.tensor_tensor(v, v, st[:, 57 + 2 * t:58 + 2 * t], ALU.add))
                rsqrt_mean(v, v, D)
                if t == 0:
                    dve.wait_ge(ld_late, 16 * 2)
                for i in range(2):
                    dve.scalar_tensor_tensor(out_sb[:, t, i * 512:(i + 1) * 512], pt[4 + 2 * t + i][:], v,
                                             gfin[:, i * 512:(i + 1) * 512], ALU.mult, ALU.mult)\
                        .then_inc(fin_ready, 1)

        @block.tensor
        def _(pe):
            mm = pe.matmul

            def fill(name):
                if TURN[name]:
                    pe.wait_ge(free[BANK[name]], TURN[name])
                return pt[BANK[name]]

            def filled(ins, name):
                ins.then_inc(full[BANK[name]], 1)

            def weights(name):
                u = HALVES.index(name)
                pe.wait_ge(w_low, u + 1)
                return cut[u % EARLY].rearrange("p k (c n) -> p k c n", n=SRC[name].shape[2])

            PASSES = ((0, 0), (0, 1), (1, 0))

            def feature_major(name, w, rhs, nk, col=0, chunk_ready=None):
                b = fill(name)
                for i in range(2):
                    o = col + i * P
                    for c in range(nk):
                        if chunk_ready and i == 0:
                            chunk_ready(c)
                        for k, (pw, px) in enumerate(PASSES):
                            ins = mm(b[:, i * T:(i + 1) * T], w[:, pw, c, o:o + P], rhs[:, px, c, :],
                                     start=(c == 0 and k == 0), stop=(c == nk - 1 and k == 2))
                filled(ins, name)

            def pairs_ready(prefix):
                def ready(c):
                    if c % 2 == 0:
                        emptied(pe, f"{prefix}{c // 2}")
                return ready

            def merged_pairs(c):
                if c % 2 == 0:
                    pe.wait_ge(merged_ready, c // 2 + 1)

            def token_major(name, w, lhs, nk, tiles, n, chunk_ready=None):
                b = fill(name)
                for i, t in enumerate(tiles):
                    for c in range(nk):
                        if chunk_ready and i == 0:
                            chunk_ready(c)
                        for k, (pw, px) in enumerate(PASSES):
                            ins = mm(b[:, i * n:(i + 1) * n], lhs[:, px, c, t * P:(t + 1) * P], w[:, pw, c, 0:n],
                                     start=(c == 0 and k == 0), stop=(c == nk - 1 and k == 2))
                filled(ins, name)

            def norm_transposes(prefix, src, count):
                for q in range(4):
                    b = fill(f"{prefix}{q}")
                    for t in range(TT):
                        if q == 0:
                            pe.wait_ge(norm_xn, count - TT + t + 1)
                        for i in range(2):
                            ins = pe.transpose(b[:, i * T + t * P:i * T + (t + 1) * P], src(t, 2 * q + i), ident[:])
                    filled(ins, f"{prefix}{q}")

            pe.wait_ge(consts, 1)
            pe.wait_ge(ld_rows, 16 * 5)
            b = fill("vec")
            filled(pe.transpose(b[:, 0:44], rows[0:44, :], ident[0:44, 0:44]), "vec")

            norm_transposes("x_T", lambda t, c: xn[:, t, c * P:(c + 1) * P], 2)
            feature_major("q_g", weights("q_g"), aT, C, chunk_ready=pairs_ready("x_T"))
            feature_major("k_g", weights("k_g"), aT, C)
            pe.wait_ge(consts, 9)
            pe.wait_ge(alr_cut, 2)
            b = fill("alr")
            for c in range(C):
                for k, (pw, px) in enumerate(PASSES):
                    ins = mm(b[0:16, 0:T], w_alr16[:, pw, c, :], aT[:, px, c, :], start=(c == 0 and k == 0),
                             stop=(c == C - 1 and k == 2))
            filled(ins, "alr")
            for k in ("v_g0", "v_g1", "r_g0", "r_g1"):
                token_major(k, weights(k), aT, C, (0, 1), 256)
            b = fill("lg")
            pe.wait_ge(ld_small, 16 * 4)
            emptied(pe, "alr")
            for t in range(TT):
                ins = mm(b[:, t * T:(t + 1) * T], alr[0:17, t * P:(t + 1) * P], w2[0:17, :], start=True, stop=True)
            filled(ins, "lg")

            def rotary_halves(name):
                pe.wait_ge(w_low, HALVES.index(name) + 1)
                w = paired(HALVES.index(name))
                b = fill(name)
                for i in range(2):
                    for c in range(C):
                        for k, (pw, px) in enumerate(PASSES):
                            ins = mm(b[:, i * T:(i + 1) * T], w[:, pw, i, c, :], aT[:, px, c, :],
                                     start=(c == 0 and k == 0), stop=(c == C - 1 and k == 2))
                filled(ins, name)

            for g in range(NG):
                for a in range(2):
                    rotary_halves(f"q_d{g}{a}")
            pe.wait_ge(ld_brows, 32)
            b = fill("bias")
            for k in range(2):
                for c in range(C):
                    o = (k * C + c) * E
                    ins = pe.transpose(b[:, o:o + E], brows[0:E, k, c::C], ident[0:E, 0:E])
            filled(ins, "bias")
            b = fill("cum")
            emptied(pe, "lg")
            for fc in range(2):
                for t in range(TT):
                    ins = mm(b[:, fc * T + t * P:fc * T + (t + 1) * P], la[:, t, fc * P:(fc + 1) * P], tri16[:],
                             start=True, stop=True)
            filled(ins, "cum")
            for g in range(NG):
                for a in range(2):
                    rotary_halves(f"k_d{g}{a}")

            def v_dil(g, a):
                token_major(f"v_d{g}{a}", weights(f"v_d{g}{a}"), aT, C, (0, 1), 256)

            pe.wait_ge(gla_qk, 1)
            for hd in range(GH):
                v_dil(hd // 2, hd % 2)
                b = fill(f"gs{hd}")
                hp, fc = slice(64 * (hd % 2), 64 * (hd % 2) + 64), hd // 2
                for t in range(TT):
                    for i in range(NSUB):
                        a0 = t * P + i * SUB
                        mm(b[:, a0:a0 + SUB], kS[hp, fc, t, i, :], qS[hp, fc, a0:a0 + SUB], start=True, stop=True)
                filled(mm(b[:, 2 * P:3 * P], kX[hp, fc, :], qX[hp, fc, :], start=True, stop=True), f"gs{hd}")
            norm_transposes("m_T", lambda t, c: memx[:, t, c * P:(c + 1) * P], 4)
            for a in range(2):
                v_dil(2, a)
            emptied(pe, "gs3")
            emptied(pe, "v_g1")
            for t in range(TT):
                b = fill(f"go{t}")
                for hd in range(GH):
                    sl = slice(hd * P, (hd + 1) * P)
                    ins = mm(b[:, sl], scT[:, hd, t * P:(t + 1) * P], vg[:, t, sl], start=True, stop=(t == 0))
                    if t:
                        ins = mm(b[:, sl], scT[:, hd, 2 * P:3 * P], vg[:, 0, sl], start=False, stop=True)
                filled(ins, f"go{t}")

            def dil_scores(hd):
                hp, a = slice(64 * (hd % 2), 64 * (hd % 2) + 64), hd // 2

                def one(dst, g, t):
                    for j in range(2):
                        ins = mm(dst, qr[hp, 2 * g + a, j, t * P:(t + 1) * P], kr[hp, 2 * g + a, j, 0:(t + 1) * P],
                                 start=(j == 0), stop=(j == 1))
                    return ins
                b = fill(f"s{hd}0")
                for g in range(NG):
                    ins = one(b[:, g * P:(g + 1) * P], g, 0)
                filled(ins, f"s{hd}0")
                b = fill(f"s{hd}1a")
                for g in range(2):
                    ins = one(b[:, g * T:(g + 1) * T], g, 1)
                filled(ins, f"s{hd}1a")
                b = fill(f"s{hd}1b")
                filled(one(b[:, 0:T], 2, 1), f"s{hd}1b")

            def dil_transposes(hd):
                pe.wait_ge(s_prob, hd + 1)
                for g in range(NG):
                    b = fill(f"pt{hd}{g}")
                    for i, c0 in enumerate((g * P, 3 * P + g * T, 3 * P + g * T + P)):
                        ins = pe.transpose(b[:, i * P:(i + 1) * P], S[:, hd % 2, c0:c0 + P], ident[:])
                    filled(ins, f"pt{hd}{g}")

            def dil_out(a):
                b = fill(f"pv{a}")
                for i in range(2):
                    hd = 2 * a + i
                    for g in range(NG):
                        emptied(pe, f"pt{hd}{g}")
                        mm(b[:, i * T:(i + 1) * T], vd[:, 0, g * 512 + hd * P:g * 512 + (hd + 1) * P],
                           PT[:, i, g, 0:T], start=(g == 0), stop=False)
                    for g in range(NG):
                        ins = mm(b[:, i * T + P:(i + 1) * T], vd[:, 1, g * 512 + hd * P:g * 512 + (hd + 1) * P],
                                 PT[:, i, g, T:3 * P], start=False, stop=(g == NG - 1))
                filled(ins, f"pv{a}")

            for hd in range(NH):
                dil_scores(hd)
                for q in (2 * hd, 2 * hd + 1):
                    feature_major(f"eg{q}", weights(f"eg{q}"), aT, C)
                if hd == 0:
                    emptied(pe, "go0")
                    emptied(pe, "go1")
                    for q in range(2):
                        b = fill(f"gt{q}")
                        for i in range(2):
                            for t in range(TT):
                                c = 2 * q + i
                                ins = pe.transpose(b[:, i * T + t * P:i * T + (t + 1) * P],
                                                   og[:, t, c * P:(c + 1) * P], ident[:])
                        filled(ins, f"gt{q}")
                else:
                    dil_transposes(hd - 1)
                if hd == 2:
                    dil_out(0)
            for q in range(4):
                emptied(pe, f"m_T{q}")
            feature_major("xk0", weights("xk0"), memT, C)
            dil_transposes(3)
            dil_out(1)

            emptied(pe, "gt0")
            emptied(pe, "gt1")
            for i in range(2):
                for k, half, src in (("bg", "gla", ogT), ("bd", "dil", odT)):
                    if k == "bd" and i == 0:
                        emptied(pe, "pv0")
                        emptied(pe, "pv1")
                    w = weights(f"{half}{i}")
                    for j in range(2):
                        feature_major(f"{k}{2 * i + j}", w, src, 4, j * 256)
            feature_major("xk1", weights("xk1"), memT, C)
            for q in range(4):
                token_major(f"mix{q}", weights(f"mix{q}"), mergedT, C, (0, 1), 256,
                            chunk_ready=None if q else merged_pairs)
            token_major("xv0", weights("xv0"), memT, C, (0, 1), 256)

            norm_transposes("c_T", lambda t, c: xn[:, t, c * P:(c + 1) * P], 6)
            w_xv1 = weights("xv1")
            token_major("xv10", w_xv1, memT, C, (0,), 256)
            feature_major("xq0", weights("xq0"), aT, C, chunk_ready=pairs_ready("c_T"))
            token_major("xv11", w_xv1, memT, C, (1,), 256)

            def x_scores(hd):
                emptied(pe, f"xq{hd // 2}")
                b = fill(f"xs{hd}")
                for t in range(TT):
                    ins = mm(b[:, t * M:(t + 1) * M], xq[:, hd, t * P:(t + 1) * P], xk[:, hd, :], start=True,
                             stop=True)
                filled(ins, f"xs{hd}")

            def x_transposes(hd):
                pe.wait_ge(xs_prob, hd + 1)
                b = fill(f"xt{hd}")
                for s in range(2):
                    for t in range(TT):
                        ins = pe.transpose(b[:, s * T + t * P:s * T + (t + 1) * P],
                                           xP[:, hd, t, s * P:(s + 1) * P], ident[:])
                filled(ins, f"xt{hd}")

            def x_out(a):
                b = fill(f"xpv{a}")
                for i in range(2):
                    hd = 2 * a + i
                    emptied(pe, f"xt{hd}")
                    for s in range(2):
                        ins = mm(b[:, i * T:(i + 1) * T], xv[:, s, hd * P:(hd + 1) * P], xPT[:, hd, s, :],
                                 start=(s == 0), stop=(s == 1))
                filled(ins, f"xpv{a}")

            for name in ("xk0", "xk1", "xv0", "xv10"):
                emptied(pe, name)
            feature_major("xq1", weights("xq1"), aT, C)
            for hd in range(NH):
                x_scores(hd)
            x_transposes(0)
            x_transposes(1)
            x_transposes(2)
            x_out(0)
            x_transposes(3)
            emptied(pe, "xv11")
            x_out(1)
            for n in range(2):
                w = weights(f"xo{n}")
                for t in range(TT):
                    token_major(f"xo{n}{t}", w, oxT, 4, (t,), 512, chunk_ready=None if n or t else pairs_ready("xpv"))
            acc = [[pt[4 + 2 * t + n] for n in range(2)] for t in range(TT)]
            for b in range(4, BANKS):
                pe.wait_ge(free[b], USES[b])
            for n in range(2):
                for t in range(TT):
                    emptied(pe, f"xo{n}{t}")
                    mm(acc[t][n][:], ident[:], h[:, t, n * 512:(n + 1) * 512], start=True, stop=False)

            norm_transposes("f_T", lambda t, c: f[:, t, c, :], 8)
            pe.wait_ge(ld_route, 48)
            b = fill("rt")
            mm(b[:, 0:TT * E], ones[0:1, :], mid(b_rt[:], TT), start=True, stop=False)
            for c in range(C):
                if c % 2 == 0:
                    emptied(pe, f"f_T{c // 2}")
                for t in range(TT):
                    ins = mm(b[:, t * E:(t + 1) * E], fT[:, c, t * P:(t + 1) * P], w_rt[:, c, :], start=False,
                             stop=(c == C - 1 and t == TT - 1))
            filled(ins, "rt")
            pe.wait_ge(gate_ready, 1)
            b = fill("pos")
            mm(b[:, 0:TT * E], tri_s[:], mask.rearrange("p a b -> p (a b)"), start=True, stop=False)
            filled(mm(b[:, E:2 * E], ones[:], mask[:, 0, :], start=False, stop=True), "pos")
            b = fill("all")
            mm(b[:, 0:E], ones[:], mask[:, 0, :], start=True, stop=False)
            filled(mm(b[:, 0:E], ones[:], mask[:, 1, :], start=False, stop=True), "all")
            pe.wait_ge(gate_ready, 2)
            b = fill("gT")
            for t in range(TT):
                ins = pe.transpose(b[0:E, t * P:(t + 1) * P], gate[:, t, :], ident[:])
            filled(ins, "gT")

            for b in range(4):
                pe.wait_ge(free[b], USES[b])

            pe.wait_ge(f_low, TT)
            per = 12 * EG

            def body(n, k):
                pe.wait_ge(sel_ready, k + 1)

                def gather(q):
                    if q >= 2:
                        pe.wait_ge((xg_act, xg_dve)[q - 2], 2 * k + 1)
                    for i in range(2):
                        for t in range(TT):
                            for part in range(2):
                                ins = mm(pt[2 + q % 2][:, i * T:(i + 1) * T], f16[:, part, t, 2 * q + i, :],
                                         sel[:, t, :], start=(t == 0 and part == 0), stop=(t == TT - 1 and part == 1))
                    ins.then_inc(gathered, 1)

                def scatter(j):
                    pe.wait_ge(y_ready, k * EG + (j + 1))
                    for t in range(TT):
                        for nh in range(2):
                            rows_h = slice(64 * nh, 64 * nh + 64)
                            mm(acc[t][nh][:], selT[rows_h, j, t, :], y[rows_h, :], start=False, stop=False)

                def scatter_matrices():
                    pe.wait_ge(selG_ready, k + 1)
                    for q in range(2):
                        for i in range(2):
                            for t in range(TT):
                                o = (i * TT + t) * P
                                ins = pe.transpose(pt[2 + q][:, o:o + P],
                                                   selG[:, t, 2 * q + i].rearrange("p a s -> p (a s)"), ident[:])
                        ins.then_inc(selT_full, 1)

                def loaded(v):
                    pe.wait_ge(late_ld[slot_of(v)], k * (16 * per // NSLOT) + 16 * (v // NSLOT + 1))
                    return slot[slot_of(v)].rearrange("p (c n) -> p c n", n=D)

                gather(0)
                gather(1)
                for j in range(EG):
                    v = 12 * j
                    xe = [xg[:, c, j * SLOTS:(j + 1) * SLOTS] for c in range(C)]
                    for q in range(4):
                        wg, wu = loaded(v + 2 * q), loaded(v + 2 * q + 1)
                        if j == 0:
                            pe.wait_ge((xg_act, xg_dve)[q % 2], 2 * k + (q // 2 + 1))
                        for i in range(2):
                            c = 2 * q + i
                            for nh in range(2):
                                for col, w in ((0, wg), (64, wu)):
                                    ins = mm(pt[nh][col:col + 64, :], xe[c], w[:, i, nh * 512:(nh + 1) * 512],
                                             start=(c == 0), stop=(c == C - 1))
                        if q < 3:
                            ins.then_inc(gu_used, 1)
                        if j == 0 and q == 0:
                            gather(2)
                            gather(3)
                    ins.then_inc(h_full, 1)
                    if j == 0:
                        scatter_matrices()
                    pe.wait_ge(hs_act, k * EG + (j + 1))
                    pe.wait_ge(hs_dve, k * EG + (j + 1))
                    for i in range(2):
                        for c in range(4):
                            ins = pe.transpose(pt[i][:, c * P:(c + 1) * P], hs[:, 4 * i + c, :], ident[:])
                        ins.then_inc(T_full, 1)
                    if j:
                        scatter(j - 1)
                    if j == 0:
                        pe.wait_ge(selT_act, k + 1)
                        pe.wait_ge(selT_dve, k + 1)
                    for q in range(4):
                        w = loaded(v + 8 + q)
                        if q % 2 == 0:
                            pe.wait_ge(act_ready, k * 2 * EG + (2 * j + q // 2 + 1))
                        for i in range(2):
                            c = 2 * q + i
                            for nh in range(2):
                                ins = mm(pt[2][64 * nh:64 * nh + 64, :], actT[:, c, :],
                                         w[:, i, nh * 512:(nh + 1) * 512], start=(c == 0), stop=(c == C - 1))
                        if q < 3:
                            ins.then_inc(dn_used, 1)
                    ins.then_inc(y_full, 1)
                scatter(EG - 1)

            expert_groups(pe, body)

            pe.wait_ge(ld_late, 16 * 2)
            for t in range(TT):
                for n in range(2):
                    mm(acc[t][n][:], gateT[0:E, t * P:(t + 1) * P], b_dn[0:E, n * 512:(n + 1) * 512],
                       start=False, stop=True).then_inc(acc_full, 1)


_INS = ['x', 'mem', 'positions', 'norm1_g', 'w_in', 'w_gla_a2', 'b_gla_a2', 'gla_norm_g', 'w_branch_gla',
        'w_branch_dil', 'w_branch_gate', 'b_branch_gate', 'w_mix_out', 'norm2_g', 'mem_norm_g', 'w_xq', 'w_xkv',
        'w_xo', 'norm3_g', 'w_router', 'b_router', 'w_gate', 'b_gate', 'w_up', 'b_up', 'w_down', 'b_down',
        'final_norm_g']


def kernel(**inputs):
    import concourse.bacc as bacc
    from concourse.bass_utils import run_bass_kernel_spmd

    nc = bacc.Bacc("TRN2", target_bir_lowering=False, num_devices=1)
    arrays, A = {}, {}
    freq = np.float32(10000.0) ** (-np.arange(64, dtype=np.float32) / np.float32(64))
    inputs["inv_freq"] = np.concatenate([freq, freq]).reshape(128, 1).astype(np.float32)
    for name in _INS + ["inv_freq"]:
        a = np.ascontiguousarray(inputs[name])
        arrays[f"in_{name}"] = a
        A[name] = nc.dram_tensor(f"in_{name}", a.shape, mybir.dt.from_np(a.dtype), kind="ExternalInput").ap()
    out = nc.dram_tensor("out_0", (1, T, D), F32, kind="ExternalOutput").ap()
    _program(nc, A, out)
    r = run_bass_kernel_spmd(nc, [arrays], core_ids=[0])
    return r.results[0]["out_0"]
```
